# Optimizing a Trainium2 kernel written in Bass

```python
import math
import jax
import jax.numpy as jnp
from jax import lax
import numpy as np

'''Hybrid decoder block (Hymba-style parallel head groups).

Per layer:
  h = RMSNorm(x)
  p = h @ W_in                       single combined input projection, columns split into
                                     [NSA q | NSA k/v for cmp, slc, win | NSA gates | RWKV-7 r,k,v,lora inputs]
  y_nsa  = NSA(...)                  8 heads x 64 (causal, ALiBi)
  y_rwkv = RWKV7(...)                8 heads x 64 (causal vector-state recurrence)
  x = x + concat(y_nsa, y_rwkv) @ W_out
  x = x + PEER(RMSNorm(x))           product-key retrieval over 128^2 single-neuron experts
out = RMSNorm(x)

Inputs: x (BATCH, SEQ, D_MODEL) float32 plus per-layer parameters (leading DEPTH axis).
Output: (BATCH, SEQ, D_MODEL).
'''

D_MODEL = 1024
BATCH = 1
SEQ = 512
DEPTH = 1

D_MIX = D_MODEL
HEAD_DIM = 64
NSA_HEADS = 8
NSA_KV_HEADS = 2
NSA_GROUP = NSA_HEADS // NSA_KV_HEADS
RWKV_HEADS = 8
D_NSA = NSA_HEADS * HEAD_DIM
D_RWKV = RWKV_HEADS * HEAD_DIM
D_KV = NSA_KV_HEADS * HEAD_DIM
CMP_LEN = 32
CMP_STRIDE = 16
CMP_HIDDEN = 128
SEL_LEN = 64
SEL_TOPN = 16
WINDOW = 512
Q_CHUNK = 64
RANK_W = 64
RANK_A = 64
RANK_G = 128
D_RWKV_IN = 3 * D_RWKV + RANK_W + RANK_A + RANK_G
RWKV_SIZES = (D_RWKV, D_RWKV, D_RWKV, RANK_W, RANK_A, RANK_G)
COL_SIZES = (D_NSA, D_KV, D_KV, D_KV, D_KV, D_KV, D_KV, 3 * NSA_HEADS, D_RWKV_IN)
D_IN = D_NSA + 6 * D_KV + 3 * NSA_HEADS + D_RWKV_IN
PEER_HEADS = 8
PEER_N_KEYS = 128
PEER_N_EXPERTS = PEER_N_KEYS * PEER_N_KEYS
PEER_D_QUERY = 256
PEER_TOPK = 16
PEER_CHUNK = 128
EPS = 1e-6
GN_EPS = 64e-5

kernel_name = 'hymba_nsa_rwkv7_peer_block'

def rms_norm(x, g):
    xf = x.astype(jnp.float32)
    y = xf * lax.rsqrt(jnp.mean(xf * xf, axis=-1, keepdims=True) + EPS)
    return (y * g.astype(jnp.float32)).astype(x.dtype)

def masked_softmax(s, mask):
    s = jnp.where(mask, s.astype(jnp.float32), -1e30)
    s = s - jnp.max(s, axis=-1, keepdims=True)
    p = jnp.where(mask, jnp.exp(s), 0.0)
    return p / jnp.maximum(jnp.sum(p, axis=-1, keepdims=True), 1e-30)

def alibi_slopes(n):
    return jnp.exp2(-8.0 * jnp.arange(1, n + 1, dtype=jnp.float32) / n)

def split_cols(p, sizes):
    return jnp.split(p, np.cumsum(np.array(sizes))[:-1].tolist(), axis=-1)

def compress_blocks(k, idx, pe, w1, w2):
    b, _, g, d = k.shape
    blk = k[:, idx] + pe[None, None, :, None, :]
    flat = blk.transpose(0, 1, 3, 2, 4).reshape(b, idx.shape[0], g, CMP_LEN * d)
    return jax.nn.gelu(flat @ w1) @ w2

def nsa_mixer(q, kc, vc, ks, vs, kw, vw, gates, k_pe, k_w1, k_w2, v_pe, v_w1, v_w2):
    b, t_len = q.shape[0], q.shape[1]
    G, R, d = NSA_KV_HEADS, NSA_GROUP, HEAD_DIM
    scale = d ** -0.5
    slopes = alibi_slopes(NSA_HEADS).reshape(G, R)
    n_cmp = (t_len - CMP_LEN) // CMP_STRIDE + 1
    cmp_idx = np.arange(n_cmp)[:, None] * CMP_STRIDE + np.arange(CMP_LEN)[None, :]
    kc_blk = compress_blocks(kc, cmp_idx, k_pe, k_w1, k_w2)
    vc_blk = compress_blocks(vc, cmp_idx, v_pe, v_w1, v_w2)
    cmp_end = jnp.asarray(cmp_idx[:, -1], dtype=jnp.int32)
    n_sel = t_len // SEL_LEN
    top_n = min(SEL_TOPN, n_sel)
    ks_blk = ks.reshape(b, n_sel, SEL_LEN, G, d).transpose(0, 3, 1, 2, 4)
    vs_blk = vs.reshape(b, n_sel, SEL_LEN, G, d).transpose(0, 3, 1, 2, 4)
    cmp_start = cmp_idx[:, 0]
    sel_start = np.arange(n_sel) * SEL_LEN
    overlap = np.clip(np.minimum(cmp_start[:, None] + CMP_LEN, sel_start[None, :] + SEL_LEN)
                      - np.maximum(cmp_start[:, None], sel_start[None, :]), 0, None)
    overlap = jnp.asarray(overlap / CMP_LEN, dtype=jnp.float32)
    blk_ids = jnp.arange(n_sel)
    bi = jnp.arange(b)[:, None, None, None]
    gi = jnp.arange(G)[None, :, None, None]
    kw_pad = jnp.pad(kw, ((0, 0), (WINDOW, 0), (0, 0), (0, 0)))
    vw_pad = jnp.pad(vw, ((0, 0), (WINDOW, 0), (0, 0), (0, 0)))
    n_q = t_len // Q_CHUNK
    q_ch = q.reshape(b, n_q, Q_CHUNK, G, R, d).transpose(1, 0, 3, 4, 2, 5)
    g_ch = gates.reshape(b, n_q, Q_CHUNK, G, R, 3).transpose(1, 0, 3, 4, 2, 5)

    def chunk(args):
        ci, qc, gc = args
        q0 = ci * Q_CHUNK
        t = q0 + jnp.arange(Q_CHUNK)
        dist = t[:, None] - cmp_end[None, :]
        s = jnp.einsum('bgrqd,bngd->bgrqn', qc, kc_blk).astype(jnp.float32) * scale \
            - slopes[:, :, None, None] * dist
        p_cmp = masked_softmax(s, dist >= 0)
        o_cmp = jnp.einsum('bgrqn,bngd->bgrqd', p_cmp.astype(vc_blk.dtype), vc_blk)
        imp = jnp.einsum('bgrqn,ns->bgqs', p_cmp, overlap)
        cur = t // SEL_LEN
        forced = (blk_ids[None] == 0) | (blk_ids[None] == cur[:, None]) | (blk_ids[None] == cur[:, None] - 1)
        valid = blk_ids[None] * SEL_LEN <= t[:, None]
        imp = jnp.where(forced, 1e6, jnp.where(valid, imp, -1.0))
        _, sel = lax.top_k(imp, top_n)
        k_sel = ks_blk[bi, gi, sel].reshape(b, G, Q_CHUNK, top_n * SEL_LEN, d)
        v_sel = vs_blk[bi, gi, sel].reshape(b, G, Q_CHUNK, top_n * SEL_LEN, d)
        pos = (sel[..., None] * SEL_LEN + jnp.arange(SEL_LEN)).reshape(b, G, Q_CHUNK, top_n * SEL_LEN)
        dist = t[None, None, :, None] - pos
        s = jnp.einsum('bgrqd,bgqkd->bgrqk', qc, k_sel).astype(jnp.float32) * scale \
            - slopes[None, :, :, None, None] * dist[:, :, None]
        p = masked_softmax(s, (dist >= 0)[:, :, None])
        o_slc = jnp.einsum('bgrqk,bgqkd->bgrqd', p.astype(v_sel.dtype), v_sel)
        k_win = lax.dynamic_slice_in_dim(kw_pad, q0, Q_CHUNK + WINDOW, axis=1)
        v_win = lax.dynamic_slice_in_dim(vw_pad, q0, Q_CHUNK + WINDOW, axis=1)
        pos = q0 - WINDOW + jnp.arange(Q_CHUNK + WINDOW)
        dist = t[:, None] - pos[None, :]
        mask = (dist >= 0) & (dist < WINDOW) & (pos[None, :] >= 0)
        s = jnp.einsum('bgrqd,bkgd->bgrqk', qc, k_win).astype(jnp.float32) * scale \
            - slopes[:, :, None, None] * dist
        p = masked_softmax(s, mask)
        o_win = jnp.einsum('bgrqk,bkgd->bgrqd', p.astype(v_win.dtype), v_win)
        return gc[..., 0:1] * o_cmp + gc[..., 1:2] * o_slc + gc[..., 2:3] * o_win

    out = lax.map(chunk, (jnp.arange(n_q), q_ch, g_ch))
    return out.transpose(1, 0, 4, 2, 3, 5).reshape(b, t_len, NSA_HEADS * d)

def rwkv7_mixer(p, mu, w0, w2, a0, a2, g2, k_k, k_a, r_k, ln_w, ln_b):
    b, t_len, _ = p.shape
    H, d = RWKV_HEADS, HEAD_DIM
    prev = jnp.pad(p, ((0, 0), (1, 0), (0, 0)))[:, :-1]
    p = p + (prev - p) * mu
    r, k, v, xw, xa, xg = split_cols(p, RWKV_SIZES)
    w = -jax.nn.softplus(-(w0 + jnp.tanh(xw) @ w2)) - 0.5
    decay = jnp.exp(-jnp.exp(w.astype(jnp.float32)))
    a = jax.nn.sigmoid(a0 + xa @ a2)
    g = jax.nn.sigmoid(xg) @ g2
    kk = (k * k_k).reshape(b, t_len, H, d).astype(jnp.float32)
    kk = kk / jnp.maximum(jnp.sqrt(jnp.sum(kk * kk, axis=-1, keepdims=True)), 1e-12)
    k = k * (1.0 + (a - 1.0) * k_a)
    r_h = r.reshape(b, t_len, H, d).astype(jnp.float32)
    k_h = k.reshape(b, t_len, H, d).astype(jnp.float32)
    v_h = v.reshape(b, t_len, H, d).astype(jnp.float32)
    w_h = decay.reshape(b, t_len, H, d)
    a_h = a.reshape(b, t_len, H, d).astype(jnp.float32)
    xs = tuple(z.transpose(1, 0, 2, 3) for z in (r_h, w_h, k_h, v_h, kk, a_h))

    def step(S, inp):
        r_t, w_t, k_t, v_t, kk_t, a_t = inp
        sa = jnp.einsum('bhvk,bhk->bhv', S, -kk_t)
        S = S * w_t[:, :, None, :] + sa[..., None] * (kk_t * a_t)[:, :, None, :] \
            + v_t[..., None] * k_t[:, :, None, :]
        return S, jnp.einsum('bhvk,bhk->bhv', S, r_t)

    S0 = jnp.zeros((b, H, d, d), jnp.float32)
    _, o = lax.scan(step, S0, xs)
    o = o.transpose(1, 0, 2, 3)
    mean = jnp.mean(o, axis=-1, keepdims=True)
    var = jnp.mean(jnp.square(o - mean), axis=-1, keepdims=True)
    o = (o - mean) * lax.rsqrt(var + GN_EPS) * ln_w + ln_b
    o = o + jnp.sum(r_h * k_h * r_k, axis=-1, keepdims=True) * v_h
    return (o.reshape(b, t_len, H * d) * g).astype(p.dtype)

def peer_ffn(h, w_q, sub_keys, u, v):
    b, t_len, dm = h.shape
    H, K, nk = PEER_HEADS, PEER_TOPK, PEER_N_KEYS
    q = (h @ w_q).reshape(b, t_len, H, 2, PEER_D_QUERY // 2)
    s = jnp.einsum('bthcd,hckd->bthck', q, sub_keys).astype(jnp.float32)
    s_top, i_top = lax.top_k(s, K)
    cand = (s_top[..., 0, :, None] + s_top[..., 1, None, :]).reshape(b, t_len, H, K * K)
    best, j = lax.top_k(cand, K)
    i1 = jnp.take_along_axis(i_top[..., 0, :], j // K, axis=-1)
    i2 = jnp.take_along_axis(i_top[..., 1, :], j % K, axis=-1)
    experts = (i1 * nk + i2).reshape(-1, H * K)
    gates = jax.nn.softmax(best, axis=-1).reshape(-1, H * K)
    n_ch = (b * t_len) // PEER_CHUNK
    xs = (h.reshape(n_ch, PEER_CHUNK, dm),
          experts.reshape(n_ch, PEER_CHUNK, H * K),
          gates.reshape(n_ch, PEER_CHUNK, H * K))

    def chunk(args):
        xc, ec, gc = args
        act = jax.nn.gelu(jnp.einsum('cd,ckd->ck', xc, u[ec]))
        return jnp.einsum('ck,ckd->cd', (act * gc).astype(v.dtype), v[ec])

    return lax.map(chunk, xs).reshape(b, t_len, dm)

def setup_inputs(seed: int = 0) -> dict:
    key = jax.random.key(seed)
    ks = jax.random.split(key, 32)
    L = DEPTH
    f32 = jnp.float32

    def nrm(k, shape, scale):
        return jax.random.normal(k, shape, f32) * scale

    return {
        'x': nrm(ks[0], (BATCH, SEQ, D_MODEL), 1.0),
        'norm_mix_g': 1.0 + nrm(ks[1], (L, D_MODEL), 0.02),
        'w_in': nrm(ks[2], (L, D_MODEL, D_IN), D_MODEL ** -0.5),
        'cmp_k_pe': nrm(ks[3], (L, CMP_LEN, HEAD_DIM), 0.1),
        'cmp_k_w1': nrm(ks[4], (L, CMP_LEN * HEAD_DIM, CMP_HIDDEN), (CMP_LEN * HEAD_DIM) ** -0.5),
        'cmp_k_w2': nrm(ks[5], (L, CMP_HIDDEN, HEAD_DIM), CMP_HIDDEN ** -0.5),
        'cmp_v_pe': nrm(ks[6], (L, CMP_LEN, HEAD_DIM), 0.1),
        'cmp_v_w1': nrm(ks[7], (L, CMP_LEN * HEAD_DIM, CMP_HIDDEN), (CMP_LEN * HEAD_DIM) ** -0.5),
        'cmp_v_w2': nrm(ks[8], (L, CMP_HIDDEN, HEAD_DIM), CMP_HIDDEN ** -0.5),
        'rwkv_mu': jax.random.uniform(ks[9], (L, D_RWKV_IN), f32),
        'rwkv_w0': jax.random.uniform(ks[10], (L, D_RWKV), f32, minval=-4.0, maxval=1.0),
        'rwkv_w2': nrm(ks[11], (L, RANK_W, D_RWKV), RANK_W ** -0.5),
        'rwkv_a0': nrm(ks[12], (L, D_RWKV), 0.5),
        'rwkv_a2': nrm(ks[13], (L, RANK_A, D_RWKV), RANK_A ** -0.5),
        'rwkv_g2': nrm(ks[14], (L, RANK_G, D_RWKV), RANK_G ** -0.5),
        'rwkv_k_k': 0.85 + nrm(ks[15], (L, D_RWKV), 0.05),
        'rwkv_k_a': 1.0 + nrm(ks[16], (L, D_RWKV), 0.05),
        'rwkv_r_k': nrm(ks[17], (L, RWKV_HEADS, HEAD_DIM), 0.1),
        'rwkv_ln_w': 1.0 + nrm(ks[18], (L, RWKV_HEADS, HEAD_DIM), 0.02),
        'rwkv_ln_b': nrm(ks[19], (L, RWKV_HEADS, HEAD_DIM), 0.02),
        'w_out': nrm(ks[20], (L, D_MIX, D_MODEL), D_MIX ** -0.5),
        'norm_ffn_g': 1.0 + nrm(ks[21], (L, D_MODEL), 0.02),
        'peer_w_q': nrm(ks[22], (L, D_MODEL, PEER_HEADS * PEER_D_QUERY), D_MODEL ** -0.5),
        'peer_sub_keys': nrm(ks[23], (L, PEER_HEADS, 2, PEER_N_KEYS, PEER_D_QUERY // 2), (PEER_D_QUERY // 2) ** -0.5),
        'peer_u': nrm(ks[24], (L, PEER_N_EXPERTS, D_MODEL), D_MODEL ** -0.5),
        'peer_v': nrm(ks[25], (L, PEER_N_EXPERTS, D_MODEL), PEER_HEADS ** -0.5),
        'norm_final_g': 1.0 + nrm(ks[26], (D_MODEL,), 0.02),
    }

def reference(x, norm_mix_g, w_in, cmp_k_pe, cmp_k_w1, cmp_k_w2, cmp_v_pe, cmp_v_w1, cmp_v_w2,
              rwkv_mu, rwkv_w0, rwkv_w2, rwkv_a0, rwkv_a2, rwkv_g2, rwkv_k_k, rwkv_k_a, rwkv_r_k,
              rwkv_ln_w, rwkv_ln_b, w_out, norm_ffn_g, peer_w_q, peer_sub_keys, peer_u, peer_v,
              norm_final_g):
    b, t_len, _ = x.shape
    for l in range(DEPTH):
        h = rms_norm(x, norm_mix_g[l])
        p = h @ w_in[l]
        q, kc, vc, ks_, vs_, kw, vw, gl, p_rwkv = split_cols(p, COL_SIZES)
        kv = lambda z: z.reshape(b, t_len, NSA_KV_HEADS, HEAD_DIM)
        gates = jax.nn.sigmoid(gl).reshape(b, t_len, NSA_HEADS, 3)
        y_nsa = nsa_mixer(q, kv(kc), kv(vc), kv(ks_), kv(vs_), kv(kw), kv(vw), gates,
                          cmp_k_pe[l], cmp_k_w1[l], cmp_k_w2[l], cmp_v_pe[l], cmp_v_w1[l], cmp_v_w2[l])
        y_rwkv = rwkv7_mixer(p_rwkv, rwkv_mu[l], rwkv_w0[l], rwkv_w2[l], rwkv_a0[l], rwkv_a2[l],
                             rwkv_g2[l], rwkv_k_k[l], rwkv_k_a[l], rwkv_r_k[l], rwkv_ln_w[l], rwkv_ln_b[l])
        y = jnp.concatenate([y_nsa.astype(x.dtype), y_rwkv.astype(x.dtype)], axis=-1)
        x = x + y @ w_out[l]
        h = rms_norm(x, norm_ffn_g[l])
        x = x + peer_ffn(h, peer_w_q[l], peer_sub_keys[l], peer_u[l], peer_v[l]).astype(x.dtype)
    return rms_norm(x, norm_final_g)


_drawn_inputs = setup_inputs


def setup_inputs(seed=0):
    import zlib

    import numpy as np

    out = dict(_drawn_inputs(seed))
    spreads = {}
    factors = {'cmp_k_pe': 140.254,
     'rwkv_k_k': 3.317,
     'rwkv_ln_w': 10.789,
     'rwkv_ln_b': 9.925,
     'norm_final_g': 22.065,
     'cmp_v_pe': 2.97,
     'norm_ffn_g': 10.868,
     'cmp_k_w1': 3.888,
     'cmp_k_w2': 3.805}
    for name, (base, spread) in spreads.items():
        noise = np.random.default_rng([zlib.crc32(name.encode()), seed]).standard_normal(out[name].shape)
        drawn = base * np.exp(spread * noise) if base else spread * noise
        out[name] = jnp.asarray(drawn.astype(out[name].dtype))
    for name, factor in factors.items():
        out[name] = (out[name] * factor).astype(out[name].dtype)
    return out
```

```python
from contextlib import ExitStack

import concourse.bass as bass
from concourse import mybir

ALU = mybir.AluOpType
ACT = mybir.ActivationFunctionType
F32 = mybir.dt.float32
U32 = mybir.dt.uint32
AX = mybir.AxisListType.X

P = 128
T = 512
NT = T // P
D = 1024
DC = D // P
HD = 64
NH = 8
EPS = 1e-6
GN_EPS = 64e-5
GELU_A = 0.044715
GELU_B = 0.7978845608028654

NRW = 14
CQ, CKC, CVC, CKS, CKW, CR = 0, 4, 5, 6, 7, 8
NCH = CR + NRW
VS, VW, GL, NTOK = 0, 128, 256, 280
TP = T + 1
RING = 4

V_GMIX, V_MU, V_W0, V_A0, V_KK, V_KA, V_RK, V_LW, V_LB, NVEC = 0, 8, 22, 26, 30, 34, 38, 42, 46, 50

CMP_L, CMP_STRIDE, CMP_N = 32, 16, 31
MASKED = -1e34
FLOOR = -1e29


class Shared:
    pass


class Space:

    def __init__(self, whole, at, end):
        self.whole, self.at, self.end = whole, at, end

    def take(self, *shape):
        n = 1
        for s in shape:
            n *= s
        assert self.at + n <= self.end, (self.at, n, self.end)
        v = self.whole[:, self.at:self.at + n]
        self.at += n
        if len(shape) == 2:
            v = v.rearrange("p (a b) -> p a b", b=shape[1])
        elif len(shape) == 3:
            v = v.rearrange("p (a b c) -> p a b c", b=shape[1], c=shape[2])
        elif len(shape) == 4:
            v = v.rearrange("p (a b c d) -> p a b c d", b=shape[1], c=shape[2], d=shape[3])
        return v


def spread(v, n):
    return v.unsqueeze(2).to_broadcast([v.shape[0], v.shape[1], n])


def over(v, n):
    return v.unsqueeze(1).to_broadcast([v.shape[0], n, v.shape[1]])


class Steps:

    def __init__(self, sem, names):
        self.sem, self.names, self.k = sem, list(names), 0
        self.place = {n: j + 1 for j, n in enumerate(self.names)}
        assert len(self.place) == len(self.names)

    def done(self, ins, name):
        assert self.names[self.k] == name, (self.names[self.k], name)
        self.k += 1
        ins.then_inc(self.sem, 1)

    def await_(self, eng, name, i=0):
        eng.wait_ge(self.sem, i * len(self.names) + self.place[name] + 1)

    def await_last_run(self, eng, i):
        eng.wait_ge(self.sem, i * len(self.names) + 1)


def project(nc, K):
    sb, ps, sem = K.sb, K.ps, K.sem
    mem = Space(sb, K.F0, K.NW)
    K.attn = mem.take(CR, TP)
    K.tok = mem.take(NT, NTOK)
    K.F1 = mem.at
    xt = mem.take(NT, D)
    hT = mem.take(DC, T)
    ring = mem.take(2, DC, P)
    wtok = mem.take(DC, NTOK)
    junk = mem.take(D)
    ms = K.stat[:, 0, 0:NT]
    rstd = K.stat[:, 1, 0:NT]
    x_in = [sem(f"x_in{t}") for t in range(NT)]
    small_in, wtok_in = sem("small_in"), sem("wtok_in")
    w_in = [sem("w_in0"), sem("w_in1")]
    const_set = sem("const_set")
    squares, eps_added, rooted, inverted = sem("squares"), sem("eps_added"), sem("rooted"), sem("inverted")
    h_scaled, h_turned, hT_kept = sem("h_scaled"), sem("h_turned"), sem("hT_kept")
    chunk_out = [sem("chunk_out0"), sem("chunk_out1")]
    chunk_kept = [sem("chunk_kept0"), sem("chunk_kept1")]
    tok_out, tok_kept, gate_tanh = sem("tok_out"), sem("tok_kept"), sem("gate_tanh")
    K.small_in, K.const_set = small_in, const_set

    with nc.Block() as block:
        @block.sync
        def _(sp):
            for t in range(NT):
                sp.dma_start(xt[:, t, :], K.x[:, t, :]).then_inc(x_in[t], 16)
            sp.dma_start(K.vec, K.vecs).then_inc(small_in, 16)
            with sp.Fori(0, NCH // 2) as i:
                for s in range(2):
                    sp.wait_ge(chunk_out[s], i + 1)
                    sp.dma_start(ring[:, s, :, :].rearrange("p c n -> p (c n)"),
                                 K.w_ch[2 * i + s]).then_inc(w_in[s], 16)
            sp.dma_start(wtok.rearrange("p c n -> p (c n)"), K.w_tok).then_inc(wtok_in, 16)
            sp.dma_start(K.lw[0:64, :], K.lora_w).then_inc(small_in, 16)
            sp.dma_start(K.lw[64:128, :], K.lora_a).then_inc(small_in, 16)
            sp.dma_start(K.lg, K.lora_g).then_inc(small_in, 16)
            sp.wait_ge(small_in, 64)

        @block.gpsimd
        def _(pool):
            n = [0]

            def step(ins):
                n[0] += 1
                ins.then_inc(const_set, 1)
                pool.wait_ge(const_set, n[0])

            def cut(v, pattern, base, cm, fill=0.0, op=ALU.is_ge):
                step(nc.gpsimd.affine_select(out=v, in_=v, compare_op=op, fill=fill, base=base,
                                             pattern=pattern, channel_multiplier=cm))

            step(nc.gpsimd.memset(K.ident, 0.0))
            cut(K.ident, [[-1, P]], 0, 1, fill=1.0, op=ALU.not_equal)
            K.n_ident = n[0]
            step(nc.gpsimd.memset(K.ones, 1.0))
            step(nc.gpsimd.memset(K.head_sum, 1.0))
            v = K.head_sum.rearrange("p (a b) -> p a b", b=HD)
            cut(v, [[-HD, 2], [0, HD]], 0, 1)
            cut(v, [[HD, 2], [0, HD]], HD - 1, -1)
            step(nc.gpsimd.memset(K.m_d, 1.0))
            v = K.m_d.rearrange("p (a b) -> p a b", b=16)
            cut(v, [[-16, 8], [-1, 16]], -1, 1)
            cut(v, [[16, 8], [0, 16]], 15, -1)
            step(nc.gpsimd.memset(K.m_dt, 1.0))
            v = K.m_dt.rearrange("p (a b) -> p a b", b=16)
            cut(v, [[16, 8], [1, 16]], -1, -1)
            cut(v, [[-16, 8], [0, 16]], 0, 1)
            for k, b in enumerate((16, 32, 64)):
                step(nc.gpsimd.memset(K.m_off[k], 0.0))
                v = K.m_off[k].rearrange("p (a h b) -> p a h b", h=2, b=b)[:, :, 1, :]
                step(nc.gpsimd.memset(v, 1.0))
                nb = P // (2 * b)
                cut(v, [[-2 * b, nb], [0, b]], 0, 1)
                cut(v, [[2 * b, nb], [0, b]], b - 1, -1)
            step(nc.gpsimd.memset(K.m_after, 1.0))
            cut(K.m_after, [[1, P]], -1, -1)
            step(nc.gpsimd.memset(K.m_from, 1.0))
            cut(K.m_from, [[1, P]], 0, -1)
            for h in range(NH):
                step(nc.gpsimd.memset(K.slopes[:, h:h + 1], 2.0 ** (-8.0 * (h + 1) / NH)))
            step(nc.gpsimd.iota(K.iota16, pattern=[[1, 16]], base=0, channel_multiplier=0,
                                allow_small_or_imprecise_dtypes=True))
            step(nc.gpsimd.iota(K.ndist, pattern=[[1, T]], base=-(T - P), channel_multiplier=-1,
                                allow_small_or_imprecise_dtypes=True))
            cut(K.ndist, [[-1, T]], T - P, 1, fill=MASKED)
            step(nc.gpsimd.iota(K.ndcmp, pattern=[[-P, NT], [CMP_STRIDE, 32]], base=CMP_L - 1,
                                channel_multiplier=-1, allow_small_or_imprecise_dtypes=True))
            cut(K.ndcmp, [[P, NT], [-CMP_STRIDE, 32]], -(CMP_L - 1), 1, fill=MASKED)
            step(nc.gpsimd.memset(K.prw[:, :, 0:1], 0.0))
            step(nc.gpsimd.memset(K.attn[:, :, 0:1], 0.0))
            step(nc.gpsimd.memset(K.key_val[:, NT * 16:, :], 0.0))
            step(nc.gpsimd.memset(K.key_idx[:, NT * 16:, :], 0.0))

        @block.vector
        def _(dve):
            dve.sem_inc(chunk_kept[1], 1)
            for t in range(NT):
                dve.wait_ge(x_in[t], 16)
                if t:
                    dve.wait_ge(squares, t)
                nc.vector.tensor_tensor_reduce(out=junk, in0=xt[:, t, :], in1=xt[:, t, :], scale=1.0,
                                               scalar=0.0, op0=ALU.mult, op1=ALU.add,
                                               accum_out=ms[:, t:t + 1]).then_inc(squares, 1)
            dve.wait_ge(squares, NT)
            nc.vector.tensor_scalar(ms, ms, 1.0 / D, EPS, ALU.mult, ALU.add).then_inc(eps_added, 1)
            dve.wait_ge(rooted, 1)
            nc.vector.reciprocal(rstd, rstd).then_inc(inverted, 1)
            dve.wait_ge(inverted, 1)
            for t in range(NT):
                nc.vector.tensor_scalar(xt[:, t, :], xt[:, t, :], rstd[:, t:t + 1], None,
                                        ALU.mult).then_inc(h_scaled, 1)
            dve.wait_ge(small_in, 16)
            for n in range(8):
                t, c0 = n // 2, 4 * (n % 2)
                dve.wait_ge(h_turned, n + 1)
                nc.vector.tensor_tensor(hT[:, c0:c0 + 4, t * P:(t + 1) * P],
                                        ps[:, n % 4, :].rearrange("p (c t) -> p c t", c=4),
                                        spread(K.vec[:, V_GMIX + c0:V_GMIX + c0 + 4], P),
                                        ALU.mult).then_inc(hT_kept, 1)

            with dve.Fori(0, NCH // 2) as i:
                dve.wait_ge(chunk_out[1], i + 2)
                nc.vector.tensor_copy(K.chunk(2 * i + 1), ps[:, 1, :]).then_inc(chunk_kept[1], 1)
            for t in range(NT):
                dve.wait_ge(tok_out, t + 1)
                nc.vector.tensor_copy(K.tok[:, t, :], ps[:, 4 + t, 0:NTOK]).then_inc(tok_kept, 1)
            dve.wait_ge(gate_tanh, 1)
            g = K.tok[:, :, GL:NTOK]
            nc.vector.tensor_scalar(g, g, 0.5, 0.5, ALU.mult, ALU.add).then_inc(tok_kept, 1)

        @block.scalar
        def _(act):
            act.sem_inc(chunk_kept[0], 1)
            act.wait_ge(eps_added, 1)
            nc.scalar.activation(rstd, ms, ACT.Sqrt).then_inc(rooted, 1)
            with act.Fori(0, NCH // 2) as i:
                act.wait_ge(chunk_out[0], i + 2)
                nc.scalar.copy(K.chunk(2 * i), ps[:, 0, :]).then_inc(chunk_kept[0], 1)
            act.wait_ge(tok_kept, NT)
            g = K.tok[:, :, GL:NTOK]
            nc.scalar.activation(g, g, ACT.Tanh, scale=0.5).then_inc(gate_tanh, 1)

        @block.tensor
        def _(pe):
            for s in range(2):
                pe.sem_inc(chunk_out[s], 1)
            pe.wait_ge(const_set, K.n_ident)
            for n in range(8):
                t, c0 = n // 2, 4 * (n % 2)
                pe.wait_ge(h_scaled, t + 1)
                if n >= 4:
                    pe.wait_ge(hT_kept, n - 3)
                for c in range(4):
                    mm = pe.transpose(ps[:, n % 4, c * P:(c + 1) * P],
                                      xt[:, t, (c0 + c) * P:(c0 + c + 1) * P], K.ident)
                mm.then_inc(h_turned, 1)
            pe.wait_ge(hT_kept, 8)
            with pe.Fori(0, NCH // 2) as i:
                for s in range(2):
                    pe.wait_ge(w_in[s], 16 * i + 16)
                    pe.wait_ge(chunk_kept[s], i + 1)
                    for c in range(DC):
                        mm = pe.matmul(ps[:, s, :], ring[:, s, c, :], hT[:, c, :],
                                       start=(c == 0), stop=(c == DC - 1))
                    mm.then_inc(chunk_out[s], 1)
            pe.wait_ge(wtok_in, 16)
            for t in range(NT):
                for c in range(DC):
                    mm = pe.matmul(ps[:, 4 + t, 0:NTOK], hT[:, c, t * P:(t + 1) * P], wtok[:, c, :],
                                   start=(c == 0), stop=(c == DC - 1))
                mm.then_inc(tok_out, 1)

def attend(nc, K):
    ps, sem = K.ps, K.sem
    mem = Space(K.sb, K.F1, K.NW)
    w1 = mem.take(2, CMP_L, P)
    win = mem.take(2, CMP_L, 32)
    pe_t = mem.take(2, CMP_L)
    w2k = mem.take(2, HD)
    w2v = mem.take(HD)
    hid = mem.take(4, 32)
    hid2 = mem.take(4, 32)
    hid3 = mem.take(4, 32)
    kcmp = mem.take(2, 32)
    vcmp = mem.take(2, HD)
    kdup = mem.take(2, 2, T)
    k_g = mem.take(2, T)
    kc_g = mem.take(32)
    v_g = mem.take(2, NT, HD)
    vc_g = mem.take(HD)
    q_p = mem.take(T)
    gate_p = mem.take(NT, 6)
    slope_p = mem.take(2)
    score = mem.take(2, T)
    prob = mem.take(2, T)
    probT = mem.take(2, T)
    top_s = mem.take(2, 1)
    nmax = mem.take(2, 1)
    psum_ = mem.take(2, 1)
    inv = mem.take(2, 1)
    coef = mem.take(2, 1)
    y = mem.take(NT, 2, HD)

    w1_in, pe_in, w2_in, kdup_in = sem("w1_in"), sem("pe_in"), sem("w2_in"), sem("kdup_in")
    win_set, hid_out, gelu_dve, gelu_act = sem("win_set"), sem("hid_out"), sem("gelu_dve"), sem("gelu_act")
    cmp_out, cmp_kept = sem("cmp_out"), sem("cmp_kept")
    group_set, pair_set, q_set = sem("group_set"), sem("pair_set"), sem("q_set")
    score_out, score_kept, max_kept, nmax_kept = (sem(n) for n in ("score_out", "score_kept", "max_kept", "nmax_kept"))
    prob_kept, turned, turned_kept, pv_out, pv_kept = (
        sem(n) for n in ("prob_kept", "prob_turned", "probT_kept", "pv_out", "pv_kept"))
    sum_floored, sum_inverted, coef_kept = sem("sum_floored"), sem("sum_inverted"), sem("coef_kept")
    y_out, yT_kept = sem("y_turned"), sem("yT_kept")

    TASKS = [(hp, t, br) for hp in range(2) for t in range(NT) for br in range(3)]
    N = len(TASKS)

    def width(t, br):
        return 32 if br == 0 else (t + 1) * P

    def after(eng, s, m):
        eng.wait_ge(s, m + 3)

    with nc.Block() as block:
        @block.sync
        def _(sp):
            sp.dma_start(pe_t[0:64, 0, :], K.pe_k).then_inc(pe_in, 16)
            sp.dma_start(pe_t[64:128, 0, :], K.pe_k).then_inc(pe_in, 16)
            sp.dma_start(pe_t[0:64, 1, :], K.pe_v).then_inc(pe_in, 16)
            sp.dma_start(pe_t[64:128, 1, :], K.pe_v).then_inc(pe_in, 16)
            for kv, w in enumerate((K.w1_k, K.w1_v)):
                for g in range(2):
                    sp.dma_start(w1[g * HD:(g + 1) * HD, kv, :, :],
                                 w.rearrange("(l d) n -> d l n", d=HD)).then_inc(w1_in, 16)
            for r in range(2):
                sp.dma_start(w2k[:, r, :], K.w2_k).then_inc(w2_in, 16)
            sp.dma_start(w2v, K.w2_v).then_inc(w2_in, 16)
            for b, c in enumerate((CKS, CKW)):
                for g in range(2):
                    for half in range(2):
                        sp.dma_start(kdup[half * HD:(half + 1) * HD, b, g, :],
                                     K.attn[g * HD:(g + 1) * HD, c, 1:TP]).then_inc(kdup_in, 16)
            sp.wait_ge(kdup_in, 16 * 8)

        @block.gpsimd
        def _(pool):
            pool.wait_ge(kdup_in, 16 * 8)
            pool.wait_ge(cmp_kept, 2)
            with pool.Fori(0, 2) as g:
                after(pool, pv_out, g * 2 * N - 1)
                nc.gpsimd.tensor_copy(k_g, kdup[:, :, g, :]).then_inc(group_set, 1)
                nc.gpsimd.tensor_copy(kc_g, kcmp[:, g, :]).then_inc(group_set, 1)
                for b, c in enumerate((VS, VW)):
                    nc.gpsimd.tensor_copy(v_g[:, b, :, :], K.tok[:, :, bass.ds(c + g * HD, HD)]).then_inc(group_set, 1)
                nc.gpsimd.tensor_copy(vc_g[0:32, :], vcmp[0:32, g, :]).then_inc(group_set, 1)

        @block.tensor
        def _(pe):
            for s in (score_out, turned, pv_out):
                pe.sem_inc(s, 2)
            pe.sem_inc(y_out, 1)
            pe.wait_ge(w1_in, 64)
            for kv in range(2):
                pe.wait_ge(win_set, 1 + 2 * (kv + 1))
                for g in range(2):
                    half = slice(g * HD, (g + 1) * HD)
                    for l in range(CMP_L):
                        mm = pe.matmul(ps[:, 2 * kv + g, 0:32], w1[half, kv, l, :],
                                       win[half, kv, l, :], start=(l == 0), stop=(l == CMP_L - 1))
            mm.then_inc(hid_out, 1)
            pe.wait_ge(gelu_dve, 5)
            pe.wait_ge(w2_in, 48)
            pe.matmul(ps[:, 4, 0:64], w2k.rearrange("p a b -> p (a b)"),
                      hid2[:, 0:2, :].rearrange("p a b -> p (a b)"), start=True, stop=True).then_inc(cmp_out, 1)
            for g in range(2):
                mm = pe.matmul(ps[0:32, 5, g * HD:(g + 1) * HD], hid2[:, 2 + g, :], w2v,
                               start=True, stop=True)
            mm.then_inc(cmp_out, 1)

            with pe.Fori(0, 2) as g, pe.Fori(0, 2) as r:
                p = g * 2 + r
                done = p * N

                def scores(n):
                    hp, t, br = TASKS[n]
                    half = slice(hp * HD, (hp + 1) * HD)
                    if n == 0:
                        pe.wait_ge(q_set, p + 1)
                        pe.wait_ge(group_set, g * 5 + 5)
                    after(pe, score_kept, done + n - 2)
                    keys = kc_g[half, :] if br == 0 else k_g[half, br - 1, 0:width(t, br)]
                    pe.matmul(ps[:, n % 2, 0:width(t, br)], q_p[half, t * P:(t + 1) * P], keys,
                              start=True, stop=True).then_inc(score_out, 1)

                def turn(n):
                    _, t, br = TASKS[n]
                    after(pe, prob_kept, done + n)
                    after(pe, turned_kept, done + n - 2)
                    if br == 0:
                        mm = pe.transpose(ps[0:32, 2 + n % 2, 0:P], prob[:, n % 2, 0:32], K.ident)
                    else:
                        for k in range(t + 1):
                            mm = pe.transpose(ps[:, 2 + n % 2, k * P:(k + 1) * P],
                                              prob[:, n % 2, k * P:(k + 1) * P], K.ident)
                    mm.then_inc(turned, 1)

                def values(n):
                    _, t, br = TASKS[n]
                    after(pe, turned_kept, done + n)
                    after(pe, pv_kept, done + n - 2)
                    if br == 0:
                        mm = pe.matmul(ps[:, 4 + n % 2, 0:HD], probT[0:32, n % 2, 0:P], vc_g[0:32, :],
                                       start=True, stop=True)
                    else:
                        for k in range(t + 1):
                            mm = pe.matmul(ps[:, 4 + n % 2, 0:HD], probT[:, n % 2, k * P:(k + 1) * P],
                                           v_g[:, br - 1, k, :], start=(k == 0), stop=(k == t))
                    mm.then_inc(pv_out, 1)

                scores(0)
                for n in range(N):
                    if n + 1 < N:
                        scores(n + 1)
                    turn(n)
                    if n:
                        values(n - 1)
                values(N - 1)
                after(pe, pv_kept, done + N - 1)
                pe.wait_ge(yT_kept, p + 1)
                for t in range(NT):
                    mm = pe.transpose(ps[:, 6, t * P:(t + 1) * P], y[:, t, :, :].rearrange("p a b -> p (a b)"),
                                      K.ident)
                mm.then_inc(y_out, 1)

        @block.vector
        def _(dve):
            for s in (score_kept, max_kept, nmax_kept, sum_floored, sum_inverted, coef_kept, pv_kept):
                dve.sem_inc(s, 2)
            dve.sem_inc(yT_kept, 1)
            nc.vector.memset(win.rearrange("p a b c -> p (a b c)"), 0.0).then_inc(win_set, 1)
            dve.wait_ge(win_set, 1)
            dve.wait_ge(pe_in, 64)
            for kv, c in enumerate((CKC, CVC)):
                for lh in range(2):
                    src = K.attn[:, c, 1 + 16 * lh:1 + 16 * lh + 16 * CMP_N].rearrange(
                        "p (n l) -> p l n", l=16)
                    nc.vector.tensor_tensor(win[:, kv, 16 * lh:16 * lh + 16, 0:CMP_N], src,
                                            spread(pe_t[:, kv, 16 * lh:16 * lh + 16], CMP_N),
                                            ALU.add).then_inc(win_set, 1)
            dve.wait_ge(hid_out, 1)
            nc.vector.tensor_copy(hid, ps[:, 0:4, 0:32]).then_inc(gelu_dve, 1)
            dve.wait_ge(gelu_dve, 1)
            nc.vector.tensor_tensor(hid2, hid, hid, ALU.mult).then_inc(gelu_dve, 1)
            dve.wait_ge(gelu_dve, 2)
            nc.vector.tensor_scalar(hid2, hid2, GELU_A, 1.0, ALU.mult, ALU.add).then_inc(gelu_dve, 1)
            dve.wait_ge(gelu_dve, 3)
            nc.vector.tensor_tensor(hid3, hid2, hid, ALU.mult).then_inc(gelu_dve, 1)
            dve.wait_ge(gelu_act, 2)
            nc.vector.scalar_tensor_tensor(out=hid2.rearrange("p a b -> p (a b)"),
                                           in0=hid3.rearrange("p a b -> p (a b)"), scalar=1.0,
                                           in1=hid.rearrange("p a b -> p (a b)"),
                                           op0=ALU.add, op1=ALU.mult).then_inc(gelu_dve, 1)
            dve.wait_ge(cmp_out, 2)
            nc.vector.tensor_copy(kcmp.rearrange("p a b -> p (a b)"), ps[:, 4, 0:64]).then_inc(cmp_kept, 1)
            nc.vector.tensor_copy(vcmp[0:32, :, :].rearrange("p a b -> p (a b)"),
                                  ps[0:32, 5, 0:2 * HD]).then_inc(cmp_kept, 1)

            with dve.Fori(0, 4) as p:
                done = p * N

                def bias(n):
                    hp, t, br = TASKS[n]
                    w = width(t, br)
                    dist = K.ndcmp[:, t, :] if br == 0 else K.ndist[:, T - w:T]
                    s = score[:, n % 2, 0:w]
                    after(dve, score_out, done + n)
                    after(dve, prob_kept, done + n - 2)
                    nc.vector.scalar_tensor_tensor(out=s, in0=dist, scalar=slope_p[:, hp:hp + 1],
                                                   in1=ps[:, n % 2, 0:w], op0=ALU.mult,
                                                   op1=ALU.add).then_inc(score_kept, 1)
                    after(dve, score_kept, done + n)
                    nc.vector.tensor_reduce(top_s[:, n % 2, :], s, AX, ALU.max).then_inc(max_kept, 1)
                    after(dve, max_kept, done + n)
                    nc.vector.tensor_scalar(nmax[:, n % 2, :], top_s[:, n % 2, :], FLOOR, -1.0,
                                            ALU.max, ALU.mult).then_inc(nmax_kept, 1)

                def weigh(n):
                    hp, t, br = TASKS[n]
                    b = n % 2
                    after(dve, prob_kept, done + n)
                    nc.vector.tensor_scalar(psum_[:, b, :], psum_[:, b, :], 1e-30, None,
                                            ALU.max).then_inc(sum_floored, 1)
                    after(dve, sum_floored, done + n)
                    nc.vector.reciprocal(inv[:, b, :], psum_[:, b, :]).then_inc(sum_inverted, 1)
                    after(dve, sum_inverted, done + n)
                    k = 3 * hp + br
                    nc.vector.tensor_tensor(coef[:, b, :], inv[:, b, :], gate_p[:, t, k:k + 1],
                                            ALU.mult).then_inc(coef_kept, 1)
                    after(dve, coef_kept, done + n)
                    after(dve, pv_out, done + n)
                    out = y[:, t, hp, :]
                    o = ps[:, 4 + b, 0:HD]
                    if br == 0:
                        if n == 0:
                            dve.wait_ge(y_out, p + 1)
                        ins = nc.vector.tensor_scalar(out, o, coef[:, b, :], None, ALU.mult)
                    else:
                        after(dve, pv_kept, done + n - 1)
                        ins = nc.vector.scalar_tensor_tensor(out=out, in0=o, scalar=coef[:, b, :], in1=out,
                                                             op0=ALU.mult, op1=ALU.add)
                    ins.then_inc(pv_kept, 1)

                after(dve, score_out, done - 1)
                nc.vector.tensor_scalar(q_p, K.attn[:, CQ + p, 1:TP], HD ** -0.5, None,
                                        ALU.mult).then_inc(q_set, 1)
                nc.vector.tensor_copy(gate_p, K.tok[:, :, bass.ds(GL + p * 6, 6)]).then_inc(pair_set, 1)
                nc.vector.tensor_copy(slope_p, K.slopes[:, bass.ds(p * 2, 2)]).then_inc(pair_set, 1)
                dve.wait_ge(pair_set, 2 * p + 2)
                bias(0)
                bias(1)
                for n in range(N):
                    weigh(n)
                    if n + 2 < N:
                        bias(n + 2)
                dve.wait_ge(y_out, p + 2)
                nc.vector.tensor_copy(K.yT[:, p, :], ps[:, 6, :]).then_inc(yT_kept, 1)

        @block.scalar
        def _(act):
            act.wait_ge(gelu_dve, 4)
            nc.scalar.activation(hid3, hid3, ACT.Tanh, scale=GELU_B).then_inc(gelu_act, 1)
            act.wait_ge(gelu_act, 1)
            nc.scalar.mul(hid, hid, 0.5).then_inc(gelu_act, 1)
            for s in (prob_kept, turned_kept):
                act.sem_inc(s, 2)
            with act.Fori(0, 4) as p:
                done = p * N

                def exps(n):
                    _, t, br = TASKS[n]
                    w = width(t, br)
                    after(act, nmax_kept, done + n)
                    after(act, turned, done + n - 2)
                    after(act, coef_kept, done + n - 2)
                    nc.scalar.activation(prob[:, n % 2, 0:w], score[:, n % 2, 0:w], ACT.Exp,
                                         bias=nmax[:, n % 2, :], accum_out=psum_[:, n % 2, :]).then_inc(prob_kept, 1)

                def keep_turned(n):
                    _, t, br = TASKS[n]
                    after(act, turned, done + n)
                    after(act, pv_out, done + n - 2)
                    rows, w = (32, P) if br == 0 else (P, width(t, br))
                    nc.scalar.copy(probT[0:rows, n % 2, 0:w], ps[0:rows, 2 + n % 2, 0:w]).then_inc(turned_kept, 1)

                exps(0)
                for n in range(N):
                    if n + 1 < N:
                        exps(n + 1)
                    keep_turned(n)

DECAY = 0.6065306597126334


def recur(nc, K):
    ps, sem = K.ps, K.sem
    mem = Space(K.sb, K.F0, K.NW)
    K.w_out_sb = mem.take(8, D)
    diff = mem.take(NRW, P)
    m = mem.take(NRW, P)
    xw = mem.take(P)
    sg = mem.take(P)
    c4 = lambda: mem.take(4, P)
    ld, lam, a, gg, kk, gr, gi, gp = (c4() for _ in range(8))
    rT, kT, bT, aT, bonus, o, sq = (c4() for _ in range(7))
    b_tok, k_tok, v_tok = (c4() for _ in range(3))
    em, em_exp = mem.take(4), mem.take(4)
    S = mem.take(4, HD)
    Sh = mem.take(4, HD)
    rhs = [mem.take(4, HD) for _ in range(2)]
    SA = [mem.take(4, HD) for _ in range(2)]
    G2 = lambda: [mem.take(4, P) for _ in range(2)]
    Dm, DTm, AkT, RbT, RkT, Tm, TT, X2, X2T, X4, X4T, Y = (G2() for _ in range(12))
    A_T = [diff[:, 4 * g:4 * g + 4, :] for g in range(2)]
    X8T = X2T
    off = [[mem.take(4, P) for _ in range(3)] for _ in range(2)]
    r, k, v = m[:, 0:4, :], m[:, 4:8, :], m[:, 8:12, :]
    vec = lambda at, n=4: spread(K.vec[:, at:at + n], P)
    flat = lambda z: z.rearrange("p a b -> p (a b)")
    bank = lambda b: ps[:, b, :].rearrange("p (a b) -> p a b", b=P)

    wout_in = sem("wout_in")
    K.wout_in = wout_in
    GR = range(2)
    LV = range(3)
    D_ = Steps(sem("recur_dve_step"),
               ["diff", "mixed_in", "m", "sg", "zw", "ld", "za", "a", "kk0", "kk_sq", "norm_floor",
                "norm_inv", "kk", "a1", "k", "scan0", "scan1", "scan2", "scan3", "lam_rel", "lam_prev",
                "rT", "kT", "ba", "bT", "aT", "Sh", "rk", "rk2", "bonus"]
               + [f"{n}{g}" for g in GR for n in ("D", "DT", "T0", "AkT", "RbT", "RkT")]
               + [f"{n}{g}" for n in ("T1", "T2", "T3") for g in GR]
               + [f"{n}_{l}{g}" for l in LV for n in ("T", "TT") for g in GR if (n, l) != ("T", 2)]
               + ["S_add", "S", "oc", "o_sq", "var", "std_inv", "on", "ow", "ob", "o_bonus", "y"])
    A_ = Steps(sem("recur_act_step"),
               ["xw", "sg", "gg", "ld", "a", "norm", "em", "em_exp", "gr", "gi", "gp", "b_tok", "k_tok", "v_tok"]
               + [f"A_T{g}" for g in GR]
               + [f"{n}{g}" for n in ("X2", "X2T", "X4", "X4T", "X8T", "TT") for g in GR]
               + [f"Y{l}{g}" for l in LV for g in GR]
               + [f"rhs{g}" for g in GR] + [f"SA{g}" for g in GR] + ["o", "std"])
    G_ = Steps(sem("recur_pool_step"), [f"off{l}{g}" for g in GR for l in LV])
    P_ = Steps(sem("recur_pe_step"),
               ["zw", "za", "zg", "norm", "bonus", "b_tok", "k_tok", "v_tok"]
               + [f"{n}{g}" for g in GR for n in ("A", "A_T", "AkT", "RbT", "RkT")]
               + [f"{n}{g}" for n in ("X2", "X2T", "T1", "X4", "X4T", "T2", "X8T", "T3", "TT") for g in GR]
               + [f"{n}_{l}{g}" for l in LV for n in ("Y", "T", "TT") for g in GR if (n, l) != ("T", 2)]
               + [f"rhs{g}" for g in GR] + [f"SA{g}" for g in GR] + ["o", "S", "mean", "var"])

    BANK = {"zw": 0, "za": 1, "zg": 2, "norm": 3, "bonus": 4, "b_tok": 5, "k_tok": 6, "v_tok": 7,
            "o": 0, "S": 4, "mean": 1, "var": 5}
    for g in GR:
        for j, n in enumerate(("A", "A_T", "AkT", "RbT", "RkT")):
            BANK[f"{n}{g}"] = 4 * g + j % 4
        for j, n in enumerate(("X2", "X2T", "T1", "X4", "X4T", "T2", "X8T", "T3", "TT")):
            BANK[f"{n}{g}"] = 4 * g + (j + 1) % 4
        for l in LV:
            for j, n in enumerate(("Y", "T", "TT")):
                BANK[f"{n}_{l}{g}"] = 4 * g + (3 * l + j + 2) % 4
        BANK[f"rhs{g}"] = 4 * g + 2
        BANK[f"SA{g}"] = 4 * g + 3
    READ = {"zw": (D_, "zw"), "za": (D_, "za"), "zg": (A_, "gg"), "norm": (A_, "norm"),
            "bonus": (D_, "bonus"), "b_tok": (A_, "b_tok"), "k_tok": (A_, "k_tok"), "v_tok": (A_, "v_tok"),
            "o": (A_, "o"), "S": (D_, "S_add"), "mean": (D_, "oc"), "var": (D_, "var")}
    for g in GR:
        READ[f"A{g}"], READ[f"A_T{g}"] = (D_, f"D{g}"), (D_, f"DT{g}")
        for n in ("AkT", "RbT", "RkT", "T1", "T2", "T3"):
            READ[f"{n}{g}"] = (D_, f"{n}{g}")
        for n in ("X2", "X2T", "X4", "X4T", "X8T", "TT", "rhs", "SA"):
            READ[f"{n}{g}"] = (A_, f"{n}{g}")
        for l in LV:
            READ[f"Y_{l}{g}"] = (A_, f"Y{l}{g}")
            READ[f"T_{l}{g}"], READ[f"TT_{l}{g}"] = (D_, f"T_{l}{g}"), (D_, f"TT_{l}{g}")

    with nc.Block() as block:
        @block.sync
        def _(sp):
            sp.dma_start(flat(K.w_out_sb), K.w_out).then_inc(wout_in, 16)
            sp.wait_ge(wout_in, 16)

        @block.gpsimd
        def _(pool):
            pool.sem_inc(G_.sem, 1)
            with pool.Fori(0, NT) as i:
                G_.k = 0
                for g in GR:
                    for l in LV:
                        if l == 0:
                            A_.await_(pool, f"A_T{g}", i)
                            if g == 0:
                                P_.await_last_run(pool, i)
                        G_.done(nc.gpsimd.tensor_tensor(off[g][l], A_T[g], over(K.m_off[l], 4), ALU.mult),
                                f"off{l}{g}")

        @block.vector
        def _(dve):
            vt = nc.vector
            tt, ts, stt = vt.tensor_tensor, vt.tensor_scalar, vt.scalar_tensor_tensor
            mul, add = ALU.mult, ALU.add
            vt.memset(flat(S), 0.0).then_inc(D_.sem, 1)
            with dve.Fori(0, NT) as i:
                D_.k = 0

                def w(*names):
                    for n in names:
                        D_.await_(dve, n, i)

                def wa(*names):
                    for n in names:
                        A_.await_(dve, n, i)

                def wp(*names):
                    for n in names:
                        P_.await_(dve, n, i)

                A_.await_last_run(dve, i)
                P_.await_last_run(dve, i)
                D_.await_last_run(dve, i)
                now = K.prw[:, :, bass.ds(i * P + 1, P)]
                D_.done(tt(diff, K.prw[:, :, bass.ds(i * P, P)], now, ALU.subtract), "diff")
                w("diff")
                D_.done(tt(diff, diff, vec(V_MU, NRW), mul), "mixed_in")
                w("mixed_in")
                D_.done(tt(m, diff, now, add), "m")
                wa("sg")
                D_.done(ts(sg, sg, 0.5, 0.5, mul, add), "sg")
                wp("zw")
                D_.done(tt(ld, bank(0), vec(V_W0), add), "zw")
                wa("ld")
                D_.done(ts(ld, ld, -DECAY / 2, -DECAY / 2, mul, add), "ld")
                wp("za")
                D_.done(tt(a, bank(1), vec(V_A0), add), "za")
                wa("a")
                D_.done(ts(a, a, 0.5, 0.5, mul, add), "a")
                D_.done(tt(kk, k, vec(V_KK), mul), "kk0")
                w("kk0")
                D_.done(tt(sq, kk, kk, mul), "kk_sq")
                wa("norm")
                D_.done(ts(sq, sq, 1e-12, None, ALU.max), "norm_floor")
                w("norm_floor")
                D_.done(vt.reciprocal(flat(sq), flat(sq)), "norm_inv")
                w("norm_inv")
                D_.done(tt(kk, kk, sq, mul), "kk")
                w("a", "kk")
                D_.done(stt(out=sq, in0=a, scalar=-1.0, in1=vec(V_KA), op0=add, op1=mul), "a1")
                w("a1")
                D_.done(stt(out=k, in0=sq, scalar=1.0, in1=k, op0=add, op1=mul), "k")
                w("ld")
                for c in range(4):
                    D_.done(vt.tensor_tensor_scan(lam[:, c, :], K.ones, ld[:, c, :], 0.0, mul, add), f"scan{c}")
                w("scan3")
                wa("em_exp")
                D_.done(tt(lam, lam, spread(em, P), ALU.subtract), "lam_rel")
                w("lam_rel")
                D_.done(tt(gp, lam, ld, ALU.subtract), "lam_prev")
                wa("gp")
                w("k")
                D_.done(tt(rT, r, gr, mul), "rT")
                D_.done(tt(kT, k, gi, mul), "kT")
                D_.done(tt(bT, kk, a, mul), "ba")
                w("ba")
                D_.done(tt(bT, bT, gi, mul), "bT")
                D_.done(stt(out=aT, in0=kk, scalar=-1.0, in1=gp, op0=mul, op1=mul), "aT")
                D_.done(tt(Sh, S, spread(em_exp, HD), mul), "Sh")
                D_.done(tt(sq, r, k, mul), "rk")
                w("rk")
                D_.done(tt(sq, sq, vec(V_RK), mul), "rk2")
                wp("bonus")
                D_.done(tt(bonus, bank(4), v, mul), "bonus")
                for g in GR:
                    b0 = 4 * g
                    wp(f"A{g}")
                    D_.done(tt(Dm[g], bank(b0), over(K.m_d, 4), mul), f"D{g}")
                    wp(f"A_T{g}")
                    wa(f"A_T{g}")
                    D_.done(tt(DTm[g], bank(b0 + 1), over(K.m_dt, 4), mul), f"DT{g}")
                    w(f"D{g}")
                    D_.done(tt(Tm[g], Dm[g], over(K.ident, 4), add), f"T0{g}")
                    for j, (n, dst, mask) in enumerate((("AkT", AkT, K.m_after), ("RbT", RbT, K.m_from),
                                                        ("RkT", RkT, K.m_from))):
                        wp(f"{n}{g}")
                        D_.done(tt(dst[g], bank(BANK[f"{n}{g}"]), over(mask, 4), mul), f"{n}{g}")
                for n in ("T1", "T2", "T3"):
                    for g in GR:
                        wp(f"{n}{g}")
                        D_.done(tt(Tm[g], bank(BANK[f"{n}{g}"]), Tm[g], add), f"{n}{g}")
                for l in LV:
                    for n, dst in (("T", Tm), ("TT", TT)):
                        for g in GR:
                            if (n, l) == ("T", 2):
                                continue
                            if n == "T":
                                wp(f"T_{l}{g}")
                            else:
                                wp(f"TT_{l}{g}")
                            D_.done(tt(dst[g], bank(BANK[f"{n}_{l}{g}"]), dst[g], add), f"{n}_{l}{g}")
                wp("S")
                D_.done(tt(S, ps[:, 4, 0:4 * HD].rearrange("p (a b) -> p a b", b=HD), Sh, add), "S_add")
                w("S_add")
                D_.done(tt(S, S, gr[:, :, P - 1:P].to_broadcast([P, 4, HD]), mul), "S")
                wp("mean")
                D_.done(stt(out=o, in0=bank(1), scalar=-1.0 / HD, in1=o, op0=mul, op1=add), "oc")
                w("oc")
                D_.done(tt(sq, o, o, mul), "o_sq")
                wp("var")
                D_.done(ts(sq, bank(5), 1.0 / HD, GN_EPS, mul, add), "var")
                wa("std")
                D_.done(vt.reciprocal(flat(sq), flat(sq)), "std_inv")
                w("std_inv")
                D_.done(tt(o, o, sq, mul), "on")
                w("on")
                D_.done(tt(o, o, vec(V_LW), mul), "ow")
                w("ow")
                D_.done(tt(o, o, vec(V_LB), add), "ob")
                w("ob")
                D_.done(tt(o, o, bonus, add), "o_bonus")
                w("o_bonus")
                D_.done(tt(K.yT[:, 4:8, bass.ds(i * P, P)], o, gg, mul), "y")

        @block.scalar
        def _(act):
            f = nc.scalar.activation
            act.sem_inc(A_.sem, 1)
            with act.Fori(0, NT) as i:
                A_.k = 0

                def w(*names):
                    for n in names:
                        D_.await_(act, n, i)

                def wp(*names):
                    for n in names:
                        P_.await_(act, n, i)

                w("m")
                A_.done(f(xw[0:HD, :], m[0:HD, 12, :], ACT.Tanh), "xw")
                A_.done(f(sg, m[:, 13, :], ACT.Tanh, scale=0.5), "sg")
                wp("zg")
                A_.done(nc.scalar.copy(gg, bank(2)), "gg")
                w("zw")
                A_.done(f(ld, ld, ACT.Tanh, scale=0.5), "ld")
                w("za")
                A_.done(f(a, a, ACT.Tanh, scale=0.5), "a")
                wp("norm")
                A_.done(f(sq, bank(3), ACT.Sqrt), "norm")
                w("scan3")
                A_.done(nc.scalar.copy(em, lam[:, :, 63]), "em")
                A_.done(f(em_exp, lam[:, :, 63], ACT.Exp), "em_exp")
                w("lam_rel")
                A_.done(f(gr, lam, ACT.Exp), "gr")
                A_.done(f(gi, lam, ACT.Exp, scale=-1.0), "gi")
                w("lam_prev")
                A_.done(f(gp, gp, ACT.Exp), "gp")
                for n, dst in (("b_tok", b_tok), ("k_tok", k_tok), ("v_tok", v_tok)):
                    wp(n)
                    A_.done(nc.scalar.copy(dst, bank(BANK[n])), n)
                for g in GR:
                    wp(f"A_T{g}")
                    A_.done(nc.scalar.copy(A_T[g], bank(4 * g + 1)), f"A_T{g}")
                for n, dst in (("X2", X2), ("X2T", X2T), ("X4", X4), ("X4T", X4T), ("X8T", X8T), ("TT", TT)):
                    for g in GR:
                        wp(f"{n}{g}")
                        A_.done(nc.scalar.copy(dst[g], bank(BANK[f"{n}{g}"])), f"{n}{g}")
                for l in LV:
                    for g in GR:
                        wp(f"Y_{l}{g}")
                        A_.done(nc.scalar.copy(Y[g], bank(BANK[f"Y_{l}{g}"])), f"Y{l}{g}")
                for n, dst in (("rhs", rhs), ("SA", SA)):
                    for g in GR:
                        wp(f"{n}{g}")
                        A_.done(nc.scalar.copy(flat(dst[g]), ps[:, BANK[f"{n}{g}"], 0:4 * HD]), f"{n}{g}")
                wp("o")
                A_.done(nc.scalar.copy(o, bank(0)), "o")
                w("var")
                A_.done(f(sq, sq, ACT.Sqrt), "std")

        @block.tensor
        def _(pe):
            pe.sem_inc(P_.sem, 1)
            with pe.Fori(0, NT) as i:
                P_.k = 0
                held = {}

                def w(*names):
                    for n in names:
                        D_.await_(pe, n, i)

                def wa(*names):
                    for n in names:
                        A_.await_(pe, n, i)

                def free(name):
                    if BANK[name] in held:
                        steps, n = READ[held[BANK[name]]]
                        steps.await_(pe, n, i)
                    held[BANK[name]] = name

                w("m")
                wa("xw")
                free("zw")
                for c in range(4):
                    mm = pe.matmul(bank(0)[:, c, :], K.lw[0:HD, c * P:(c + 1) * P], xw[0:HD, :],
                                   start=True, stop=True)
                P_.done(mm, "zw")
                free("za")
                for c in range(4):
                    mm = pe.matmul(bank(1)[:, c, :], K.lw[HD:P, c * P:(c + 1) * P], m[HD:P, 12, :],
                                   start=True, stop=True)
                P_.done(mm, "za")
                w("sg")
                free("zg")
                for c in range(4):
                    mm = pe.matmul(bank(2)[:, c, :], K.lg[:, c * P:(c + 1) * P], sg, start=True, stop=True)
                P_.done(mm, "zg")
                w("kk_sq")
                free("norm")
                P_.done(pe.matmul(ps[:, 3, :], K.head_sum, flat(sq), start=True, stop=True), "norm")
                w("rk2")
                free("bonus")
                P_.done(pe.matmul(ps[:, 4, :], K.head_sum, flat(sq), start=True, stop=True), "bonus")
                for n, src in (("b_tok", bT), ("k_tok", kT), ("v_tok", v)):
                    free(n)
                    for c in range(4):
                        mm = pe.transpose(bank(BANK[n])[:, c, :], src[:, c, :], K.ident)
                    P_.done(mm, n)

                def heads(name, g, lhs, rhs_, n=P):
                    free(f"{name}{g}")
                    for c in range(4):
                        mm = pe.matmul(ps[:, BANK[f"{name}{g}"], c * n:(c + 1) * n], lhs[:, c, :],
                                       rhs_[:, c, :], start=True, stop=True)
                    P_.done(mm, f"{name}{g}")

                for g in GR:
                    h = slice(g * HD, (g + 1) * HD)
                    heads("A", g, aT[h], bT[h])
                    heads("A_T", g, bT[h], aT[h])
                    heads("AkT", g, kT[h], aT[h])
                    heads("RbT", g, bT[h], rT[h])
                    heads("RkT", g, kT[h], rT[h])
                for name, lhs, r_, need, needa in (
                        ("X2", DTm, Dm, ("DT",), ()), ("X2T", Dm, DTm, (), ()),
                        ("T1", X2T, Tm, ("T0",), ("X2T",)),
                        ("X4", X2T, X2, (), ("X2",)), ("X4T", X2, X2T, (), ()),
                        ("T2", X4T, Tm, ("T1",), ("X4T",)),
                        ("X8T", X4, X4T, (), ()), ("T3", X8T, Tm, ("T2",), ("X8T",))):
                    for g in GR:
                        w(*(n + str(g) for n in need))
                        wa(*(n + str(g) for n in needa))
                        heads(name, g, lhs[g], r_[g])
                for g in GR:
                    w(f"T3{g}")
                    free(f"TT{g}")
                    for c in range(4):
                        mm = pe.transpose(bank(BANK[f"TT{g}"])[:, c, :], Tm[g][:, c, :], K.ident)
                    P_.done(mm, f"TT{g}")
                for l in LV:
                    for g in GR:
                        G_.await_(pe, f"off{l}{g}", i)
                        if l:
                            w(f"T_{l - 1}{g}")
                        heads(f"Y_{l}", g, off[g][l], Tm[g])
                    if l < 2:
                        for g in GR:
                            wa(f"Y{l}{g}", f"TT{g}")
                            if l:
                                w(f"TT_{l - 1}{g}")
                            heads(f"T_{l}", g, TT[g], Y[g])
                    for g in GR:
                        wa(f"Y{l}{g}", f"TT{g}")
                        if l:
                            w(f"TT_{l - 1}{g}")
                        heads(f"TT_{l}", g, Y[g], TT[g])
                for g in GR:
                    h = slice(g * HD, (g + 1) * HD)
                    free(f"rhs{g}")
                    for c in range(4):
                        dst = ps[:, BANK[f"rhs{g}"], c * HD:(c + 1) * HD]
                        pe.matmul(dst, AkT[g][:, c, :], v_tok[:, c, h], start=True, stop=False)
                        mm = pe.matmul(dst, aT[h, c, :], Sh[h, c, :], start=False, stop=True)
                    P_.done(mm, f"rhs{g}")
                for g in GR:
                    w(f"TT_2{g}")
                    wa(f"rhs{g}")
                    heads("SA", g, TT[g], rhs[g], HD)
                wa("SA1")
                free("o")
                for g in GR:
                    h = slice(g * HD, (g + 1) * HD)
                    for c in range(4):
                        dst = ps[h, 0, c * P:(c + 1) * P]
                        pe.matmul(dst, v_tok[:, c, h], RkT[g][:, c, :], start=True, stop=False)
                        pe.matmul(dst, SA[g][:, c, :], RbT[g][:, c, :], start=False, stop=False)
                        mm = pe.matmul(dst, Sh[h, c, :], rT[h, c, :], start=False, stop=True)
                P_.done(mm, "o")
                free("S")
                for g in GR:
                    h = slice(g * HD, (g + 1) * HD)
                    for c in range(4):
                        dst = ps[h, 4, c * HD:(c + 1) * HD]
                        pe.matmul(dst, b_tok[:, c, h], SA[g][:, c, :], start=True, stop=False)
                        mm = pe.matmul(dst, k_tok[:, c, h], v_tok[:, c, h], start=False, stop=True)
                P_.done(mm, "S")
                wa("o")
                free("mean")
                P_.done(pe.matmul(ps[:, 1, :], K.head_sum, flat(o), start=True, stop=True), "mean")
                w("o_sq")
                free("var")
                P_.done(pe.matmul(ps[:, 5, :], K.head_sum, flat(sq), start=True, stop=True), "var")


def mix(nc, K):
    ps, sem = K.ps, K.sem
    mem = Space(K.sb, K.F0 + 8 * D, K.TOP)
    h2T = mem.take(DC, T)
    g_row = mem.take(D)
    junk = mem.take(D)
    ring = K.sb[:, K.LOW:K.LOW + 2 * 9 * P].rearrange("p (s c n) -> p s c n", s=2, n=P)
    assert K.LOW + 2 * 9 * P <= K.F0 - NRW * TP - 8 * T
    q_sb = Space(K.sb, mem.at, K.TOP).take(2, T)
    old = Space(K.sb, K.F0 - NRW * TP, K.F0)
    sc = old.take(2, NT, P)
    sc2 = old.take(2, NT, P)
    val = old.take(2, NT, 16)
    idx = old.take(2, NT, 16).bitcast(U32)
    ms, rstd = K.stat[:, 0, 0:NT], K.stat[:, 1, 0:NT]
    x_in, g_in = sem("x_again"), sem("g_ffn_in")
    y_out, x_added, sq_kept, eps_kept, rooted, inverted = (
        sem(n) for n in ("mixed_out", "x_added", "sq2_kept", "eps2_kept", "rooted2", "inverted2"))
    waited = sem("waited")
    h_kept, h_turned = sem("h2_kept"), sem("h2_turned")
    hT_kept = [sem("h2T_kept_act"), sem("h2T_kept_dve")]
    wq_in = [sem("wq_in0"), sem("wq_in1")]
    q_out, q_kept, s_out, s_kept = sem("query_out"), sem("query_kept"), sem("key_score_out"), sem("key_score_kept")
    top = Steps(sem("top_key_step"), [f"{n}{t}" for n in ("max", "idx", "cut", "max2", "idx2") for t in range(NT)]
                + ["val", "index"])
    key_val = K.key_val[:, 0:NT * 16, :].rearrange("p (t k) j -> p t k j", t=NT)
    key_idx = K.key_idx[:, 0:NT * 16, :].rearrange("p (t k) j -> p t k j", t=NT)

    with nc.Block() as block:
        @block.sync
        def _(sp):
            sp.dma_start(K.x1.rearrange("p t d -> p (t d)"), K.x.rearrange("p t d -> p (t d)")).then_inc(x_in, 16)
            sp.dma_start(g_row, K.g_ffn.to_broadcast([P, D])).then_inc(g_in, 16)
            with sp.Fori(0, 8) as i:
                for s in range(2):
                    sp.wait_ge(s_out, 2 * i + s + 1)
                    sp.dma_start(ring[:, s, :, :].rearrange("p c n -> p (c n)"),
                                 K.wq_sk[2 * i + s]).then_inc(wq_in[s], 16)
            sp.wait_ge(wq_in[1], 16 * 8)

        @block.tensor
        def _(pe):
            pe.sem_inc(q_out, 2)
            pe.sem_inc(s_out, 2)
            pe.wait_ge(K.wout_in, 16)
            for n in range(2 * NT):
                t, half = n // 2, n % 2
                for c in range(8):
                    mm = pe.matmul(ps[:, n, :], K.yT[:, c, t * P:(t + 1) * P],
                                   K.w_out_sb[:, c, half * 512:(half + 1) * 512],
                                   start=(c == 0), stop=(c == 7))
                mm.then_inc(y_out, 1)
            for n in range(2 * NT):
                t, c0 = n // 2, 4 * (n % 2)
                pe.wait_ge(h_kept, t + 1)
                for c in range(4):
                    mm = pe.transpose(ps[:, n, c * P:(c + 1) * P], K.h2[:, t, (c0 + c) * P:(c0 + c + 1) * P],
                                      K.ident)
                mm.then_inc(h_turned, 1)
            pe.wait_ge(hT_kept[0], 4)
            pe.wait_ge(hT_kept[1], 4)
            with pe.Fori(0, 8) as i:
                for s in range(2):
                    pe.wait_ge(wq_in[s], 16 * i + 16)
                    pe.wait_ge(q_kept, 2 * i + s + 1)
                    for c in range(DC):
                        mm = pe.matmul(ps[:, s, :], ring[:, s, c, :], h2T[:, c, :],
                                       start=(c == 0), stop=(c == DC - 1))
                    mm.then_inc(q_out, 1)
                for s in range(2):
                    pe.wait_ge(q_kept, 2 * i + s + 3)
                    pe.wait_ge(s_kept, 2 * i + s + 1)
                    for t in range(NT):
                        mm = pe.matmul(ps[:, 2 + s, t * P:(t + 1) * P], q_sb[:, s, t * P:(t + 1) * P],
                                       ring[:, s, DC, :], start=True, stop=True)
                    mm.then_inc(s_out, 1)

        @block.scalar
        def _(act):
            act.sem_inc(q_kept, 2)
            act.wait_ge(eps_kept, 1)
            for t in range(NT):
                act.wait_ge(eps_kept, t + 1)
                nc.scalar.activation(rstd[:, t:t + 1], ms[:, t:t + 1], ACT.Sqrt).then_inc(rooted, 1)
            for n in range(0, 2 * NT, 2):
                act.wait_ge(h_turned, n + 1)
                nc.scalar.copy(h2T[:, 0:4, (n // 2) * P:(n // 2 + 1) * P],
                               ps[:, n, :].rearrange("p (c t) -> p c t", c=4)).then_inc(hT_kept[0], 1)
            with act.Fori(0, 8) as i:
                for s in range(2):
                    act.wait_ge(q_out, 2 * i + s + 3)
                    act.wait_ge(s_out, 2 * i + s + 1)
                    nc.scalar.copy(q_sb[:, s, :], ps[:, s, :]).then_inc(q_kept, 1)

        @block.vector
        def _(dve):
            v = nc.vector
            dve.sem_inc(s_kept, 2)
            dve.sem_inc(top.sem, 1)
            dve.wait_ge(x_in, 16)
            dve.wait_ge(g_in, 16)
            for t in range(NT):
                x = K.x1[:, t, :]
                dve.wait_ge(y_out, 2 * t + 2)
                v.tensor_tensor(x, ps[:, 2 * t:2 * t + 2, :].rearrange("p a b -> p (a b)"), x,
                                ALU.add).then_inc(x_added, 1)
                dve.wait_ge(x_added, t + 1)
                if t:
                    dve.wait_ge(sq_kept, t)
                v.tensor_tensor_reduce(out=junk, in0=x, in1=x, scale=1.0, scalar=0.0, op0=ALU.mult,
                                       op1=ALU.add, accum_out=ms[:, t:t + 1]).then_inc(sq_kept, 1)
                dve.wait_ge(sq_kept, t + 1)
                v.tensor_scalar(ms[:, t:t + 1], ms[:, t:t + 1], 1.0 / D, EPS, ALU.mult,
                                ALU.add).then_inc(eps_kept, 1)
                dve.wait_ge(rooted, t + 1)
                v.reciprocal(rstd[:, t:t + 1], rstd[:, t:t + 1]).then_inc(inverted, 1)
                dve.wait_ge(inverted, t + 1)
                v.scalar_tensor_tensor(out=K.h2[:, t, :], in0=x, scalar=rstd[:, t:t + 1], in1=g_row,
                                       op0=ALU.mult, op1=ALU.mult).then_inc(h_kept, 1)
            for n in range(1, 2 * NT, 2):
                dve.wait_ge(h_turned, n + 1)
                v.tensor_copy(h2T[:, 4:8, (n // 2) * P:(n // 2 + 1) * P],
                              ps[:, n, :].rearrange("p (c t) -> p c t", c=4)).then_inc(hT_kept[1], 1)
            with dve.Fori(0, 8) as i:
                for s in range(2):
                    n = i * 2 + s
                    top.k = 0
                    dve.wait_ge(s_out, n + 3)
                    top.await_last_run(dve, n)
                    v.tensor_copy(sc[:, s, :, :].rearrange("p a b -> p (a b)"), ps[:, 2 + s, :]).then_inc(s_kept, 1)
                    dve.wait_ge(s_kept, n + 3)
                    dve.sem_inc(waited, 1)
                    for t in range(NT):
                        top.done(v.max(val[:, s, t, 0:8], sc[:, s, t, :]), f"max{t}")
                    for t in range(NT):
                        top.await_(dve, f"max{t}", n)
                        dve.sem_inc(waited, 1)
                        top.done(v.max_index(idx[:, s, t, 0:8], val[:, s, t, 0:8], sc[:, s, t, :]), f"idx{t}")
                    for t in range(NT):
                        top.done(v.match_replace(sc2[:, s, t, :], val[:, s, t, 0:8], sc[:, s, t, :],
                                                 -3.0e38), f"cut{t}")
                    for t in range(NT):
                        top.await_(dve, f"cut{t}", n)
                        dve.sem_inc(waited, 1)
                        top.done(v.max(val[:, s, t, 8:16], sc2[:, s, t, :]), f"max2{t}")
                    for t in range(NT):
                        top.await_(dve, f"max2{t}", n)
                        dve.sem_inc(waited, 1)
                        top.done(v.max_index(idx[:, s, t, 8:16], val[:, s, t, 8:16], sc2[:, s, t, :]), f"idx2{t}")
                    top.await_(dve, "idx23", n)
                    top.done(v.tensor_copy(key_val[:, :, n, :], val[:, s, :, :]), "val")
                    top.done(v.tensor_copy(key_idx[:, :, n, :], idx[:, s, :, :]), "index")


def experts(nc, K):
    ps, sem = K.ps, K.sem
    mem = Space(K.sb, K.LOW, K.TOP)
    u = mem.take(16, D)
    w = mem.take(16, D)
    h_now = mem.take(D)
    g_row = mem.take(D)
    cand, cand2, hit_a, hit_b = (mem.take(16, 16) for _ in range(4))
    best, z, z2, ex, gate, wt = (mem.take(2, 16) for _ in range(6))
    pos = mem.take(16).bitcast(U32)
    pos_a = mem.take(16).bitcast(U32)
    pos_b = mem.take(16).bitcast(U32)
    i_a, i_b = mem.take(16), mem.take(16)
    idx = mem.take(2, 16).bitcast(U32)
    nbest, ex_sum = mem.take(2, 1), mem.take(2, 1)
    diag = mem.take(4, P)
    flat = lambda a: a.rearrange("p a b -> p (a b)")
    key_val, key_idx = flat(K.key_val), flat(K.key_idx)
    N = NT * NH
    ms, rstd = K.stat[:, 0, 0:NT], K.stat[:, 1, 0:NT]

    u_in = [sem(f"u_in{k}") for k in range(16)]
    v_in = [sem(f"v_in{k}") for k in range(16)]
    g_in, h_staged = sem("g_fin_in"), sem("h_staged")
    u_used, v_used, diag_set, idx_set = sem("u_used"), sem("v_used"), sem("diag_set"), sem("idx_set")
    best_neg, exp_kept, tanh_kept, y_kept = sem("best_negated"), sem("exp_kept"), sem("tanh_kept"), sem("y_kept")
    final = sem("final_step")
    waited = sem("waited2")
    rooted, out_done = sem("rooted3"), sem("out_done")
    R = Steps(sem("route_step"), ["cand", "best", "pos", "cut", "best2", "pos2", "row", "col", "hit_a",
                                  "val_a", "i_a", "hit_b", "val_b", "i_b"])
    G = Steps(sem("gelu_step"), ["sq", "poly", "arg", "sum_inv", "gate", "half", "wt"])

    with nc.Block() as block:
        @block.sync
        def _(sp):
            sp.dma_start(g_row, K.g_fin.to_broadcast([P, D])).then_inc(g_in, 16)
            for t in range(NT):
                sp.wait_ge(final, 3 * NT + t + 1)
                sp.dma_start(K.out[:, t, :], K.x1[:, t, :]).then_inc(out_done, 16)
            sp.wait_ge(out_done, 16 * NT)

        @block.gpsimd
        def _(pool):
            with pool.Fori(0, N // 2) as i:
                for par in range(2):
                    n = i * 2 + par
                    pool.wait_ge(idx_set, n + 1)
                    for k in range(16):
                        pool.wait_ge(u_used, n * 16 + k + 1)
                        pool.sem_inc(waited, 1)
                        pool.indirect_dma_start(
                            u[:, k, :], None, K.peer_u,
                            bass.IndirectOffsetOnAxis(ap=idx[:, par, k:k + 1], axis=0)).then_inc(u_in[k], 16)
                    for k in range(16):
                        pool.wait_ge(v_used, n * 16 + k + 1)
                        pool.sem_inc(waited, 1)
                        pool.indirect_dma_start(
                            w[:, k, :], None, K.peer_v,
                            bass.IndirectOffsetOnAxis(ap=idx[:, par, k:k + 1], axis=0)).then_inc(v_in[k], 16)

        @block.tensor
        def _(pe):
            pe.sem_inc(v_used, 16)
            with pe.Fori(0, N // 2) as i:
                for par in range(2):
                    n = i * 2 + par
                    pe.wait_ge(y_kept, n + 1)
                    for k in range(16):
                        pe.wait_ge(diag_set, n * 16 + k + 1)
                        pe.wait_ge(v_in[k], n * 16 + 16)
                        for half in range(2):
                            mm = pe.matmul(ps[:, 2 * par + half, :], diag[:, k % 4, :],
                                           w[:, k, half * 512:(half + 1) * 512],
                                           start=(k == 0), stop=(k == 15))
                        mm.then_inc(v_used, 1)

        @block.scalar
        def _(act):
            def exps(n, par):
                act.wait_ge(best_neg, n + 1)
                nc.scalar.activation(ex[:, par, :], best[:, par, :], ACT.Exp, bias=nbest[:, par, :],
                                     accum_out=ex_sum[:, par, :]).then_inc(exp_kept, 1)

            exps(0, 0)
            with act.Fori(0, N // 2) as i:
                for par in range(2):
                    n = i * 2 + par
                    exps(n + 1, 1 - par)
                    G.await_(act, "arg", n)
                    nc.scalar.activation(z2[:, par, :], z2[:, par, :], ACT.Tanh, scale=GELU_B).then_inc(tanh_kept, 1)
                    G.await_(act, "wt", n)
                    for k in range(16):
                        act.wait_ge(v_used, n * 16 + k + 13)
                        nc.scalar.activation(diag[:, k % 4, :], K.ident, ACT.Copy,
                                             scale=wt[:, par, k:k + 1]).then_inc(diag_set, 1)
            act.wait_ge(final, 2 * NT)
            nc.scalar.activation(rstd, ms, ACT.Sqrt).then_inc(rooted, 1)

        @block.vector
        def _(dve):
            v = nc.vector
            dve.sem_inc(u_used, 16)
            dve.sem_inc(R.sem, 1)
            dve.sem_inc(G.sem, 1)

            def route(n, par):
                R.k = 0
                b = best[:, par, :]
                at = n * 32

                def w_(name):
                    R.await_(dve, name, n)

                R.await_last_run(dve, n)
                R.done(v.tensor_tensor(cand, spread(key_val[:, bass.ds(at, 16)], 16),
                                       over(key_val[:, bass.ds(at + 16, 16)], 16), ALU.add), "cand")
                w_("cand")
                dve.sem_inc(waited, 1)
                R.done(v.max(b[:, 0:8], flat(cand)), "best")
                w_("best")
                dve.sem_inc(waited, 1)
                R.done(v.max_index(pos[:, 0:8], b[:, 0:8], flat(cand)), "pos")
                R.done(v.match_replace(flat(cand2), b[:, 0:8], flat(cand), -3.0e38), "cut")
                w_("cut")
                dve.sem_inc(waited, 1)
                R.done(v.max(b[:, 8:16], flat(cand2)), "best2")
                w_("best2")
                dve.sem_inc(waited, 1)
                R.done(v.max_index(pos[:, 8:16], b[:, 8:16], flat(cand2)), "pos2")
                w_("pos2")
                R.done(v.tensor_scalar(pos_a, pos, 4, None, ALU.logical_shift_right), "row")
                R.done(v.tensor_scalar(pos_b, pos, 15, None, ALU.bitwise_and), "col")
                for s, hit, p_, i_, off in (("a", hit_a, pos_a, i_a, 0), ("b", hit_b, pos_b, i_b, 16)):
                    w_("row" if s == "a" else "col")
                    R.done(v.tensor_tensor(hit, spread(p_, 16), over(K.iota16, 16), ALU.is_equal), "hit_" + s)
                    w_("hit_" + s)
                    R.done(v.tensor_tensor(hit, hit, over(key_idx[:, bass.ds(at + off, 16)], 16), ALU.mult), "val_" + s)
                    w_("val_" + s)
                    R.done(v.tensor_reduce(i_, hit, AX, ALU.add), "i_" + s)
                v.tensor_scalar(nbest[:, par, :], b[:, 0:1], -1.0, None, ALU.mult).then_inc(best_neg, 1)

            def number(n, par, first=False):
                R.await_(dve, "i_b", n)
                if not first:
                    dve.wait_ge(v_used, n * 16)
                v.scalar_tensor_tensor(out=idx[:, par, :], in0=i_a, scalar=128.0, in1=i_b, op0=ALU.mult,
                                       op1=ALU.add).then_inc(idx_set, 1)

            def dots(n, par):
                G.k = 0
                for k in range(16):
                    dve.wait_ge(u_in[k], n * 16 + 16)
                    v.tensor_tensor_reduce(out=u[:, k, :], in0=u[:, k, :], in1=h_now, scale=1.0, scalar=0.0,
                                           op0=ALU.mult, op1=ALU.add,
                                           accum_out=z[:, par, k:k + 1]).then_inc(u_used, 1)
                dve.wait_ge(u_used, n * 16 + 32)
                zz, z_ = z2[:, par, :], z[:, par, :]
                G.done(v.tensor_tensor(zz, z_, z_, ALU.mult), "sq")
                G.await_(dve, "sq", n)
                G.done(v.tensor_scalar(zz, zz, GELU_A, 1.0, ALU.mult, ALU.add), "poly")
                G.await_(dve, "poly", n)
                G.done(v.tensor_tensor(zz, zz, z_, ALU.mult), "arg")
                dve.wait_ge(exp_kept, n + 1)
                G.done(v.reciprocal(ex_sum[:, par, :], ex_sum[:, par, :]), "sum_inv")
                G.await_(dve, "sum_inv", n)
                G.done(v.tensor_scalar(gate[:, par, :], ex[:, par, :], ex_sum[:, par, :], 0.5, ALU.mult, ALU.mult), "gate")
                dve.wait_ge(tanh_kept, n + 1)
                G.done(v.scalar_tensor_tensor(out=zz, in0=zz, scalar=1.0, in1=z_, op0=ALU.add, op1=ALU.mult), "half")
                G.await_(dve, "half", n)
                G.done(v.tensor_tensor(wt[:, par, :], zz, gate[:, par, :], ALU.mult), "wt")

            tiles = K.sb[:, K.TOP:K.NW]

            def add_up(n, par, tile):
                dve.wait_ge(v_used, n * 16 + 32)
                dve.wait_ge(y_kept, n + 2)
                x = tiles[:, bass.ds(tile * D, D)]
                v.tensor_tensor(x, flat(ps[:, 2 * par:2 * par + 2, :]), x, ALU.add).then_inc(y_kept, 1)

            v.memset(K.x1_pad[:, 0, :], 0.0).then_inc(h_staged, 1)
            v.memset(ps[:, 2:4, :], 0.0).then_inc(y_kept, 1)
            dve.wait_ge(h_staged, 1)
            route(0, 0)
            number(0, 0, first=True)
            dve.wait_ge(idx_set, 1)
            route(1, 1)
            with dve.Fori(0, N // 2) as i:
                n = i * 2
                dve.wait_ge(u_used, n * 16 + 16)
                v.tensor_copy(h_now, tiles[:, bass.ds((i >> 2) * D + (1 + NT) * D, D)]).then_inc(h_staged, 1)
                dve.wait_ge(h_staged, i + 2)
                dots(n, 0)
                number(n + 1, 1)
                add_up(n - 1, 1, (n + 7) >> 3)
                dve.wait_ge(idx_set, n + 2)
                route(n + 2, 0)
                dots(n + 1, 1)
                number(n + 2, 0)
                add_up(n, 0, (n + 8) >> 3)
                dve.wait_ge(idx_set, n + 3)
                route(n + 3, 1)
            add_up(N - 1, 1, NT)
            dve.wait_ge(y_kept, N + 2)
            dve.wait_ge(g_in, 16)
            for t in range(NT):
                x = K.x1[:, t, :]
                v.tensor_tensor_reduce(out=u[:, t, :], in0=x, in1=x, scale=1.0, scalar=0.0, op0=ALU.mult,
                                       op1=ALU.add, accum_out=ms[:, t:t + 1]).then_inc(final, 1)
            dve.wait_ge(final, NT)
            for t in range(NT):
                v.tensor_scalar(ms[:, t:t + 1], ms[:, t:t + 1], 1.0 / D, EPS, ALU.mult, ALU.add).then_inc(final, 1)
            dve.wait_ge(rooted, 1)
            for t in range(NT):
                v.reciprocal(rstd[:, t:t + 1], rstd[:, t:t + 1]).then_inc(final, 1)
            for t in range(NT):
                dve.wait_ge(final, 3 * NT)
                v.scalar_tensor_tensor(out=K.x1[:, t, :], in0=K.x1[:, t, :], scalar=rstd[:, t:t + 1], in1=g_row,
                                       op0=ALU.mult, op1=ALU.mult).then_inc(final, 1)


def block_kernel(nc, x, vecs, w_ch, w_tok, pe_k, pe_v, w1_k, w1_v, w2_k, w2_v, lora_w, lora_a,
                 lora_g, w_out, g_ffn, wq_sk, peer_u, peer_v, g_fin, out):
    with ExitStack() as ctx:
        def sem(name):
            return ctx.enter_context(nc.semaphore(name))

        K = Shared()
        K.sem = sem
        K.x, K.vecs, K.w_ch, K.w_tok = x, vecs, w_ch, w_tok
        K.pe_k, K.pe_v, K.w1_k, K.w1_v, K.w2_k, K.w2_v = pe_k, pe_v, w1_k, w1_v, w2_k, w2_v
        K.lora_w, K.lora_a, K.lora_g = lora_w, lora_a, lora_g
        K.w_out, K.g_ffn, K.wq_sk = w_out, g_ffn, wq_sk
        K.peer_u, K.peer_v, K.g_fin, K.out = peer_u, peer_v, g_fin, out
        K.NW = 52900
        K.sb = sb = ctx.enter_context(nc.sbuf_tensor("sb", [P, K.NW], F32))
        K.ps = ctx.enter_context(nc.psum_tensor("ps", [P, 8, 512], F32))

        keep = Space(sb, 0, K.NW)
        K.ident = keep.take(P)
        K.iota16 = keep.take(16)
        K.stat = keep.take(4, 8)
        K.LOW = keep.at
        K.head_sum = keep.take(P)
        K.m_d = keep.take(P)
        K.m_dt = keep.take(P)
        K.m_off = [keep.take(P) for _ in range(3)]
        K.m_after = keep.take(P)
        K.m_from = keep.take(P)
        K.ones = keep.take(P)
        K.slopes = keep.take(NH)
        K.vec = keep.take(NVEC)
        K.ndist = keep.take(T)
        K.ndcmp = keep.take(NT, 32)
        K.lw = keep.take(T)
        K.lg = keep.take(T)
        K.yT = keep.take(8, T)
        K.prw = keep.take(NRW, TP)
        K.F0 = keep.at
        both = sb[:, K.F0 - NRW * TP:K.F0 + CR * TP].rearrange("p (c t) -> p c t", t=TP)

        def chunk(n):
            return both[:, n, 1:TP]
        K.chunk = chunk

        K.TOP = K.NW - 10240 - D - 128
        top = Space(sb, K.TOP, K.NW)
        K.x1_pad = top.take(1 + NT, D)
        K.x1 = K.x1_pad[:, 1:, :]
        K.h2 = top.take(NT, D)
        K.key_val = top.take(NT * 16 + 4, 16)
        K.key_idx = top.take(NT * 16 + 4, 16)

        project(nc, K)
        attend(nc, K)
        recur(nc, K)
        mix(nc, K)
        experts(nc, K)


_F32 = "float32"


def layouts(i):
    import numpy as np

    def cols(w, n):
        return np.ascontiguousarray(w.reshape(DC, P, n, P).transpose(2, 1, 0, 3)).reshape(n, P, DC * P)

    def chan(v):
        return v.reshape(-1, P).T

    w = i["w_in"][0]
    kv = 512
    main = np.concatenate([w[:, 1304:3096], w[:, 0:512], w[:, kv:kv + 128], w[:, kv + 128:kv + 256],
                           w[:, kv + 256:kv + 384], w[:, kv + 512:kv + 640]], axis=1)
    tok = np.concatenate([w[:, kv + 384:kv + 512], w[:, kv + 640:kv + 768], w[:, 1280:1304]], axis=1)
    wq = cols(i["peer_w_q"][0], 16)
    sk = i["peer_sub_keys"][0].reshape(16, P, P).transpose(0, 2, 1)
    return {
        "x": np.ascontiguousarray(i["x"][0].reshape(NT, P, D).transpose(1, 0, 2)),
        "vecs": np.ascontiguousarray(np.concatenate(
            [chan(i["norm_mix_g"][0]), chan(i["rwkv_mu"][0])]
            + [chan(i[n][0].reshape(-1)) for n in ("rwkv_w0", "rwkv_a0", "rwkv_k_k", "rwkv_k_a",
                                                   "rwkv_r_k", "rwkv_ln_w", "rwkv_ln_b")], axis=1)),
        "w_ch": cols(main, NCH),
        "w_tok": np.ascontiguousarray(tok.reshape(DC, P, NTOK).transpose(1, 0, 2)).reshape(P, DC * NTOK),
        "pe_k": np.ascontiguousarray(i["cmp_k_pe"][0].T),
        "pe_v": np.ascontiguousarray(i["cmp_v_pe"][0].T),
        "w1_k": i["cmp_k_w1"][0], "w1_v": i["cmp_v_w1"][0],
        "w2_k": i["cmp_k_w2"][0], "w2_v": i["cmp_v_w2"][0],
        "lora_w": i["rwkv_w2"][0], "lora_a": i["rwkv_a2"][0], "lora_g": i["rwkv_g2"][0],
        "w_out": np.ascontiguousarray(i["w_out"][0].reshape(8, P, D).transpose(1, 0, 2)).reshape(P, 8 * D),
        "g_ffn": i["norm_ffn_g"][0].reshape(1, D),
        "wq_sk": np.ascontiguousarray(np.concatenate([wq, sk], axis=2)),
        "peer_u": i["peer_u"][0], "peer_v": i["peer_v"][0],
        "g_fin": i["norm_final_g"].reshape(1, D),
    }


def kernel(**inputs):
    import numpy as np
    import concourse.bacc as bacc
    from concourse.bass_utils import run_bass_kernel_spmd as run

    nc = bacc.Bacc("TRN2", target_bir_lowering=False, num_devices=1)
    arrays, args = {}, []
    for name, a in layouts({k: np.asarray(v) for k, v in inputs.items()}).items():
        arrays[f"in_{name}"] = a
        args.append(nc.dram_tensor(f"in_{name}", a.shape, mybir.dt.from_np(a.dtype), kind="ExternalInput").ap())
    args.append(nc.dram_tensor("out_x", (P, NT, D), F32, kind="ExternalOutput").ap())
    block_kernel(nc, *args)
    r = run(nc, [arrays], core_ids=[0])
    y = np.asarray(r.results[0]["out_x"])
    return np.ascontiguousarray(y.transpose(1, 0, 2)).reshape(1, T, D)
```

```python
from contextlib import ExitStack

import concourse.bass as bass
from concourse import mybir

ALU = mybir.AluOpType
ACT = mybir.ActivationFunctionType
F32 = mybir.dt.float32
U32 = mybir.dt.uint32
AX = mybir.AxisListType.X

P = 128
T = 512
NT = T // P
D = 1024
DC = D // P
HD = 64
NH = 8
EPS = 1e-6
GN_EPS = 64e-5
GELU_A = 0.044715
GELU_B = 0.7978845608028654

NRW = 14
CQ, CKC, CVC, CKS, CKW, CR = 0, 4, 5, 6, 7, 8
NCH = CR + NRW
VS, VW, GL, NTOK = 0, 128, 256, 280
TP = T + 1
RING = 4

V_GMIX, V_MU, V_W0, V_A0, V_KK, V_KA, V_RK, V_LW, V_LB, NVEC = 0, 8, 22, 26, 30, 34, 38, 42, 46, 50

CMP_L, CMP_STRIDE, CMP_N = 32, 16, 31
MASKED = -1e34
FLOOR = -1e29


class Shared:
    pass


class Space:

    def __init__(self, whole, at, end):
        self.whole, self.at, self.end = whole, at, end

    def take(self, *shape):
        n = 1
        for s in shape:
            n *= s
        assert self.at + n <= self.end, (self.at, n, self.end)
        v = self.whole[:, self.at:self.at + n]
        self.at += n
        if len(shape) == 2:
            v = v.rearrange("p (a b) -> p a b", b=shape[1])
        elif len(shape) == 3:
            v = v.rearrange("p (a b c) -> p a b c", b=shape[1], c=shape[2])
        elif len(shape) == 4:
            v = v.rearrange("p (a b c d) -> p a b c d", b=shape[1], c=shape[2], d=shape[3])
        return v


def spread(v, n):
    return v.unsqueeze(2).to_broadcast([v.shape[0], v.shape[1], n])


def over(v, n):
    return v.unsqueeze(1).to_broadcast([v.shape[0], n, v.shape[1]])


class Steps:

    def __init__(self, sem, names):
        self.sem, self.names, self.k = sem, list(names), 0
        self.place = {n: j + 1 for j, n in enumerate(self.names)}
        assert len(self.place) == len(self.names)

    def done(self, ins, name):
        assert self.names[self.k] == name, (self.names[self.k], name)
        self.k += 1
        ins.then_inc(self.sem, 1)

    def await_(self, eng, name, i=0):
        eng.wait_ge(self.sem, i * len(self.names) + self.place[name] + 1)

    def await_last_run(self, eng, i):
        eng.wait_ge(self.sem, i * len(self.names) + 1)


def project(nc, K):
    sb, ps, sem = K.sb, K.ps, K.sem
    mem = Space(sb, K.F0, K.NW)
    K.attn = mem.take(CR, TP)
    K.tok = mem.take(NT, NTOK)
    K.F1 = mem.at
    xt = mem.take(NT, D)
    hT = mem.take(DC, T)
    ring = mem.take(2, DC, P)
    wtok = mem.take(DC, NTOK)
    junk = mem.take(D)
    ms = K.stat[:, 0, 0:NT]
    rstd = K.stat[:, 1, 0:NT]
    x_in = [sem(f"x_in{t}") for t in range(NT)]
    small_in, wtok_in = sem("small_in"), sem("wtok_in")
    w_in = [sem("w_in0"), sem("w_in1")]
    const_set = sem("const_set")
    squares, eps_added, rooted, inverted = sem("squares"), sem("eps_added"), sem("rooted"), sem("inverted")
    h_scaled, h_turned, hT_kept = sem("h_scaled"), sem("h_turned"), sem("hT_kept")
    chunk_out = [sem("chunk_out0"), sem("chunk_out1")]
    chunk_kept = [sem("chunk_kept0"), sem("chunk_kept1")]
    tok_out, tok_kept, gate_tanh = sem("tok_out"), sem("tok_kept"), sem("gate_tanh")
    K.small_in, K.const_set = small_in, const_set

    with nc.Block() as block:
        @block.sync
        def _(sp):
            for t in range(NT):
                sp.dma_start(xt[:, t, :], K.x[:, t, :]).then_inc(x_in[t], 16)
            sp.dma_start(K.vec, K.vecs).then_inc(small_in, 16)
            with sp.Fori(0, NCH // 2) as i:
                for s in range(2):
                    sp.wait_ge(chunk_out[s], i + 1)
                    sp.dma_start(ring[:, s, :, :].rearrange("p c n -> p (c n)"),
                                 K.w_ch[2 * i + s]).then_inc(w_in[s], 16)
            sp.dma_start(wtok.rearrange("p c n -> p (c n)"), K.w_tok).then_inc(wtok_in, 16)
            sp.dma_start(K.lw[0:64, :], K.lora_w).then_inc(small_in, 16)
            sp.dma_start(K.lw[64:128, :], K.lora_a).then_inc(small_in, 16)
            sp.dma_start(K.lg, K.lora_g).then_inc(small_in, 16)
            sp.wait_ge(small_in, 64)

        @block.gpsimd
        def _(pool):
            n = [0]

            def step(ins):
                n[0] += 1
                ins.then_inc(const_set, 1)
                pool.wait_ge(const_set, n[0])

            def cut(v, pattern, base, cm, fill=0.0, op=ALU.is_ge):
                step(nc.gpsimd.affine_select(out=v, in_=v, compare_op=op, fill=fill, base=base,
                                             pattern=pattern, channel_multiplier=cm))

            step(nc.gpsimd.memset(K.ident, 0.0))
            cut(K.ident, [[-1, P]], 0, 1, fill=1.0, op=ALU.not_equal)
            K.n_ident = n[0]
            step(nc.gpsimd.memset(K.ones, 1.0))
            step(nc.gpsimd.memset(K.head_sum, 1.0))
            v = K.head_sum.rearrange("p (a b) -> p a b", b=HD)
            cut(v, [[-HD, 2], [0, HD]], 0, 1)
            cut(v, [[HD, 2], [0, HD]], HD - 1, -1)
            step(nc.gpsimd.memset(K.m_d, 1.0))
            v = K.m_d.rearrange("p (a b) -> p a b", b=16)
            cut(v, [[-16, 8], [-1, 16]], -1, 1)
            cut(v, [[16, 8], [0, 16]], 15, -1)
            step(nc.gpsimd.memset(K.m_dt, 1.0))
            v = K.m_dt.rearrange("p (a b) -> p a b", b=16)
            cut(v, [[16, 8], [1, 16]], -1, -1)
            cut(v, [[-16, 8], [0, 16]], 0, 1)
            for k, b in enumerate((16, 32, 64)):
                step(nc.gpsimd.memset(K.m_off[k], 0.0))
                v = K.m_off[k].rearrange("p (a h b) -> p a h b", h=2, b=b)[:, :, 1, :]
                step(nc.gpsimd.memset(v, 1.0))
                nb = P // (2 * b)
                cut(v, [[-2 * b, nb], [0, b]], 0, 1)
                cut(v, [[2 * b, nb], [0, b]], b - 1, -1)
            step(nc.gpsimd.memset(K.m_after, 1.0))
            cut(K.m_after, [[1, P]], -1, -1)
            step(nc.gpsimd.memset(K.m_from, 1.0))
            cut(K.m_from, [[1, P]], 0, -1)
            for h in range(NH):
                step(nc.gpsimd.memset(K.slopes[:, h:h + 1], 2.0 ** (-8.0 * (h + 1) / NH)))
            step(nc.gpsimd.iota(K.iota16, pattern=[[1, 16]], base=0, channel_multiplier=0,
                                allow_small_or_imprecise_dtypes=True))
            step(nc.gpsimd.iota(K.ndist, pattern=[[1, T]], base=-(T - P), channel_multiplier=-1,
                                allow_small_or_imprecise_dtypes=True))
            cut(K.ndist, [[-1, T]], T - P, 1, fill=MASKED)
            step(nc.gpsimd.iota(K.ndcmp, pattern=[[-P, NT], [CMP_STRIDE, 32]], base=CMP_L - 1,
                                channel_multiplier=-1, allow_small_or_imprecise_dtypes=True))
            cut(K.ndcmp, [[P, NT], [-CMP_STRIDE, 32]], -(CMP_L - 1), 1, fill=MASKED)
            step(nc.gpsimd.memset(K.prw[:, :, 0:1], 0.0))
            step(nc.gpsimd.memset(K.attn[:, :, 0:1], 0.0))

        @block.vector
        def _(dve):
            dve.sem_inc(chunk_kept[1], 1)
            for t in range(NT):
                dve.wait_ge(x_in[t], 16)
                if t:
                    dve.wait_ge(squares, t)
                nc.vector.tensor_tensor_reduce(out=junk, in0=xt[:, t, :], in1=xt[:, t, :], scale=1.0,
                                               scalar=0.0, op0=ALU.mult, op1=ALU.add,
                                               accum_out=ms[:, t:t + 1]).then_inc(squares, 1)
            dve.wait_ge(squares, NT)
            nc.vector.tensor_scalar(ms, ms, 1.0 / D, EPS, ALU.mult, ALU.add).then_inc(eps_added, 1)
            dve.wait_ge(rooted, 1)
            nc.vector.reciprocal(rstd, rstd).then_inc(inverted, 1)
            dve.wait_ge(inverted, 1)
            for t in range(NT):
                nc.vector.tensor_scalar(xt[:, t, :], xt[:, t, :], rstd[:, t:t + 1], None,
                                        ALU.mult).then_inc(h_scaled, 1)
            dve.wait_ge(small_in, 16)
            for n in range(8):
                t, c0 = n // 2, 4 * (n % 2)
                dve.wait_ge(h_turned, n + 1)
                nc.vector.tensor_tensor(hT[:, c0:c0 + 4, t * P:(t + 1) * P],
                                        ps[:, n % 4, :].rearrange("p (c t) -> p c t", c=4),
                                        spread(K.vec[:, V_GMIX + c0:V_GMIX + c0 + 4], P),
                                        ALU.mult).then_inc(hT_kept, 1)

            with dve.Fori(0, NCH // 2) as i:
                dve.wait_ge(chunk_out[1], i + 2)
                nc.vector.tensor_copy(K.chunk(2 * i + 1), ps[:, 1, :]).then_inc(chunk_kept[1], 1)
            for t in range(NT):
                dve.wait_ge(tok_out, t + 1)
                nc.vector.tensor_copy(K.tok[:, t, :], ps[:, 4 + t, 0:NTOK]).then_inc(tok_kept, 1)
            dve.wait_ge(gate_tanh, 1)
            g = K.tok[:, :, GL:NTOK]
            nc.vector.tensor_scalar(g, g, 0.5, 0.5, ALU.mult, ALU.add).then_inc(tok_kept, 1)

        @block.scalar
        def _(act):
            act.sem_inc(chunk_kept[0], 1)
            act.wait_ge(eps_added, 1)
            nc.scalar.activation(rstd, ms, ACT.Sqrt).then_inc(rooted, 1)
            with act.Fori(0, NCH // 2) as i:
                act.wait_ge(chunk_out[0], i + 2)
                nc.scalar.copy(K.chunk(2 * i), ps[:, 0, :]).then_inc(chunk_kept[0], 1)
            act.wait_ge(tok_kept, NT)
            g = K.tok[:, :, GL:NTOK]
            nc.scalar.activation(g, g, ACT.Tanh, scale=0.5).then_inc(gate_tanh, 1)

        @block.tensor
        def _(pe):
            for s in range(2):
                pe.sem_inc(chunk_out[s], 1)
            pe.wait_ge(const_set, K.n_ident)
            for n in range(8):
                t, c0 = n // 2, 4 * (n % 2)
                pe.wait_ge(h_scaled, t + 1)
                if n >= 4:
                    pe.wait_ge(hT_kept, n - 3)
                for c in range(4):
                    mm = pe.transpose(ps[:, n % 4, c * P:(c + 1) * P],
                                      xt[:, t, (c0 + c) * P:(c0 + c + 1) * P], K.ident)
                mm.then_inc(h_turned, 1)
            pe.wait_ge(hT_kept, 8)
            with pe.Fori(0, NCH // 2) as i:
                for s in range(2):
                    pe.wait_ge(w_in[s], 16 * i + 16)
                    pe.wait_ge(chunk_kept[s], i + 1)
                    for c in range(DC):
                        mm = pe.matmul(ps[:, s, :], ring[:, s, c, :], hT[:, c, :],
                                       start=(c == 0), stop=(c == DC - 1))
                    mm.then_inc(chunk_out[s], 1)
            pe.wait_ge(wtok_in, 16)
            for t in range(NT):
                for c in range(DC):
                    mm = pe.matmul(ps[:, 4 + t, 0:NTOK], hT[:, c, t * P:(t + 1) * P], wtok[:, c, :],
                                   start=(c == 0), stop=(c == DC - 1))
                mm.then_inc(tok_out, 1)

def attend(nc, K):
    ps, sem = K.ps, K.sem
    mem = Space(K.sb, K.F1, K.NW)
    w1 = mem.take(2, CMP_L, P)
    win = mem.take(2, CMP_L, 32)
    pe_t = mem.take(2, CMP_L)
    w2k = mem.take(2, HD)
    w2v = mem.take(HD)
    hid = mem.take(4, 32)
    hid2 = mem.take(4, 32)
    hid3 = mem.take(4, 32)
    kcmp = mem.take(2, 32)
    vcmp = mem.take(2, HD)
    kdup = mem.take(2, 2, T)
    k_g = mem.take(2, T)
    kc_g = mem.take(32)
    v_g = mem.take(2, NT, HD)
    vc_g = mem.take(HD)
    q_p = mem.take(T)
    gate_p = mem.take(NT, 6)
    slope_p = mem.take(2)
    BUF = 4
    score = mem.take(BUF, T)
    prob = mem.take(BUF, T)
    probT = mem.take(2, T)
    top_s, nmax, total, inv, coef = (mem.take(BUF, 1) for _ in range(5))
    y = mem.take(NT, 2, HD)

    w1_in, pe_in, w2_in, kdup_in = sem("w1_in"), sem("pe_in"), sem("w2_in"), sem("kdup_in")
    win_set, hid_out, gelu_dve, gelu_act = sem("win_set"), sem("hid_out"), sem("gelu_dve"), sem("gelu_act")
    cmp_out, cmp_kept = sem("cmp_out"), sem("cmp_kept")
    group_set, pair_set, q_set = sem("group_set"), sem("pair_set"), sem("q_set")
    score_out, score_kept, max_kept, nmax_kept = (sem(n) for n in ("score_out", "score_kept", "max_kept", "nmax_kept"))
    prob_kept, turned, turned_kept, pv_out, pv_kept = (
        sem(n) for n in ("prob_kept", "prob_turned", "probT_kept", "pv_out", "pv_kept"))
    sum_floored, sum_inverted, coef_kept = sem("sum_floored"), sem("sum_inverted"), sem("coef_kept")
    y_out, yT_kept = sem("y_turned"), sem("yT_kept")

    TASKS = [(hp, t, br) for hp in range(2) for t in range(NT) for br in range(3)]
    N = len(TASKS)

    def width(t, br):
        return 32 if br == 0 else (t + 1) * P

    def after(eng, s, m):
        eng.wait_ge(s, m + 1 + BUF)

    with nc.Block() as block:
        @block.sync
        def _(sp):
            sp.dma_start(pe_t[0:64, 0, :], K.pe_k).then_inc(pe_in, 16)
            sp.dma_start(pe_t[64:128, 0, :], K.pe_k).then_inc(pe_in, 16)
            sp.dma_start(pe_t[0:64, 1, :], K.pe_v).then_inc(pe_in, 16)
            sp.dma_start(pe_t[64:128, 1, :], K.pe_v).then_inc(pe_in, 16)
            for kv, w in enumerate((K.w1_k, K.w1_v)):
                for g in range(2):
                    sp.dma_start(w1[g * HD:(g + 1) * HD, kv, :, :],
                                 w.rearrange("(l d) n -> d l n", d=HD)).then_inc(w1_in, 16)
            for r in range(2):
                sp.dma_start(w2k[:, r, :], K.w2_k).then_inc(w2_in, 16)
            sp.dma_start(w2v, K.w2_v).then_inc(w2_in, 16)
            for b, c in enumerate((CKS, CKW)):
                for g in range(2):
                    for half in range(2):
                        sp.dma_start(kdup[half * HD:(half + 1) * HD, b, g, :],
                                     K.attn[g * HD:(g + 1) * HD, c, 1:TP]).then_inc(kdup_in, 16)
            sp.wait_ge(kdup_in, 16 * 8)

        @block.gpsimd
        def _(pool):
            pool.wait_ge(kdup_in, 16 * 8)
            pool.wait_ge(cmp_kept, 2)
            with pool.Fori(0, 2) as g:
                after(pool, pv_out, g * 2 * N - 1)
                nc.gpsimd.tensor_copy(k_g, kdup[:, :, g, :]).then_inc(group_set, 1)
                nc.gpsimd.tensor_copy(kc_g, kcmp[:, g, :]).then_inc(group_set, 1)
                for b, c in enumerate((VS, VW)):
                    nc.gpsimd.tensor_copy(v_g[:, b, :, :], K.tok[:, :, bass.ds(c + g * HD, HD)]).then_inc(group_set, 1)
                nc.gpsimd.tensor_copy(vc_g[0:32, :], vcmp[0:32, g, :]).then_inc(group_set, 1)

        @block.tensor
        def _(pe):
            for s in (score_out, turned, pv_out):
                pe.sem_inc(s, BUF)
            pe.sem_inc(y_out, 1)
            pe.wait_ge(w1_in, 64)
            for kv in range(2):
                pe.wait_ge(win_set, 1 + 2 * (kv + 1))
                for g in range(2):
                    half = slice(g * HD, (g + 1) * HD)
                    for l in range(CMP_L):
                        mm = pe.matmul(ps[:, 2 * kv + g, 0:32], w1[half, kv, l, :],
                                       win[half, kv, l, :], start=(l == 0), stop=(l == CMP_L - 1))
            mm.then_inc(hid_out, 1)
            pe.wait_ge(gelu_dve, 5)
            pe.wait_ge(w2_in, 48)
            pe.matmul(ps[:, 4, 0:64], w2k.rearrange("p a b -> p (a b)"),
                      hid2[:, 0:2, :].rearrange("p a b -> p (a b)"), start=True, stop=True).then_inc(cmp_out, 1)
            for g in range(2):
                mm = pe.matmul(ps[0:32, 5, g * HD:(g + 1) * HD], hid2[:, 2 + g, :], w2v,
                               start=True, stop=True)
            mm.then_inc(cmp_out, 1)

            with pe.Fori(0, 2) as g, pe.Fori(0, 2) as r:
                p = g * 2 + r
                done = p * N

                def scores(n):
                    hp, t, br = TASKS[n]
                    half = slice(hp * HD, (hp + 1) * HD)
                    if n == 0:
                        pe.wait_ge(q_set, p + 1)
                        pe.wait_ge(group_set, g * 5 + 5)
                    after(pe, score_kept, done + n - 2)
                    keys = kc_g[half, :] if br == 0 else k_g[half, br - 1, 0:width(t, br)]
                    pe.matmul(ps[:, n % 2, 0:width(t, br)], q_p[half, t * P:(t + 1) * P], keys,
                              start=True, stop=True).then_inc(score_out, 1)

                def turn(n):
                    _, t, br = TASKS[n]
                    after(pe, prob_kept, done + n)
                    after(pe, turned_kept, done + n - 2)
                    if br == 0:
                        mm = pe.transpose(ps[0:32, 2 + n % 2, 0:P], prob[:, n % BUF, 0:32], K.ident)
                    else:
                        for k in range(t + 1):
                            mm = pe.transpose(ps[:, 2 + n % 2, k * P:(k + 1) * P],
                                              prob[:, n % BUF, k * P:(k + 1) * P], K.ident)
                    mm.then_inc(turned, 1)

                def values(n):
                    _, t, br = TASKS[n]
                    after(pe, turned_kept, done + n)
                    after(pe, pv_kept, done + n - 2)
                    if br == 0:
                        mm = pe.matmul(ps[:, 4 + n % 2, 0:HD], probT[0:32, n % 2, 0:P], vc_g[0:32, :],
                                       start=True, stop=True)
                    else:
                        for k in range(t + 1):
                            mm = pe.matmul(ps[:, 4 + n % 2, 0:HD], probT[:, n % 2, k * P:(k + 1) * P],
                                           v_g[:, br - 1, k, :], start=(k == 0), stop=(k == t))
                    mm.then_inc(pv_out, 1)

                for n in range(3):
                    scores(n)
                turn(0)
                for n in range(N):
                    if n + 3 < N:
                        scores(n + 3)
                    if n + 1 < N:
                        turn(n + 1)
                    values(n)
                after(pe, pv_kept, done + N - 1)
                pe.wait_ge(yT_kept, p + 1)
                for t in range(NT):
                    mm = pe.transpose(ps[:, 6, t * P:(t + 1) * P], y[:, t, :, :].rearrange("p a b -> p (a b)"),
                                      K.ident)
                mm.then_inc(y_out, 1)

        @block.vector
        def _(dve):
            for s in (score_kept, max_kept, nmax_kept, sum_floored, sum_inverted, coef_kept, pv_kept):
                dve.sem_inc(s, BUF)
            dve.sem_inc(yT_kept, 1)
            nc.vector.memset(win.rearrange("p a b c -> p (a b c)"), 0.0).then_inc(win_set, 1)
            dve.wait_ge(win_set, 1)
            dve.wait_ge(pe_in, 64)
            for kv, c in enumerate((CKC, CVC)):
                for lh in range(2):
                    src = K.attn[:, c, 1 + 16 * lh:1 + 16 * lh + 16 * CMP_N].rearrange(
                        "p (n l) -> p l n", l=16)
                    nc.vector.tensor_tensor(win[:, kv, 16 * lh:16 * lh + 16, 0:CMP_N], src,
                                            spread(pe_t[:, kv, 16 * lh:16 * lh + 16], CMP_N),
                                            ALU.add).then_inc(win_set, 1)
            dve.wait_ge(hid_out, 1)
            nc.vector.tensor_copy(hid, ps[:, 0:4, 0:32]).then_inc(gelu_dve, 1)
            dve.wait_ge(gelu_dve, 1)
            nc.vector.tensor_tensor(hid2, hid, hid, ALU.mult).then_inc(gelu_dve, 1)
            dve.wait_ge(gelu_dve, 2)
            nc.vector.tensor_scalar(hid2, hid2, GELU_A, 1.0, ALU.mult, ALU.add).then_inc(gelu_dve, 1)
            dve.wait_ge(gelu_dve, 3)
            nc.vector.tensor_tensor(hid3, hid2, hid, ALU.mult).then_inc(gelu_dve, 1)
            dve.wait_ge(gelu_act, 2)
            nc.vector.scalar_tensor_tensor(out=hid2.rearrange("p a b -> p (a b)"),
                                           in0=hid3.rearrange("p a b -> p (a b)"), scalar=1.0,
                                           in1=hid.rearrange("p a b -> p (a b)"),
                                           op0=ALU.add, op1=ALU.mult).then_inc(gelu_dve, 1)
            dve.wait_ge(cmp_out, 2)
            nc.vector.tensor_copy(kcmp.rearrange("p a b -> p (a b)"), ps[:, 4, 0:64]).then_inc(cmp_kept, 1)
            nc.vector.tensor_copy(vcmp[0:32, :, :].rearrange("p a b -> p (a b)"),
                                  ps[0:32, 5, 0:2 * HD]).then_inc(cmp_kept, 1)

            with dve.Fori(0, 4) as p:
                done = p * N

                def bias(n):
                    hp, t, br = TASKS[n]
                    w = width(t, br)
                    dist = K.ndcmp[:, t, :] if br == 0 else K.ndist[:, T - w:T]
                    after(dve, score_out, done + n)
                    after(dve, prob_kept, done + n - BUF)
                    nc.vector.scalar_tensor_tensor(out=score[:, n % BUF, 0:w], in0=dist,
                                                   scalar=slope_p[:, hp:hp + 1], in1=ps[:, n % 2, 0:w],
                                                   op0=ALU.mult, op1=ALU.add).then_inc(score_kept, 1)

                def greatest(n):
                    _, t, br = TASKS[n]
                    after(dve, score_kept, done + n)
                    nc.vector.tensor_reduce(top_s[:, n % BUF, :], score[:, n % BUF, 0:width(t, br)], AX,
                                            ALU.max).then_inc(max_kept, 1)

                def minus_greatest(n):
                    after(dve, max_kept, done + n)
                    nc.vector.tensor_scalar(nmax[:, n % BUF, :], top_s[:, n % BUF, :], FLOOR, -1.0,
                                            ALU.max, ALU.mult).then_inc(nmax_kept, 1)

                def floor_sum(n):
                    after(dve, prob_kept, done + n)
                    nc.vector.tensor_scalar(total[:, n % BUF, :], total[:, n % BUF, :], 1e-30, None,
                                            ALU.max).then_inc(sum_floored, 1)

                def invert_sum(n):
                    after(dve, sum_floored, done + n)
                    nc.vector.reciprocal(inv[:, n % BUF, :], total[:, n % BUF, :]).then_inc(sum_inverted, 1)

                def gate_over_sum(n):
                    hp, t, br = TASKS[n]
                    k = 3 * hp + br
                    after(dve, sum_inverted, done + n)
                    nc.vector.tensor_tensor(coef[:, n % BUF, :], inv[:, n % BUF, :], gate_p[:, t, k:k + 1],
                                            ALU.mult).then_inc(coef_kept, 1)

                def add_branch(n):
                    hp, t, br = TASKS[n]
                    after(dve, coef_kept, done + n)
                    after(dve, pv_out, done + n)
                    out, c = y[:, t, hp, :], coef[:, n % BUF, :]
                    o = ps[:, 4 + n % 2, 0:HD]
                    if br == 0:
                        if n == 0:
                            dve.wait_ge(y_out, p + 1)
                        ins = nc.vector.tensor_scalar(out, o, c, None, ALU.mult)
                    else:
                        after(dve, pv_kept, done + n - 1)
                        ins = nc.vector.scalar_tensor_tensor(out=out, in0=o, scalar=c, in1=out,
                                                             op0=ALU.mult, op1=ALU.add)
                    ins.then_inc(pv_kept, 1)

                after(dve, score_out, done - 1)
                nc.vector.tensor_scalar(q_p, K.attn[:, CQ + p, 1:TP], HD ** -0.5, None,
                                        ALU.mult).then_inc(q_set, 1)
                nc.vector.tensor_copy(gate_p, K.tok[:, :, bass.ds(GL + p * 6, 6)]).then_inc(pair_set, 1)
                nc.vector.tensor_copy(slope_p, K.slopes[:, bass.ds(p * 2, 2)]).then_inc(pair_set, 1)
                dve.wait_ge(pair_set, 2 * p + 2)
                for n in range(3):
                    bias(n)
                    greatest(n)
                    minus_greatest(n)
                for n in range(N):
                    ahead = n + 3 < N
                    if ahead:
                        bias(n + 3)
                    floor_sum(n)
                    if ahead:
                        greatest(n + 3)
                    invert_sum(n)
                    if ahead:
                        minus_greatest(n + 3)
                    gate_over_sum(n)
                    add_branch(n)
                dve.wait_ge(y_out, p + 2)
                nc.vector.tensor_copy(K.yT[:, p, :], ps[:, 6, :]).then_inc(yT_kept, 1)

        @block.scalar
        def _(act):
            act.wait_ge(gelu_dve, 4)
            nc.scalar.activation(hid3, hid3, ACT.Tanh, scale=GELU_B).then_inc(gelu_act, 1)
            act.wait_ge(gelu_act, 1)
            nc.scalar.mul(hid, hid, 0.5).then_inc(gelu_act, 1)
            for s in (prob_kept, turned_kept):
                act.sem_inc(s, BUF)
            with act.Fori(0, 4) as p:
                done = p * N

                def exps(n):
                    _, t, br = TASKS[n]
                    w = width(t, br)
                    after(act, nmax_kept, done + n)
                    after(act, turned, done + n - BUF)
                    after(act, coef_kept, done + n - BUF)
                    b = n % BUF
                    nc.scalar.activation(prob[:, b, 0:w], score[:, b, 0:w], ACT.Exp, bias=nmax[:, b, :],
                                         accum_out=total[:, b, :]).then_inc(prob_kept, 1)

                def keep_turned(n):
                    _, t, br = TASKS[n]
                    after(act, turned, done + n)
                    after(act, pv_out, done + n - 2)
                    rows, w = (32, P) if br == 0 else (P, width(t, br))
                    nc.scalar.copy(probT[0:rows, n % 2, 0:w], ps[0:rows, 2 + n % 2, 0:w]).then_inc(turned_kept, 1)

                for n in range(3):
                    exps(n)
                for n in range(N):
                    keep_turned(n)
                    if n + 3 < N:
                        exps(n + 3)

DECAY = 0.6065306597126334


def recur(nc, K):
    ps, sem = K.ps, K.sem
    mem = Space(K.sb, K.F0, K.NW)
    K.w_out_sb = mem.take(8, D)
    diff = mem.take(NRW, P)
    m = mem.take(NRW, P)
    xw = mem.take(P)
    sg = mem.take(P)
    c4 = lambda: mem.take(4, P)
    ld, lam, a, gg, kk, gr, gi, gp = (c4() for _ in range(8))
    rT, kT, bT, aT, bonus, o, sq = (c4() for _ in range(7))
    b_tok, k_tok, v_tok = (c4() for _ in range(3))
    em, em_exp = mem.take(4), mem.take(4)
    S = mem.take(4, HD)
    Sh = mem.take(4, HD)
    rhs = [mem.take(4, HD) for _ in range(2)]
    SA = [mem.take(4, HD) for _ in range(2)]
    G2 = lambda: [mem.take(4, P) for _ in range(2)]
    Dm, DTm, AkT, RbT, RkT, Tm, TT, X2, X2T, X4, X4T, Y = (G2() for _ in range(12))
    A_T = [diff[:, 4 * g:4 * g + 4, :] for g in range(2)]
    X8T = X2T
    off = [[mem.take(4, P) for _ in range(3)] for _ in range(2)]
    r, k, v = m[:, 0:4, :], m[:, 4:8, :], m[:, 8:12, :]
    vec = lambda at, n=4: spread(K.vec[:, at:at + n], P)
    flat = lambda z: z.rearrange("p a b -> p (a b)")
    bank = lambda b: ps[:, b, :].rearrange("p (a b) -> p a b", b=P)

    wout_in = sem("wout_in")
    K.wout_in = wout_in
    GR = range(2)
    LV = range(3)
    D_ = Steps(sem("recur_dve_step"),
               ["diff", "mixed_in", "m", "sg", "zw", "ld", "za", "a", "kk0", "kk_sq", "norm_floor",
                "norm_inv", "kk", "a1", "k", "scan0", "scan1", "scan2", "scan3", "lam_rel", "lam_prev",
                "rT", "kT", "ba", "bT", "aT", "Sh", "rk", "rk2", "bonus"]
               + [f"{n}{g}" for g in GR for n in ("D", "DT", "T0", "AkT", "RbT", "RkT")]
               + [f"{n}{g}" for n in ("T1", "T2", "T3") for g in GR]
               + [f"{n}_{l}{g}" for l in LV for n in ("T", "TT") for g in GR if (n, l) != ("T", 2)]
               + ["S_add", "S", "oc", "o_sq", "var", "std_inv", "on", "ow", "ob", "o_bonus", "y"])
    A_ = Steps(sem("recur_act_step"),
               ["xw", "sg", "gg", "ld", "a", "norm", "em", "em_exp", "gr", "gi", "gp", "b_tok", "k_tok", "v_tok"]
               + [f"A_T{g}" for g in GR]
               + [f"{n}{g}" for n in ("X2", "X2T", "X4", "X4T", "X8T", "TT") for g in GR]
               + [f"Y{l}{g}" for l in LV for g in GR]
               + [f"rhs{g}" for g in GR] + [f"SA{g}" for g in GR] + ["o", "std"])
    G_ = Steps(sem("recur_pool_step"), [f"off{l}{g}" for g in GR for l in LV])
    P_ = Steps(sem("recur_pe_step"),
               ["zw", "za", "zg", "norm", "bonus", "b_tok", "k_tok", "v_tok"]
               + [f"{n}{g}" for g in GR for n in ("A", "A_T", "AkT", "RbT", "RkT")]
               + [f"{n}{g}" for n in ("X2", "X2T", "T1", "X4", "X4T", "T2", "X8T", "T3", "TT") for g in GR]
               + [f"{n}_{l}{g}" for l in LV for n in ("Y", "T", "TT") for g in GR if (n, l) != ("T", 2)]
               + [f"rhs{g}" for g in GR] + [f"SA{g}" for g in GR] + ["o", "S", "mean", "var"])

    BANK = {"zw": 0, "za": 1, "zg": 2, "norm": 3, "bonus": 4, "b_tok": 5, "k_tok": 6, "v_tok": 7,
            "o": 0, "S": 4, "mean": 1, "var": 5}
    for g in GR:
        for j, n in enumerate(("A", "A_T", "AkT", "RbT", "RkT")):
            BANK[f"{n}{g}"] = 4 * g + j % 4
        for j, n in enumerate(("X2", "X2T", "T1", "X4", "X4T", "T2", "X8T", "T3", "TT")):
            BANK[f"{n}{g}"] = 4 * g + (j + 1) % 4
        for l in LV:
            for j, n in enumerate(("Y", "T", "TT")):
                BANK[f"{n}_{l}{g}"] = 4 * g + (3 * l + j + 2) % 4
        BANK[f"rhs{g}"] = 4 * g + 2
        BANK[f"SA{g}"] = 4 * g + 3
    READ = {"zw": (D_, "zw"), "za": (D_, "za"), "zg": (A_, "gg"), "norm": (A_, "norm"),
            "bonus": (D_, "bonus"), "b_tok": (A_, "b_tok"), "k_tok": (A_, "k_tok"), "v_tok": (A_, "v_tok"),
            "o": (A_, "o"), "S": (D_, "S_add"), "mean": (D_, "oc"), "var": (D_, "var")}
    for g in GR:
        READ[f"A{g}"], READ[f"A_T{g}"] = (D_, f"D{g}"), (D_, f"DT{g}")
        for n in ("AkT", "RbT", "RkT", "T1", "T2", "T3"):
            READ[f"{n}{g}"] = (D_, f"{n}{g}")
        for n in ("X2", "X2T", "X4", "X4T", "X8T", "TT", "rhs", "SA"):
            READ[f"{n}{g}"] = (A_, f"{n}{g}")
        for l in LV:
            READ[f"Y_{l}{g}"] = (A_, f"Y{l}{g}")
            READ[f"T_{l}{g}"], READ[f"TT_{l}{g}"] = (D_, f"T_{l}{g}"), (D_, f"TT_{l}{g}")

    with nc.Block() as block:
        @block.sync
        def _(sp):
            sp.dma_start(flat(K.w_out_sb), K.w_out).then_inc(wout_in, 16)
            sp.wait_ge(wout_in, 16)

        @block.gpsimd
        def _(pool):
            pool.sem_inc(G_.sem, 1)
            with pool.Fori(0, NT) as i:
                G_.k = 0
                for g in GR:
                    for l in LV:
                        if l == 0:
                            A_.await_(pool, f"A_T{g}", i)
                            if g == 0:
                                P_.await_last_run(pool, i)
                        G_.done(nc.gpsimd.tensor_tensor(off[g][l], A_T[g], over(K.m_off[l], 4), ALU.mult),
                                f"off{l}{g}")

        @block.vector
        def _(dve):
            vt = nc.vector
            tt, ts, stt = vt.tensor_tensor, vt.tensor_scalar, vt.scalar_tensor_tensor
            mul, add = ALU.mult, ALU.add
            vt.memset(flat(S), 0.0).then_inc(D_.sem, 1)
            with dve.Fori(0, NT) as i:
                D_.k = 0

                def w(*names):
                    for n in names:
                        D_.await_(dve, n, i)

                def wa(*names):
                    for n in names:
                        A_.await_(dve, n, i)

                def wp(*names):
                    for n in names:
                        P_.await_(dve, n, i)

                A_.await_last_run(dve, i)
                P_.await_last_run(dve, i)
                D_.await_last_run(dve, i)
                now = K.prw[:, :, bass.ds(i * P + 1, P)]
                D_.done(tt(diff, K.prw[:, :, bass.ds(i * P, P)], now, ALU.subtract), "diff")
                w("diff")
                D_.done(tt(diff, diff, vec(V_MU, NRW), mul), "mixed_in")
                w("mixed_in")
                D_.done(tt(m, diff, now, add), "m")
                wa("sg")
                D_.done(ts(sg, sg, 0.5, 0.5, mul, add), "sg")
                wp("zw")
                D_.done(tt(ld, bank(0), vec(V_W0), add), "zw")
                wa("ld")
                D_.done(ts(ld, ld, -DECAY / 2, -DECAY / 2, mul, add), "ld")
                wp("za")
                D_.done(tt(a, bank(1), vec(V_A0), add), "za")
                wa("a")
                D_.done(ts(a, a, 0.5, 0.5, mul, add), "a")
                D_.done(tt(kk, k, vec(V_KK), mul), "kk0")
                w("kk0")
                D_.done(tt(sq, kk, kk, mul), "kk_sq")
                wa("norm")
                D_.done(ts(sq, sq, 1e-12, None, ALU.max), "norm_floor")
                w("norm_floor")
                D_.done(vt.reciprocal(flat(sq), flat(sq)), "norm_inv")
                w("norm_inv")
                D_.done(tt(kk, kk, sq, mul), "kk")
                w("a", "kk")
                D_.done(stt(out=sq, in0=a, scalar=-1.0, in1=vec(V_KA), op0=add, op1=mul), "a1")
                w("a1")
                D_.done(stt(out=k, in0=sq, scalar=1.0, in1=k, op0=add, op1=mul), "k")
                w("ld")
                for c in range(4):
                    D_.done(vt.tensor_tensor_scan(lam[:, c, :], K.ones, ld[:, c, :], 0.0, mul, add), f"scan{c}")
                w("scan3")
                wa("em_exp")
                D_.done(tt(lam, lam, spread(em, P), ALU.subtract), "lam_rel")
                w("lam_rel")
                D_.done(tt(gp, lam, ld, ALU.subtract), "lam_prev")
                wa("gp")
                w("k")
                D_.done(tt(rT, r, gr, mul), "rT")
                D_.done(tt(kT, k, gi, mul), "kT")
                D_.done(tt(bT, kk, a, mul), "ba")
                w("ba")
                D_.done(tt(bT, bT, gi, mul), "bT")
                D_.done(stt(out=aT, in0=kk, scalar=-1.0, in1=gp, op0=mul, op1=mul), "aT")
                D_.done(tt(Sh, S, spread(em_exp, HD), mul), "Sh")
                D_.done(tt(sq, r, k, mul), "rk")
                w("rk")
                D_.done(tt(sq, sq, vec(V_RK), mul), "rk2")
                wp("bonus")
                D_.done(tt(bonus, bank(4), v, mul), "bonus")
                for g in GR:
                    b0 = 4 * g
                    wp(f"A{g}")
                    D_.done(tt(Dm[g], bank(b0), over(K.m_d, 4), mul), f"D{g}")
                    wp(f"A_T{g}")
                    wa(f"A_T{g}")
                    D_.done(tt(DTm[g], bank(b0 + 1), over(K.m_dt, 4), mul), f"DT{g}")
                    w(f"D{g}")
                    D_.done(tt(Tm[g], Dm[g], over(K.ident, 4), add), f"T0{g}")
                    for j, (n, dst, mask) in enumerate((("AkT", AkT, K.m_after), ("RbT", RbT, K.m_from),
                                                        ("RkT", RkT, K.m_from))):
                        wp(f"{n}{g}")
                        D_.done(tt(dst[g], bank(BANK[f"{n}{g}"]), over(mask, 4), mul), f"{n}{g}")
                for n in ("T1", "T2", "T3"):
                    for g in GR:
                        wp(f"{n}{g}")
                        D_.done(tt(Tm[g], bank(BANK[f"{n}{g}"]), Tm[g], add), f"{n}{g}")
                for l in LV:
                    for n, dst in (("T", Tm), ("TT", TT)):
                        for g in GR:
                            if (n, l) == ("T", 2):
                                continue
                            if n == "T":
                                wp(f"T_{l}{g}")
                            else:
                                wp(f"TT_{l}{g}")
                            D_.done(tt(dst[g], bank(BANK[f"{n}_{l}{g}"]), dst[g], add), f"{n}_{l}{g}")
                wp("S")
                D_.done(tt(S, ps[:, 4, 0:4 * HD].rearrange("p (a b) -> p a b", b=HD), Sh, add), "S_add")
                w("S_add")
                D_.done(tt(S, S, gr[:, :, P - 1:P].to_broadcast([P, 4, HD]), mul), "S")
                wp("mean")
                D_.done(stt(out=o, in0=bank(1), scalar=-1.0 / HD, in1=o, op0=mul, op1=add), "oc")
                w("oc")
                D_.done(tt(sq, o, o, mul), "o_sq")
                wp("var")
                D_.done(ts(sq, bank(5), 1.0 / HD, GN_EPS, mul, add), "var")
                wa("std")
                D_.done(vt.reciprocal(flat(sq), flat(sq)), "std_inv")
                w("std_inv")
                D_.done(tt(o, o, sq, mul), "on")
                w("on")
                D_.done(tt(o, o, vec(V_LW), mul), "ow")
                w("ow")
                D_.done(tt(o, o, vec(V_LB), add), "ob")
                w("ob")
                D_.done(tt(o, o, bonus, add), "o_bonus")
                w("o_bonus")
                D_.done(tt(K.yT[:, 4:8, bass.ds(i * P, P)], o, gg, mul), "y")

        @block.scalar
        def _(act):
            f = nc.scalar.activation
            act.sem_inc(A_.sem, 1)
            with act.Fori(0, NT) as i:
                A_.k = 0

                def w(*names):
                    for n in names:
                        D_.await_(act, n, i)

                def wp(*names):
                    for n in names:
                        P_.await_(act, n, i)

                w("m")
                A_.done(f(xw[0:HD, :], m[0:HD, 12, :], ACT.Tanh), "xw")
                A_.done(f(sg, m[:, 13, :], ACT.Tanh, scale=0.5), "sg")
                wp("zg")
                A_.done(nc.scalar.copy(gg, bank(2)), "gg")
                w("zw")
                A_.done(f(ld, ld, ACT.Tanh, scale=0.5), "ld")
                w("za")
                A_.done(f(a, a, ACT.Tanh, scale=0.5), "a")
                wp("norm")
                A_.done(f(sq, bank(3), ACT.Sqrt), "norm")
                w("scan3")
                A_.done(nc.scalar.copy(em, lam[:, :, 63]), "em")
                A_.done(f(em_exp, lam[:, :, 63], ACT.Exp), "em_exp")
                w("lam_rel")
                A_.done(f(gr, lam, ACT.Exp), "gr")
                A_.done(f(gi, lam, ACT.Exp, scale=-1.0), "gi")
                w("lam_prev")
                A_.done(f(gp, gp, ACT.Exp), "gp")
                for n, dst in (("b_tok", b_tok), ("k_tok", k_tok), ("v_tok", v_tok)):
                    wp(n)
                    A_.done(nc.scalar.copy(dst, bank(BANK[n])), n)
                for g in GR:
                    wp(f"A_T{g}")
                    A_.done(nc.scalar.copy(A_T[g], bank(4 * g + 1)), f"A_T{g}")
                for n, dst in (("X2", X2), ("X2T", X2T), ("X4", X4), ("X4T", X4T), ("X8T", X8T), ("TT", TT)):
                    for g in GR:
                        wp(f"{n}{g}")
                        A_.done(nc.scalar.copy(dst[g], bank(BANK[f"{n}{g}"])), f"{n}{g}")
                for l in LV:
                    for g in GR:
                        wp(f"Y_{l}{g}")
                        A_.done(nc.scalar.copy(Y[g], bank(BANK[f"Y_{l}{g}"])), f"Y{l}{g}")
                for n, dst in (("rhs", rhs), ("SA", SA)):
                    for g in GR:
                        wp(f"{n}{g}")
                        A_.done(nc.scalar.copy(flat(dst[g]), ps[:, BANK[f"{n}{g}"], 0:4 * HD]), f"{n}{g}")
                wp("o")
                A_.done(nc.scalar.copy(o, bank(0)), "o")
                w("var")
                A_.done(f(sq, sq, ACT.Sqrt), "std")

        @block.tensor
        def _(pe):
            pe.sem_inc(P_.sem, 1)
            with pe.Fori(0, NT) as i:
                P_.k = 0
                held = {}

                def w(*names):
                    for n in names:
                        D_.await_(pe, n, i)

                def wa(*names):
                    for n in names:
                        A_.await_(pe, n, i)

                def free(name):
                    if BANK[name] in held:
                        steps, n = READ[held[BANK[name]]]
                        steps.await_(pe, n, i)
                    held[BANK[name]] = name

                w("m")
                wa("xw")
                free("zw")
                for c in range(4):
                    mm = pe.matmul(bank(0)[:, c, :], K.lw[0:HD, c * P:(c + 1) * P], xw[0:HD, :],
                                   start=True, stop=True)
                P_.done(mm, "zw")
                free("za")
                for c in range(4):
                    mm = pe.matmul(bank(1)[:, c, :], K.lw[HD:P, c * P:(c + 1) * P], m[HD:P, 12, :],
                                   start=True, stop=True)
                P_.done(mm, "za")
                w("sg")
                free("zg")
                for c in range(4):
                    mm = pe.matmul(bank(2)[:, c, :], K.lg[:, c * P:(c + 1) * P], sg, start=True, stop=True)
                P_.done(mm, "zg")
                w("kk_sq")
                free("norm")
                P_.done(pe.matmul(ps[:, 3, :], K.head_sum, flat(sq), start=True, stop=True), "norm")
                w("rk2")
                free("bonus")
                P_.done(pe.matmul(ps[:, 4, :], K.head_sum, flat(sq), start=True, stop=True), "bonus")
                for n, src in (("b_tok", bT), ("k_tok", kT), ("v_tok", v)):
                    free(n)
                    for c in range(4):
                        mm = pe.transpose(bank(BANK[n])[:, c, :], src[:, c, :], K.ident)
                    P_.done(mm, n)

                def heads(name, g, lhs, rhs_, n=P):
                    free(f"{name}{g}")
                    for c in range(4):
                        mm = pe.matmul(ps[:, BANK[f"{name}{g}"], c * n:(c + 1) * n], lhs[:, c, :],
                                       rhs_[:, c, :], start=True, stop=True)
                    P_.done(mm, f"{name}{g}")

                for g in GR:
                    h = slice(g * HD, (g + 1) * HD)
                    heads("A", g, aT[h], bT[h])
                    heads("A_T", g, bT[h], aT[h])
                    heads("AkT", g, kT[h], aT[h])
                    heads("RbT", g, bT[h], rT[h])
                    heads("RkT", g, kT[h], rT[h])
                for name, lhs, r_, need, needa in (
                        ("X2", DTm, Dm, ("DT",), ()), ("X2T", Dm, DTm, (), ()),
                        ("T1", X2T, Tm, ("T0",), ("X2T",)),
                        ("X4", X2T, X2, (), ("X2",)), ("X4T", X2, X2T, (), ()),
                        ("T2", X4T, Tm, ("T1",), ("X4T",)),
                        ("X8T", X4, X4T, (), ()), ("T3", X8T, Tm, ("T2",), ("X8T",))):
                    for g in GR:
                        w(*(n + str(g) for n in need))
                        wa(*(n + str(g) for n in needa))
                        heads(name, g, lhs[g], r_[g])
                for g in GR:
                    w(f"T3{g}")
                    free(f"TT{g}")
                    for c in range(4):
                        mm = pe.transpose(bank(BANK[f"TT{g}"])[:, c, :], Tm[g][:, c, :], K.ident)
                    P_.done(mm, f"TT{g}")
                for l in LV:
                    for g in GR:
                        G_.await_(pe, f"off{l}{g}", i)
                        if l:
                            w(f"T_{l - 1}{g}")
                        heads(f"Y_{l}", g, off[g][l], Tm[g])
                    if l < 2:
                        for g in GR:
                            wa(f"Y{l}{g}", f"TT{g}")
                            if l:
                                w(f"TT_{l - 1}{g}")
                            heads(f"T_{l}", g, TT[g], Y[g])
                    for g in GR:
                        wa(f"Y{l}{g}", f"TT{g}")
                        if l:
                            w(f"TT_{l - 1}{g}")
                        heads(f"TT_{l}", g, Y[g], TT[g])
                for g in GR:
                    h = slice(g * HD, (g + 1) * HD)
                    free(f"rhs{g}")
                    for c in range(4):
                        dst = ps[:, BANK[f"rhs{g}"], c * HD:(c + 1) * HD]
                        pe.matmul(dst, AkT[g][:, c, :], v_tok[:, c, h], start=True, stop=False)
                        mm = pe.matmul(dst, aT[h, c, :], Sh[h, c, :], start=False, stop=True)
                    P_.done(mm, f"rhs{g}")
                for g in GR:
                    w(f"TT_2{g}")
                    wa(f"rhs{g}")
                    heads("SA", g, TT[g], rhs[g], HD)
                wa("SA1")
                free("o")
                for g in GR:
                    h = slice(g * HD, (g + 1) * HD)
                    for c in range(4):
                        dst = ps[h, 0, c * P:(c + 1) * P]
                        pe.matmul(dst, v_tok[:, c, h], RkT[g][:, c, :], start=True, stop=False)
                        pe.matmul(dst, SA[g][:, c, :], RbT[g][:, c, :], start=False, stop=False)
                        mm = pe.matmul(dst, Sh[h, c, :], rT[h, c, :], start=False, stop=True)
                P_.done(mm, "o")
                free("S")
                for g in GR:
                    h = slice(g * HD, (g + 1) * HD)
                    for c in range(4):
                        dst = ps[h, 4, c * HD:(c + 1) * HD]
                        pe.matmul(dst, b_tok[:, c, h], SA[g][:, c, :], start=True, stop=False)
                        mm = pe.matmul(dst, k_tok[:, c, h], v_tok[:, c, h], start=False, stop=True)
                P_.done(mm, "S")
                wa("o")
                free("mean")
                P_.done(pe.matmul(ps[:, 1, :], K.head_sum, flat(o), start=True, stop=True), "mean")
                w("o_sq")
                free("var")
                P_.done(pe.matmul(ps[:, 5, :], K.head_sum, flat(sq), start=True, stop=True), "var")


def mix(nc, K):
    ps, sem = K.ps, K.sem
    mem = Space(K.sb, K.F0 + 8 * D, K.TOP)
    g_row = mem.take(D)
    junk = mem.take(D)
    ms, rstd = K.stat[:, 0, 0:NT], K.stat[:, 1, 0:NT]
    x_in, g_in = sem("x_again"), sem("g_ffn_in")
    y_out, x_added, sq_kept, eps_kept, rooted, inverted = (
        sem(n) for n in ("mixed_out", "x_added", "sq2_kept", "eps2_kept", "rooted2", "inverted2"))
    h_kept, h_turned = sem("h2_kept"), sem("h2_turned")
    hT_kept = [sem("h2T_kept_act"), sem("h2T_kept_dve")]

    with nc.Block() as block:
        @block.sync
        def _(sp):
            sp.dma_start(K.x1.rearrange("p t d -> p (t d)"), K.x.rearrange("p t d -> p (t d)")).then_inc(x_in, 16)
            sp.dma_start(g_row, K.g_ffn.to_broadcast([P, D])).then_inc(g_in, 16)
            sp.wait_ge(g_in, 16)

        @block.tensor
        def _(pe):
            pe.wait_ge(K.wout_in, 16)
            for n in range(2 * NT):
                t, half = n // 2, n % 2
                for c in range(8):
                    mm = pe.matmul(ps[:, n, :], K.yT[:, c, t * P:(t + 1) * P],
                                   K.w_out_sb[:, c, half * 512:(half + 1) * 512],
                                   start=(c == 0), stop=(c == 7))
                mm.then_inc(y_out, 1)
            for n in range(2 * NT):
                t, c0 = n // 2, 4 * (n % 2)
                pe.wait_ge(h_kept, t + 1)
                for c in range(4):
                    mm = pe.transpose(ps[:, n, c * P:(c + 1) * P], K.h2[:, t, (c0 + c) * P:(c0 + c + 1) * P],
                                      K.ident)
                mm.then_inc(h_turned, 1)
        @block.scalar
        def _(act):
            for t in range(NT):
                act.wait_ge(eps_kept, t + 1)
                nc.scalar.activation(rstd[:, t:t + 1], ms[:, t:t + 1], ACT.Sqrt).then_inc(rooted, 1)
            for n in range(0, 2 * NT, 2):
                act.wait_ge(h_turned, n + 1)
                nc.scalar.copy(K.h2T[:, 0:4, (n // 2) * P:(n // 2 + 1) * P],
                               ps[:, n, :].rearrange("p (c t) -> p c t", c=4)).then_inc(hT_kept[0], 1)
            act.wait_ge(hT_kept[0], NT)

        @block.vector
        def _(dve):
            v = nc.vector
            dve.wait_ge(x_in, 16)
            dve.wait_ge(g_in, 16)
            for t in range(NT):
                x = K.x1[:, t, :]
                dve.wait_ge(y_out, 2 * t + 2)
                v.tensor_tensor(x, ps[:, 2 * t:2 * t + 2, :].rearrange("p a b -> p (a b)"), x,
                                ALU.add).then_inc(x_added, 1)
                dve.wait_ge(x_added, t + 1)
                if t:
                    dve.wait_ge(sq_kept, t)
                v.tensor_tensor_reduce(out=junk, in0=x, in1=x, scale=1.0, scalar=0.0, op0=ALU.mult,
                                       op1=ALU.add, accum_out=ms[:, t:t + 1]).then_inc(sq_kept, 1)
                dve.wait_ge(sq_kept, t + 1)
                v.tensor_scalar(ms[:, t:t + 1], ms[:, t:t + 1], 1.0 / D, EPS, ALU.mult,
                                ALU.add).then_inc(eps_kept, 1)
                dve.wait_ge(rooted, t + 1)
                v.reciprocal(rstd[:, t:t + 1], rstd[:, t:t + 1]).then_inc(inverted, 1)
                dve.wait_ge(inverted, t + 1)
                v.scalar_tensor_tensor(out=K.h2[:, t, :], in0=x, scalar=rstd[:, t:t + 1], in1=g_row,
                                       op0=ALU.mult, op1=ALU.mult).then_inc(h_kept, 1)
            for n in range(1, 2 * NT, 2):
                dve.wait_ge(h_turned, n + 1)
                v.tensor_copy(K.h2T[:, 4:8, (n // 2) * P:(n // 2 + 1) * P],
                              ps[:, n, :].rearrange("p (c t) -> p c t", c=4)).then_inc(hT_kept[1], 1)
            dve.wait_ge(hT_kept[1], NT)


def experts(nc, K):
    ps, sem = K.ps, K.sem
    mem = Space(K.sb, K.LOW, K.TOP)
    u = mem.take(16, D)
    w = mem.take(16, D)
    g_row = mem.take(D)
    cand, cand2, hit_a, hit_b = (mem.take(16, 16) for _ in range(4))
    best, z, z2, ex, gate, wt = (mem.take(2, 16) for _ in range(6))
    pos = mem.take(16).bitcast(U32)
    pos_a = mem.take(16).bitcast(U32)
    pos_b = mem.take(16).bitcast(U32)
    i_a, i_b = mem.take(16), mem.take(16)
    idx = mem.take(2, 16).bitcast(U32)
    nbest, ex_sum = mem.take(2, 1), mem.take(2, 1)
    diag = mem.take(4, P)
    flat = lambda a: a.rearrange("p a b -> p (a b)")
    ring = mem.take(2, DC + 1, P)
    q_sb, sc, sc2 = mem.take(T), mem.take(NT, P), mem.take(NT, P)
    key_val, key_idx = mem.take(2, NT, 16), mem.take(2, NT, 16)
    key_num = mem.take(2, NT, 16).bitcast(U32)
    N = NT * NH
    ms, rstd = K.stat[:, 0, 0:NT], K.stat[:, 1, 0:NT]

    u_in = [sem(f"u_in{k}") for k in range(16)]
    v_in = [sem(f"v_in{k}") for k in range(16)]
    g_in = sem("g_fin_in")
    u_used, v_used, diag_set, idx_set = sem("u_used"), sem("v_used"), sem("diag_set"), sem("idx_set")
    best_neg, exp_kept, tanh_kept, y_kept = sem("best_negated"), sem("exp_kept"), sem("tanh_kept"), sem("y_kept")
    final = sem("final_step")
    waited = sem("waited2")
    rooted, out_done = sem("rooted3"), sem("out_done")
    wq_in = [sem("wq_in0"), sem("wq_in1")]
    q_out, q_kept, s_out, s_kept = sem("query_out"), sem("query_kept"), sem("key_score_out"), sem("key_score_kept")
    top = Steps(sem("top_key_step"), [f"{n}{t}" for n in ("max", "idx", "cut", "max2", "idx2") for t in range(NT)]
                + ["index"])
    R = Steps(sem("route_step"), ["cand", "best", "pos", "cut", "best2", "pos2", "row", "col", "hit_a",
                                  "val_a", "i_a", "hit_b", "val_b", "i_b"])
    G = Steps(sem("gelu_step"), ["sq", "poly", "arg", "sum_inv", "gate", "half", "wt"])

    with nc.Block() as block:
        @block.sync
        def _(sp):
            def load(h):
                for s in range(2):
                    sp.wait_ge(s_out, 2 * h + s + 1)
                    sp.dma_start(ring[:, s, :, :].rearrange("p c n -> p (c n)"),
                                 K.wq_sk[2 * h + s]).then_inc(wq_in[s], 16)

            load(0)
            with sp.Fori(0, NH - 1) as h:
                load(h + 1)
            sp.dma_start(g_row, K.g_fin.to_broadcast([P, D])).then_inc(g_in, 16)
            for t in range(NT):
                sp.wait_ge(final, 3 * NT + t + 1)
                sp.dma_start(K.out[:, t, :], K.x1[:, t, :]).then_inc(out_done, 16)
            sp.wait_ge(out_done, 16 * NT)

        @block.gpsimd
        def _(pool):
            with pool.Fori(0, N // 2) as i:
                for par in range(2):
                    n = 2 * i + par
                    pool.wait_ge(idx_set, n + 1)
                    for k in range(16):
                        pool.wait_ge(u_used, n * 16 + k + 1)
                        pool.sem_inc(waited, 1)
                        pool.indirect_dma_start(
                            u[:, k, :], None, K.peer_u,
                            bass.IndirectOffsetOnAxis(ap=idx[:, par, k:k + 1], axis=0)).then_inc(u_in[k], 16)
                    for k in range(16):
                        pool.wait_ge(v_used, n * 16 + k + 1)
                        pool.sem_inc(waited, 1)
                        pool.indirect_dma_start(
                            w[:, k, :], None, K.peer_v,
                            bass.IndirectOffsetOnAxis(ap=idx[:, par, k:k + 1], axis=0)).then_inc(v_in[k], 16)

        @block.tensor
        def _(pe):
            pe.sem_inc(v_used, 16)
            pe.sem_inc(s_out, 2)

            def queries(h, s):
                m = 2 * h + s
                pe.wait_ge(wq_in[s], 16 * h + 16)
                pe.wait_ge(q_kept, m + 1)
                for c in range(DC):
                    mm = pe.matmul(ps[:, 4 + s, :], ring[:, s, c, :], K.h2T[:, c, :],
                                   start=(c == 0), stop=(c == DC - 1))
                mm.then_inc(q_out, 1)

            def scores(h, s):
                m = 2 * h + s
                pe.wait_ge(q_kept, m + 3)
                pe.wait_ge(s_kept, m + 1)
                for t in range(NT):
                    mm = pe.matmul(ps[:, 6 + s, t * P:(t + 1) * P], q_sb[:, t * P:(t + 1) * P],
                                   ring[:, s, DC, :], start=True, stop=True)
                mm.then_inc(s_out, 1)

            def add_rows(n, par):
                pe.wait_ge(y_kept, n + 1)
                for k in range(16):
                    pe.wait_ge(diag_set, n * 16 + k + 1)
                    pe.wait_ge(v_in[k], n * 16 + 16)
                    for half in range(2):
                        mm = pe.matmul(ps[:, 2 * par + half, :], diag[:, k % 4, :],
                                       w[:, k, half * 512:(half + 1) * 512],
                                       start=(k == 0), stop=(k == 15))
                    mm.then_inc(v_used, 1)

            def head(h, last=False):
                for t in range(NT):
                    if not last and t == 0:
                        queries(h + 1, 0)
                    if not last and t == 1:
                        scores(h + 1, 0)
                        queries(h + 1, 1)
                    if not last and t == 2:
                        scores(h + 1, 1)
                    add_rows(NT * h + t, t % 2)

            for s in range(2):
                queries(0, s)
                scores(0, s)
            with pe.Fori(0, NH - 1) as h:
                head(h)
            head(NH - 1, last=True)

        @block.scalar
        def _(act):
            def exps(n, par):
                act.wait_ge(best_neg, n + 1)
                nc.scalar.activation(ex[:, par, :], best[:, par, :], ACT.Exp, bias=nbest[:, par, :],
                                     accum_out=ex_sum[:, par, :]).then_inc(exp_kept, 1)

            def keep_queries(h, s):
                m = 2 * h + s
                act.wait_ge(q_out, m + 1)
                act.wait_ge(s_out, m + 2)
                nc.scalar.copy(q_sb, ps[:, 4 + s, :]).then_inc(q_kept, 1)

            def head(h, last=False):
                for t in range(NT):
                    n, par = NT * h + t, t % 2
                    if not (last and t == NT - 1):
                        exps(n + 1, 1 - par)
                    G.await_(act, "arg", n)
                    nc.scalar.activation(z2[:, par, :], z2[:, par, :], ACT.Tanh, scale=GELU_B).then_inc(tanh_kept, 1)
                    G.await_(act, "wt", n)
                    for k in range(16):
                        act.wait_ge(v_used, n * 16 + k + 13)
                        nc.scalar.activation(diag[:, k % 4, :], K.ident, ACT.Copy,
                                             scale=wt[:, par, k:k + 1]).then_inc(diag_set, 1)
                    if not last and t < 2:
                        keep_queries(h + 1, t)

            act.sem_inc(q_kept, 2)
            for s in range(2):
                keep_queries(0, s)
            exps(0, 0)
            with act.Fori(0, NH - 1) as h:
                head(h)
            head(NH - 1, last=True)
            act.wait_ge(final, 2 * NT)
            nc.scalar.activation(rstd, ms, ACT.Sqrt).then_inc(rooted, 1)

        @block.vector
        def _(dve):
            v = nc.vector
            dve.sem_inc(u_used, 16)
            dve.sem_inc(R.sem, 1)
            dve.sem_inc(G.sem, 1)
            dve.sem_inc(top.sem, 1)
            dve.sem_inc(s_kept, 2)

            def best_keys(h, s):
                m = 2 * h + s
                top.k = 0
                dve.wait_ge(s_out, m + 3)
                v.tensor_copy(flat(sc), ps[:, 6 + s, :]).then_inc(s_kept, 1)
                dve.wait_ge(s_kept, m + 3)
                dve.sem_inc(waited, 1)
                val, num = key_val[:, s, :, :], key_num[:, s, :, :]
                for t in range(NT):
                    top.done(v.max(val[:, t, 0:8], sc[:, t, :]), f"max{t}")
                for t in range(NT):
                    top.await_(dve, f"max{t}", m)
                    dve.sem_inc(waited, 1)
                    top.done(v.max_index(num[:, t, 0:8], val[:, t, 0:8], sc[:, t, :]), f"idx{t}")
                for t in range(NT):
                    top.done(v.match_replace(sc2[:, t, :], val[:, t, 0:8], sc[:, t, :], -3.0e38), f"cut{t}")
                for t in range(NT):
                    top.await_(dve, f"cut{t}", m)
                    dve.sem_inc(waited, 1)
                    top.done(v.max(val[:, t, 8:16], sc2[:, t, :]), f"max2{t}")
                for t in range(NT):
                    top.await_(dve, f"max2{t}", m)
                    dve.sem_inc(waited, 1)
                    top.done(v.max_index(num[:, t, 8:16], val[:, t, 8:16], sc2[:, t, :]), f"idx2{t}")
                top.await_(dve, f"idx2{NT - 1}", m)
                top.done(v.tensor_copy(key_idx[:, s, :, :], num), "index")

            def route(n, t):
                par = t % 2
                R.k = 0
                b = best[:, par, :]

                def w_(name):
                    R.await_(dve, name, n)

                R.await_last_run(dve, n)
                R.done(v.tensor_tensor(cand, spread(key_val[:, 0, t, :], 16),
                                       over(key_val[:, 1, t, :], 16), ALU.add), "cand")
                w_("cand")
                dve.sem_inc(waited, 1)
                R.done(v.max(b[:, 0:8], flat(cand)), "best")
                w_("best")
                dve.sem_inc(waited, 1)
                R.done(v.max_index(pos[:, 0:8], b[:, 0:8], flat(cand)), "pos")
                R.done(v.match_replace(flat(cand2), b[:, 0:8], flat(cand), -3.0e38), "cut")
                w_("cut")
                dve.sem_inc(waited, 1)
                R.done(v.max(b[:, 8:16], flat(cand2)), "best2")
                w_("best2")
                dve.sem_inc(waited, 1)
                R.done(v.max_index(pos[:, 8:16], b[:, 8:16], flat(cand2)), "pos2")
                w_("pos2")
                R.done(v.tensor_scalar(pos_a, pos, 4, None, ALU.logical_shift_right), "row")
                R.done(v.tensor_scalar(pos_b, pos, 15, None, ALU.bitwise_and), "col")
                for s, hit, p_, i_, side in (("a", hit_a, pos_a, i_a, 0), ("b", hit_b, pos_b, i_b, 1)):
                    w_("row" if s == "a" else "col")
                    R.done(v.tensor_tensor(hit, spread(p_, 16), over(K.iota16, 16), ALU.is_equal), "hit_" + s)
                    w_("hit_" + s)
                    R.done(v.tensor_tensor(hit, hit, over(key_idx[:, side, t, :], 16), ALU.mult), "val_" + s)
                    w_("val_" + s)
                    R.done(v.tensor_reduce(i_, hit, AX, ALU.add), "i_" + s)
                v.tensor_scalar(nbest[:, par, :], b[:, 0:1], -1.0, None, ALU.mult).then_inc(best_neg, 1)

            def number(n, par, first=False):
                R.await_(dve, "i_b", n)
                if not first:
                    dve.wait_ge(v_used, n * 16)
                v.scalar_tensor_tensor(out=idx[:, par, :], in0=i_a, scalar=128.0, in1=i_b, op0=ALU.mult,
                                       op1=ALU.add).then_inc(idx_set, 1)

            def dots(n, t):
                G.k = 0
                par = t % 2
                for k in range(16):
                    dve.wait_ge(u_in[k], n * 16 + 16)
                    v.tensor_tensor_reduce(out=u[:, k, :], in0=u[:, k, :], in1=K.h2[:, t, :], scale=1.0, scalar=0.0,
                                           op0=ALU.mult, op1=ALU.add,
                                           accum_out=z[:, par, k:k + 1]).then_inc(u_used, 1)
                dve.wait_ge(u_used, n * 16 + 32)
                zz, z_ = z2[:, par, :], z[:, par, :]
                G.done(v.tensor_tensor(zz, z_, z_, ALU.mult), "sq")
                G.await_(dve, "sq", n)
                G.done(v.tensor_scalar(zz, zz, GELU_A, 1.0, ALU.mult, ALU.add), "poly")
                G.await_(dve, "poly", n)
                G.done(v.tensor_tensor(zz, zz, z_, ALU.mult), "arg")
                dve.wait_ge(exp_kept, n + 1)
                G.done(v.reciprocal(ex_sum[:, par, :], ex_sum[:, par, :]), "sum_inv")
                G.await_(dve, "sum_inv", n)
                G.done(v.tensor_scalar(gate[:, par, :], ex[:, par, :], ex_sum[:, par, :], 0.5, ALU.mult, ALU.mult), "gate")
                dve.wait_ge(tanh_kept, n + 1)
                G.done(v.scalar_tensor_tensor(out=zz, in0=zz, scalar=1.0, in1=z_, op0=ALU.add, op1=ALU.mult), "half")
                G.await_(dve, "half", n)
                G.done(v.tensor_tensor(wt[:, par, :], zz, gate[:, par, :], ALU.mult), "wt")

            def add_up(n, t):
                par = t % 2
                dve.wait_ge(v_used, n * 16 + 32)
                dve.wait_ge(y_kept, n + 2)
                x = K.x1[:, t, :]
                v.tensor_tensor(x, flat(ps[:, 2 * par:2 * par + 2, :]), x, ALU.add).then_inc(y_kept, 1)

            def head(h, last=False):
                for t in range(NT):
                    n = NT * h + t
                    dots(n, t)
                    if not (last and t == NT - 1):
                        number(n + 1, (t + 1) % 2)
                    add_up(n - 1, (t - 1) % NT)
                    if last and t >= NT - 2:
                        continue
                    dve.wait_ge(idx_set, n + 2)
                    if t == 2:
                        best_keys(h + 1, 1)
                        top.await_(dve, "index", 2 * h + 3)
                        dve.sem_inc(waited, 1)
                    route(n + 2, (t + 2) % NT)
                    if t == 1 and not last:
                        R.await_(dve, "i_b", n + 2)
                        best_keys(h + 1, 0)

            v.memset(ps[:, 2:4, :], 0.0).then_inc(y_kept, 1)
            for s in range(2):
                best_keys(0, s)
            top.await_(dve, "index", 1)
            route(0, 0)
            number(0, 0, first=True)
            dve.wait_ge(idx_set, 1)
            route(1, 1)
            with dve.Fori(0, NH - 1) as h:
                head(h)
            head(NH - 1, last=True)
            add_up(N - 1, NT - 1)
            dve.wait_ge(y_kept, N + 2)
            dve.wait_ge(g_in, 16)
            for t in range(NT):
                x = K.x1[:, t, :]
                v.tensor_tensor_reduce(out=u[:, t, :], in0=x, in1=x, scale=1.0, scalar=0.0, op0=ALU.mult,
                                       op1=ALU.add, accum_out=ms[:, t:t + 1]).then_inc(final, 1)
            dve.wait_ge(final, NT)
            for t in range(NT):
                v.tensor_scalar(ms[:, t:t + 1], ms[:, t:t + 1], 1.0 / D, EPS, ALU.mult, ALU.add).then_inc(final, 1)
            dve.wait_ge(rooted, 1)
            for t in range(NT):
                v.reciprocal(rstd[:, t:t + 1], rstd[:, t:t + 1]).then_inc(final, 1)
            for t in range(NT):
                dve.wait_ge(final, 3 * NT)
                v.scalar_tensor_tensor(out=K.x1[:, t, :], in0=K.x1[:, t, :], scalar=rstd[:, t:t + 1], in1=g_row,
                                       op0=ALU.mult, op1=ALU.mult).then_inc(final, 1)


def block_kernel(nc, x, vecs, w_ch, w_tok, pe_k, pe_v, w1_k, w1_v, w2_k, w2_v, lora_w, lora_a,
                 lora_g, w_out, g_ffn, wq_sk, peer_u, peer_v, g_fin, out):
    with ExitStack() as ctx:
        def sem(name):
            return ctx.enter_context(nc.semaphore(name))

        K = Shared()
        K.sem = sem
        K.x, K.vecs, K.w_ch, K.w_tok = x, vecs, w_ch, w_tok
        K.pe_k, K.pe_v, K.w1_k, K.w1_v, K.w2_k, K.w2_v = pe_k, pe_v, w1_k, w1_v, w2_k, w2_v
        K.lora_w, K.lora_a, K.lora_g = lora_w, lora_a, lora_g
        K.w_out, K.g_ffn, K.wq_sk = w_out, g_ffn, wq_sk
        K.peer_u, K.peer_v, K.g_fin, K.out = peer_u, peer_v, g_fin, out
        K.NW = 52900
        K.sb = sb = ctx.enter_context(nc.sbuf_tensor("sb", [P, K.NW], F32))
        K.ps = ctx.enter_context(nc.psum_tensor("ps", [P, 8, 512], F32))

        keep = Space(sb, 0, K.NW)
        K.ident = keep.take(P)
        K.iota16 = keep.take(16)
        K.stat = keep.take(4, 8)
        K.LOW = keep.at
        K.head_sum = keep.take(P)
        K.m_d = keep.take(P)
        K.m_dt = keep.take(P)
        K.m_off = [keep.take(P) for _ in range(3)]
        K.m_after = keep.take(P)
        K.m_from = keep.take(P)
        K.ones = keep.take(P)
        K.slopes = keep.take(NH)
        K.vec = keep.take(NVEC)
        K.ndist = keep.take(T)
        K.ndcmp = keep.take(NT, 32)
        K.lw = keep.take(T)
        K.lg = keep.take(T)
        K.yT = keep.take(8, T)
        K.prw = keep.take(NRW, TP)
        K.F0 = keep.at
        both = sb[:, K.F0 - NRW * TP:K.F0 + CR * TP].rearrange("p (c t) -> p c t", t=TP)

        def chunk(n):
            return both[:, n, 1:TP]
        K.chunk = chunk

        K.TOP = K.NW - 3 * NT * D
        top = Space(sb, K.TOP, K.NW)
        K.x1 = top.take(NT, D)
        K.h2 = top.take(NT, D)
        K.h2T = top.take(DC, T)

        project(nc, K)
        attend(nc, K)
        recur(nc, K)
        mix(nc, K)
        experts(nc, K)


_F32 = "float32"


def layouts(i):
    import numpy as np

    def cols(w, n):
        return np.ascontiguousarray(w.reshape(DC, P, n, P).transpose(2, 1, 0, 3)).reshape(n, P, DC * P)

    def chan(v):
        return v.reshape(-1, P).T

    w = i["w_in"][0]
    kv = 512
    main = np.concatenate([w[:, 1304:3096], w[:, 0:512], w[:, kv:kv + 128], w[:, kv + 128:kv + 256],
                           w[:, kv + 256:kv + 384], w[:, kv + 512:kv + 640]], axis=1)
    tok = np.concatenate([w[:, kv + 384:kv + 512], w[:, kv + 640:kv + 768], w[:, 1280:1304]], axis=1)
    wq = cols(i["peer_w_q"][0], 16)
    sk = i["peer_sub_keys"][0].reshape(16, P, P).transpose(0, 2, 1)
    return {
        "x": np.ascontiguousarray(i["x"][0].reshape(NT, P, D).transpose(1, 0, 2)),
        "vecs": np.ascontiguousarray(np.concatenate(
            [chan(i["norm_mix_g"][0]), chan(i["rwkv_mu"][0])]
            + [chan(i[n][0].reshape(-1)) for n in ("rwkv_w0", "rwkv_a0", "rwkv_k_k", "rwkv_k_a",
                                                   "rwkv_r_k", "rwkv_ln_w", "rwkv_ln_b")], axis=1)),
        "w_ch": cols(main, NCH),
        "w_tok": np.ascontiguousarray(tok.reshape(DC, P, NTOK).transpose(1, 0, 2)).reshape(P, DC * NTOK),
        "pe_k": np.ascontiguousarray(i["cmp_k_pe"][0].T),
        "pe_v": np.ascontiguousarray(i["cmp_v_pe"][0].T),
        "w1_k": i["cmp_k_w1"][0], "w1_v": i["cmp_v_w1"][0],
        "w2_k": i["cmp_k_w2"][0], "w2_v": i["cmp_v_w2"][0],
        "lora_w": i["rwkv_w2"][0], "lora_a": i["rwkv_a2"][0], "lora_g": i["rwkv_g2"][0],
        "w_out": np.ascontiguousarray(i["w_out"][0].reshape(8, P, D).transpose(1, 0, 2)).reshape(P, 8 * D),
        "g_ffn": i["norm_ffn_g"][0].reshape(1, D),
        "wq_sk": np.ascontiguousarray(np.concatenate([wq, sk], axis=2)),
        "peer_u": i["peer_u"][0], "peer_v": i["peer_v"][0],
        "g_fin": i["norm_final_g"].reshape(1, D),
    }


def kernel(**inputs):
    import numpy as np
    import concourse.bacc as bacc
    from concourse.bass_utils import run_bass_kernel_spmd as run

    nc = bacc.Bacc("TRN2", target_bir_lowering=False, num_devices=1)
    arrays, args = {}, []
    for name, a in layouts({k: np.asarray(v) for k, v in inputs.items()}).items():
        arrays[f"in_{name}"] = a
        args.append(nc.dram_tensor(f"in_{name}", a.shape, mybir.dt.from_np(a.dtype), kind="ExternalInput").ap())
    args.append(nc.dram_tensor("out_x", (P, NT, D), F32, kind="ExternalOutput").ap())
    block_kernel(nc, *args)
    r = run(nc, [arrays], core_ids=[0])
    y = np.asarray(r.results[0]["out_x"])
    return np.ascontiguousarray(y.transpose(1, 0, 2)).reshape(1, T, D)
```

```python
from contextlib import ExitStack

import concourse.bass as bass
from concourse import mybir

ALU = mybir.AluOpType
ACT = mybir.ActivationFunctionType
F32 = mybir.dt.float32
U32 = mybir.dt.uint32
AX = mybir.AxisListType.X

P = 128
T = 512
NT = T // P
D = 1024
DC = D // P
HD = 64
NH = 8
EPS = 1e-6
GN_EPS = 64e-5
GELU_A = 0.044715
GELU_B = 0.7978845608028654

NRW = 14
CQ, CKC, CVC, CKS, CKW, CR = 0, 4, 5, 6, 7, 8
NCH = CR + NRW
VS, VW, GL, NTOK = 0, 128, 256, 280
TP = T + 1

V_GMIX, V_MU, V_W0, V_A0, V_KK, V_KA, V_RK, V_LW, V_LB, NVEC = 0, 8, 22, 26, 30, 34, 38, 42, 46, 50

CMP_L, CMP_STRIDE, CMP_N = 32, 16, 31
MASKED = -1e34
FLOOR = -1e29


class Shared:
    pass


class Space:

    def __init__(self, whole, at, end):
        self.whole, self.at, self.end = whole, at, end

    def take(self, *shape):
        n = 1
        for s in shape:
            n *= s
        assert self.at + n <= self.end, (self.at, n, self.end)
        v = self.whole[:, self.at:self.at + n]
        self.at += n
        if len(shape) == 2:
            v = v.rearrange("p (a b) -> p a b", b=shape[1])
        elif len(shape) == 3:
            v = v.rearrange("p (a b c) -> p a b c", b=shape[1], c=shape[2])
        elif len(shape) == 4:
            v = v.rearrange("p (a b c d) -> p a b c d", b=shape[1], c=shape[2], d=shape[3])
        return v


def spread(v, n):
    return v.unsqueeze(2).to_broadcast([v.shape[0], v.shape[1], n])


def over(v, n):
    return v.unsqueeze(1).to_broadcast([v.shape[0], n, v.shape[1]])


class Steps:

    def __init__(self, sem, names):
        self.sem, self.names, self.k = sem, list(names), 0
        self.place = {n: j + 1 for j, n in enumerate(self.names)}
        assert len(self.place) == len(self.names)

    def done(self, ins, name):
        assert self.names[self.k] == name, (self.names[self.k], name)
        self.k += 1
        ins.then_inc(self.sem, 1)

    def await_(self, eng, name, i=0):
        eng.wait_ge(self.sem, i * len(self.names) + self.place[name] + 1)

    def await_last_run(self, eng, i):
        eng.wait_ge(self.sem, i * len(self.names) + 1)


def project(nc, K):
    sb, ps, sem = K.sb, K.ps, K.sem
    mem = Space(sb, K.F0, K.NW)
    K.attn = mem.take(CR, TP)
    K.tok = mem.take(NT, NTOK)
    K.F1 = mem.at
    K.LATE = K.NW - CMP_L * P - CMP_L - 3 * HD - 8 * T
    late = Space(sb, K.LATE, K.NW)
    mem.end = late.at
    K.w1 = late.take(2, CMP_L // 2, P)
    K.pe_t = late.take(2, CMP_L // 2)
    K.w2k = late.take(2, HD)
    K.w2v = late.take(HD)
    K.src = late.take(2, 2, T)
    K.kdup = late.take(2, 2, T)
    K.w1_in, K.pe_in, K.w2_in = sem("w1_in"), sem("pe_in"), sem("w2_in")
    K.src_in, K.kdup_in = sem("src_in"), sem("kdup_in")
    xt = mem.take(NT, D)
    hT = mem.take(DC, T)
    ring = mem.take(2, DC, P)
    wtok = mem.take(DC, NTOK)
    junk = mem.take(D)
    ms = K.stat[:, 0, 0:NT]
    rstd = K.stat[:, 1, 0:NT]
    x_in = [sem(f"x_in{t}") for t in range(NT)]
    small_in, lora_in, wtok_in = sem("small_in"), sem("lora_in"), sem("wtok_in")
    w_in = [sem("w_in0"), sem("w_in1")]
    const_set = sem("const_set")
    squares, eps_added, rooted, inverted = sem("squares"), sem("eps_added"), sem("rooted"), sem("inverted")
    h_scaled, h_turned, hT_kept = sem("h_scaled"), sem("h_turned"), sem("hT_kept")
    chunk_out = [sem("chunk_out0"), sem("chunk_out1")]
    chunk_kept = [sem("chunk_kept0"), sem("chunk_kept1")]
    tok_out, tok_kept, gate_tanh = sem("tok_out"), sem("tok_kept"), sem("gate_tanh")

    with nc.Block() as block:
        @block.sync
        def _(sp):
            for t in range(NT):
                sp.dma_start(xt[:, t, :], K.x[:, t, :]).then_inc(x_in[t], 16)
            sp.dma_start(K.vec, K.vecs).then_inc(small_in, 16)
            with sp.Fori(0, NCH // 2) as i:
                for s in range(2):
                    sp.wait_ge(chunk_out[s], i + 1)
                    sp.dma_start(ring[:, s, :, :].rearrange("p c n -> p (c n)"),
                                 K.w_ch[2 * i + s]).then_inc(w_in[s], 16)
            for s in range(2):
                sp.wait_ge(chunk_kept[s], 1 + NCH // 2)
            for dst, done, chunks in ((K.src, K.src_in, (CKC, CVC)), (K.kdup, K.kdup_in, (CKS, CKW))):
                for b, c in enumerate(chunks):
                    for g in range(2):
                        for half in range(2):
                            sp.dma_start(dst[half * HD:(half + 1) * HD, b, g, :],
                                         K.attn[g * HD:(g + 1) * HD, c, 1:TP]).then_inc(done, 16)
            sp.wait_ge(small_in, 16)
            sp.wait_ge(lora_in, 48)

        @block.gpsimd
        def _(pool):
            n = [0]

            def step(ins):
                n[0] += 1
                ins.then_inc(const_set, 1)
                pool.wait_ge(const_set, n[0])

            def cut(v, pattern, base, cm, fill=0.0, op=ALU.is_ge):
                step(nc.gpsimd.affine_select(out=v, in_=v, compare_op=op, fill=fill, base=base,
                                             pattern=pattern, channel_multiplier=cm))

            step(nc.gpsimd.memset(K.ident, 0.0))
            cut(K.ident, [[-1, P]], 0, 1, fill=1.0, op=ALU.not_equal)
            K.n_ident = n[0]
            step(nc.gpsimd.memset(K.ones, 1.0))
            step(nc.gpsimd.memset(K.head_sum, 1.0))
            v = K.head_sum.rearrange("p (a b) -> p a b", b=HD)
            cut(v, [[-HD, 2], [0, HD]], 0, 1)
            cut(v, [[HD, 2], [0, HD]], HD - 1, -1)
            step(nc.gpsimd.memset(K.m_d, 1.0))
            v = K.m_d.rearrange("p (a b) -> p a b", b=16)
            cut(v, [[-16, 8], [-1, 16]], -1, 1)
            cut(v, [[16, 8], [0, 16]], 15, -1)
            step(nc.gpsimd.memset(K.m_dt, 1.0))
            v = K.m_dt.rearrange("p (a b) -> p a b", b=16)
            cut(v, [[16, 8], [1, 16]], -1, -1)
            cut(v, [[-16, 8], [0, 16]], 0, 1)
            for k, b in enumerate((16, 32, 64)):
                step(nc.gpsimd.memset(K.m_off[k], 0.0))
                v = K.m_off[k].rearrange("p (a h b) -> p a h b", h=2, b=b)[:, :, 1, :]
                step(nc.gpsimd.memset(v, 1.0))
                nb = P // (2 * b)
                cut(v, [[-2 * b, nb], [0, b]], 0, 1)
                cut(v, [[2 * b, nb], [0, b]], b - 1, -1)
            step(nc.gpsimd.memset(K.m_after, 1.0))
            cut(K.m_after, [[1, P]], -1, -1)
            step(nc.gpsimd.memset(K.m_from, 1.0))
            cut(K.m_from, [[1, P]], 0, -1)
            for h in range(NH):
                step(nc.gpsimd.memset(K.slopes[:, h:h + 1], 2.0 ** (-8.0 * (h + 1) / NH)))
            step(nc.gpsimd.iota(K.iota16, pattern=[[1, 16]], base=0, channel_multiplier=0,
                                allow_small_or_imprecise_dtypes=True))
            step(nc.gpsimd.iota(K.ndist, pattern=[[1, T]], base=-(T - P), channel_multiplier=-1,
                                allow_small_or_imprecise_dtypes=True))
            cut(K.ndist, [[-1, T]], T - P, 1, fill=MASKED)
            step(nc.gpsimd.iota(K.ndcmp, pattern=[[-P, NT], [CMP_STRIDE, 32]], base=CMP_L - 1,
                                channel_multiplier=-1, allow_small_or_imprecise_dtypes=True))
            cut(K.ndcmp, [[P, NT], [-CMP_STRIDE, 32]], -(CMP_L - 1), 1, fill=MASKED)
            step(nc.gpsimd.memset(K.prw[:, :, 0:1], 0.0))
            step(nc.gpsimd.memset(K.attn[:, :, 0:1], 0.0))

        @block.vector
        def _(dve):
            dve.sem_inc(chunk_kept[1], 1)
            for t in range(NT):
                dve.wait_ge(x_in[t], 16)
                if t:
                    dve.wait_ge(squares, t)
                nc.vector.tensor_tensor_reduce(out=junk, in0=xt[:, t, :], in1=xt[:, t, :], scale=1.0,
                                               scalar=0.0, op0=ALU.mult, op1=ALU.add,
                                               accum_out=ms[:, t:t + 1]).then_inc(squares, 1)
                dve.wait_ge(squares, t + 1)
                nc.vector.tensor_scalar(ms[:, t:t + 1], ms[:, t:t + 1], 1.0 / D, EPS, ALU.mult,
                                        ALU.add).then_inc(eps_added, 1)
                dve.wait_ge(rooted, t + 1)
                nc.vector.reciprocal(rstd[:, t:t + 1], rstd[:, t:t + 1]).then_inc(inverted, 1)
            dve.wait_ge(small_in, 16)
            for n in range(8):
                t, c0 = n // 2, 4 * (n % 2)
                dve.wait_ge(h_turned, n + 1)
                nc.vector.tensor_tensor(hT[:, c0:c0 + 4, t * P:(t + 1) * P],
                                        ps[:, n % 4, :].rearrange("p (c t) -> p c t", c=4),
                                        spread(K.vec[:, V_GMIX + c0:V_GMIX + c0 + 4], P),
                                        ALU.mult).then_inc(hT_kept, 1)

            with dve.Fori(0, NCH // 2) as i:
                dve.wait_ge(chunk_out[1], i + 2)
                nc.vector.tensor_copy(K.chunk(2 * i + 1), ps[:, 1, :]).then_inc(chunk_kept[1], 1)
            for t in range(NT):
                dve.wait_ge(tok_out, t + 1)
                nc.vector.tensor_copy(K.tok[:, t, :], ps[:, 4 + t, 0:NTOK]).then_inc(tok_kept, 1)
            dve.wait_ge(gate_tanh, 1)
            g = K.tok[:, :, GL:NTOK]
            nc.vector.tensor_scalar(g, g, 0.5, 0.5, ALU.mult, ALU.add).then_inc(tok_kept, 1)

        @block.scalar
        def _(act):
            act.sem_inc(chunk_kept[0], 1)
            for t in range(NT):
                act.wait_ge(eps_added, t + 1)
                nc.scalar.activation(rstd[:, t:t + 1], ms[:, t:t + 1], ACT.Sqrt).then_inc(rooted, 1)
                act.wait_ge(inverted, t + 1)
                nc.scalar.activation(xt[:, t, :], xt[:, t, :], ACT.Copy,
                                     scale=rstd[:, t:t + 1]).then_inc(h_scaled, 1)
            act.dma_start(wtok.rearrange("p c n -> p (c n)"), K.w_tok).then_inc(wtok_in, 16)
            act.dma_start(K.lw[0:64, :], K.lora_w).then_inc(lora_in, 16)
            act.dma_start(K.lw[64:128, :], K.lora_a).then_inc(lora_in, 16)
            act.dma_start(K.lg, K.lora_g).then_inc(lora_in, 16)
            for kv, (w, pe) in enumerate(((K.w1_k, K.pe_k), (K.w1_v, K.pe_v))):
                act.dma_start(K.pe_t[:, kv, :], pe).then_inc(K.pe_in, 16)
                act.dma_start(K.w1[:, kv, :, :].rearrange("p l n -> p (l n)"), w).then_inc(K.w1_in, 16)
            for r in range(2):
                act.dma_start(K.w2k[:, r, :], K.w2_k).then_inc(K.w2_in, 16)
            act.dma_start(K.w2v, K.w2_v).then_inc(K.w2_in, 16)
            with act.Fori(0, NCH // 2) as i:
                act.wait_ge(chunk_out[0], i + 2)
                nc.scalar.copy(K.chunk(2 * i), ps[:, 0, :]).then_inc(chunk_kept[0], 1)
            act.wait_ge(tok_kept, NT)
            g = K.tok[:, :, GL:NTOK]
            nc.scalar.activation(g, g, ACT.Tanh, scale=0.5).then_inc(gate_tanh, 1)

        @block.tensor
        def _(pe):
            for s in range(2):
                pe.sem_inc(chunk_out[s], 1)
            pe.wait_ge(const_set, K.n_ident)
            for n in range(8):
                t, c0 = n // 2, 4 * (n % 2)
                pe.wait_ge(h_scaled, t + 1)
                if n >= 4:
                    pe.wait_ge(hT_kept, n - 3)
                for c in range(4):
                    mm = pe.transpose(ps[:, n % 4, c * P:(c + 1) * P],
                                      xt[:, t, (c0 + c) * P:(c0 + c + 1) * P], K.ident)
                mm.then_inc(h_turned, 1)
            pe.wait_ge(hT_kept, 8)
            with pe.Fori(0, NCH // 2) as i:
                for s in range(2):
                    pe.wait_ge(w_in[s], 16 * i + 16)
                    pe.wait_ge(chunk_kept[s], i + 1)
                    for c in range(DC):
                        mm = pe.matmul(ps[:, s, :], ring[:, s, c, :], hT[:, c, :],
                                       start=(c == 0), stop=(c == DC - 1))
                    mm.then_inc(chunk_out[s], 1)
            pe.wait_ge(wtok_in, 16)
            for t in range(NT):
                for c in range(DC):
                    mm = pe.matmul(ps[:, 4 + t, 0:NTOK], hT[:, c, t * P:(t + 1) * P], wtok[:, c, :],
                                   start=(c == 0), stop=(c == DC - 1))
                mm.then_inc(tok_out, 1)


def attend(nc, K):
    ps, sem = K.ps, K.sem
    mem = Space(K.sb, K.F1, K.LATE)
    w1, pe_t, w2k, w2v, w1_in, pe_in, w2_in = K.w1, K.pe_t, K.w2k, K.w2v, K.w1_in, K.pe_in, K.w2_in
    win = mem.take(2, CMP_L // 2, 2, 32)
    hid = mem.take(4, 32)
    hid2 = mem.take(4, 32)
    hid3 = mem.take(4, 32)
    kcmp = mem.take(2, 32)
    vcmp = mem.take(2, HD)
    src, kdup, src_in, kdup_in = K.src, K.kdup, K.src_in, K.kdup_in
    k_g = mem.take(2, T)
    kc_g = mem.take(32)
    v_g = mem.take(2, NT, HD)
    vc_g = mem.take(HD)
    q_p = mem.take(T)
    gate_p = mem.take(NT, 6)
    slope_p = mem.take(2)
    BUF = 4
    score = mem.take(BUF, T)
    prob = mem.take(BUF, T)
    probT = mem.take(2, T)
    top_s, nmax, total, inv, coef = (mem.take(BUF, 1) for _ in range(5))

    win_set, hid_out, gelu_dve, gelu_act = sem("win_set"), sem("hid_out"), sem("gelu_dve"), sem("gelu_act")
    cmp_out, cmp_kept = sem("cmp_out"), sem("cmp_kept")
    keys_set, values_set, pair_set, q_set = (sem(n) for n in ("keys_set", "values_set", "pair_set", "q_set"))
    score_out, score_kept, max_kept, nmax_kept = (sem(n) for n in ("score_out", "score_kept", "max_kept", "nmax_kept"))
    prob_kept, prob_scaled, turned, turned_kept, pv_out = (
        sem(n) for n in ("prob_kept", "prob_scaled", "prob_turned", "probT_kept", "pv_out"))
    sum_floored, sum_inverted, coef_kept = sem("sum_floored"), sem("sum_inverted"), sem("coef_kept")
    yT_kept = sem("yT_kept")

    TASKS = [(hp, t, br) for hp in range(2) for t in range(NT) for br in range(3)]
    N = len(TASKS)

    def width(t, br):
        return 32 if br == 0 else (t + 1) * P

    def after(eng, s, m):
        eng.wait_ge(s, m + 1 + BUF)

    with nc.Block() as block:
        @block.gpsimd
        def _(pool):
            pool.wait_ge(cmp_kept, 2)
            with pool.Fori(0, 2) as g:
                after(pool, pv_out, g * 2 * N - 1)
                for b, c in enumerate((VS, VW)):
                    nc.gpsimd.tensor_copy(v_g[:, b, :, :], K.tok[:, :, bass.ds(c + g * HD, HD)]).then_inc(values_set, 1)
                nc.gpsimd.tensor_copy(vc_g[0:32, :], vcmp[0:32, g, :]).then_inc(values_set, 1)

        @block.tensor
        def _(pe):
            for s in (score_out, turned, pv_out):
                pe.sem_inc(s, BUF)
            pe.wait_ge(w1_in, 32)
            for kv in range(2):
                pe.wait_ge(win_set, 1 + 8 * (kv + 1))
                for l in range(CMP_L // 2):
                    mm = pe.matmul(ps[:, kv, 0:64], w1[:, kv, l, :], win[:, kv, l, :, :].rearrange("p g n -> p (g n)"),
                                   start=(l == 0), stop=(l == CMP_L // 2 - 1))
            mm.then_inc(hid_out, 1)
            pe.wait_ge(gelu_dve, 5)
            pe.wait_ge(w2_in, 48)
            pe.matmul(ps[:, 4, 0:64], w2k.rearrange("p a b -> p (a b)"),
                      hid2[:, 0:2, :].rearrange("p a b -> p (a b)"), start=True, stop=True).then_inc(cmp_out, 1)
            for g in range(2):
                mm = pe.matmul(ps[0:32, 5, g * HD:(g + 1) * HD], hid2[:, 2 + g, :], w2v,
                               start=True, stop=True)
            mm.then_inc(cmp_out, 1)

            with pe.Fori(0, 2) as g, pe.Fori(0, 2) as r:
                p = g * 2 + r
                done = p * N

                def scores(n):
                    hp, t, br = TASKS[n]
                    half = slice(hp * HD, (hp + 1) * HD)
                    if n == 0:
                        pe.wait_ge(q_set, p + 1)
                        pe.wait_ge(keys_set, g * 2 + 2)
                    after(pe, score_kept, done + n - 2)
                    keys = kc_g[half, :] if br == 0 else k_g[half, br - 1, 0:width(t, br)]
                    pe.matmul(ps[:, n % 2, 0:width(t, br)], q_p[half, t * P:(t + 1) * P], keys,
                              start=True, stop=True).then_inc(score_out, 1)

                def turn(n):
                    _, t, br = TASKS[n]
                    after(pe, prob_scaled, done + n)
                    after(pe, turned_kept, done + n - 2)
                    if br == 0:
                        mm = pe.transpose(ps[0:32, 2 + n % 2, 0:P], prob[:, n % BUF, 0:32], K.ident)
                    else:
                        for k in range(t + 1):
                            mm = pe.transpose(ps[:, 2 + n % 2, k * P:(k + 1) * P],
                                              prob[:, n % BUF, k * P:(k + 1) * P], K.ident)
                    mm.then_inc(turned, 1)

                def values(n):
                    hp, t, br = TASKS[n]
                    half, tokens = slice(hp * HD, (hp + 1) * HD), slice(t * P, (t + 1) * P)
                    after(pe, turned_kept, done + n)
                    if n == 0:
                        pe.wait_ge(yT_kept, p + 1)
                        pe.wait_ge(values_set, g * 3 + 3)
                    if br == 0:
                        mm = pe.matmul(ps[half, 4, tokens], vc_g[0:32, :], probT[0:32, n % 2, 0:P],
                                       start=True, stop=False)
                    else:
                        for k in range(t + 1):
                            mm = pe.matmul(ps[half, 4, tokens], v_g[:, br - 1, k, :],
                                           probT[:, n % 2, k * P:(k + 1) * P],
                                           start=False, stop=(br == 2 and k == t))
                    mm.then_inc(pv_out, 1)

                for n in range(4):
                    scores(n)
                turn(0)
                for n in range(N):
                    if n + 4 < N:
                        scores(n + 4)
                    if n + 1 < N:
                        turn(n + 1)
                    values(n)

        @block.vector
        def _(dve):
            for s in (score_kept, max_kept, nmax_kept, sum_floored, sum_inverted, coef_kept):
                dve.sem_inc(s, BUF)
            dve.sem_inc(yT_kept, 1)
            nc.vector.memset(win.rearrange("p a b g n -> p (a b g n)"), 0.0).then_inc(win_set, 1)
            dve.wait_ge(win_set, 1)
            dve.wait_ge(pe_in, 32)
            dve.wait_ge(src_in, 16 * 8)
            for kv in range(2):
                for odd in range(2):
                    h = slice(odd * HD, (odd + 1) * HD)
                    for a in range(2):
                        pe_l = spread(pe_t[h, kv, 8 * a:8 * a + 8], CMP_N)
                        for g in range(2):
                            tokens = src[h, kv, g, 16 * a:16 * a + 16 * CMP_N].rearrange(
                                "p (n b o) -> p b o n", b=8, o=2)[:, :, odd, :]
                            nc.vector.tensor_tensor(win[h, kv, 8 * a:8 * a + 8, g, 0:CMP_N], tokens, pe_l,
                                                    ALU.add).then_inc(win_set, 1)
            dve.wait_ge(hid_out, 1)
            nc.vector.tensor_copy(hid.rearrange("p (a b) n -> p a (b n)", a=2), ps[:, 0:2, 0:64]).then_inc(gelu_dve, 1)
            dve.wait_ge(gelu_dve, 1)
            nc.vector.tensor_tensor(hid2, hid, hid, ALU.mult).then_inc(gelu_dve, 1)
            dve.wait_ge(gelu_dve, 2)
            nc.vector.tensor_scalar(hid2, hid2, GELU_A, 1.0, ALU.mult, ALU.add).then_inc(gelu_dve, 1)
            dve.wait_ge(gelu_dve, 3)
            nc.vector.tensor_tensor(hid3, hid2, hid, ALU.mult).then_inc(gelu_dve, 1)
            dve.wait_ge(gelu_act, 2)
            nc.vector.scalar_tensor_tensor(out=hid2.rearrange("p a b -> p (a b)"),
                                           in0=hid3.rearrange("p a b -> p (a b)"), scalar=1.0,
                                           in1=hid.rearrange("p a b -> p (a b)"),
                                           op0=ALU.add, op1=ALU.mult).then_inc(gelu_dve, 1)
            dve.wait_ge(cmp_out, 2)
            nc.vector.tensor_copy(kcmp.rearrange("p a b -> p (a b)"), ps[:, 4, 0:64]).then_inc(cmp_kept, 1)
            nc.vector.tensor_copy(vcmp[0:32, :, :].rearrange("p a b -> p (a b)"),
                                  ps[0:32, 5, 0:2 * HD]).then_inc(cmp_kept, 1)

            dve.wait_ge(kdup_in, 16 * 8)
            dve.wait_ge(cmp_kept, 2)
            with dve.Fori(0, 2) as g:
                after(dve, score_out, g * 2 * N - 1)
                nc.vector.tensor_copy(k_g, kdup[:, :, g, :]).then_inc(keys_set, 1)
                nc.vector.tensor_copy(kc_g, kcmp[:, g, :]).then_inc(keys_set, 1)
                with dve.Fori(0, 2) as r:
                    p = g * 2 + r
                    done = p * N

                    def bias(n):
                        hp, t, br = TASKS[n]
                        w = width(t, br)
                        dist = K.ndcmp[:, t, :] if br == 0 else K.ndist[:, T - w:T]
                        after(dve, score_out, done + n)
                        after(dve, prob_kept, done + n - BUF)
                        nc.vector.scalar_tensor_tensor(out=score[:, n % BUF, 0:w], in0=dist,
                                                       scalar=slope_p[:, hp:hp + 1], in1=ps[:, n % 2, 0:w],
                                                       op0=ALU.mult, op1=ALU.add).then_inc(score_kept, 1)

                    def greatest(n):
                        _, t, br = TASKS[n]
                        after(dve, score_kept, done + n)
                        nc.vector.tensor_reduce(top_s[:, n % BUF, :], score[:, n % BUF, 0:width(t, br)], AX,
                                                ALU.max).then_inc(max_kept, 1)

                    def minus_greatest(n):
                        after(dve, max_kept, done + n)
                        nc.vector.tensor_scalar(nmax[:, n % BUF, :], top_s[:, n % BUF, :], FLOOR, -1.0,
                                                ALU.max, ALU.mult).then_inc(nmax_kept, 1)

                    def floor_sum(n):
                        after(dve, prob_kept, done + n)
                        nc.vector.tensor_scalar(total[:, n % BUF, :], total[:, n % BUF, :], 1e-30, None,
                                                ALU.max).then_inc(sum_floored, 1)

                    def invert_sum(n):
                        after(dve, sum_floored, done + n)
                        nc.vector.reciprocal(inv[:, n % BUF, :], total[:, n % BUF, :]).then_inc(sum_inverted, 1)

                    def gate_over_sum(n):
                        hp, t, br = TASKS[n]
                        k = 3 * hp + br
                        after(dve, sum_inverted, done + n)
                        after(dve, prob_scaled, done + n - BUF)
                        nc.vector.tensor_tensor(coef[:, n % BUF, :], inv[:, n % BUF, :], gate_p[:, t, k:k + 1],
                                                ALU.mult).then_inc(coef_kept, 1)

                    after(dve, score_out, done - 1)
                    nc.vector.tensor_scalar(q_p, K.attn[:, CQ + p, 1:TP], HD ** -0.5, None,
                                            ALU.mult).then_inc(q_set, 1)
                    nc.vector.tensor_copy(gate_p, K.tok[:, :, bass.ds(GL + p * 6, 6)]).then_inc(pair_set, 1)
                    nc.vector.tensor_copy(slope_p, K.slopes[:, bass.ds(p * 2, 2)]).then_inc(pair_set, 1)
                    dve.wait_ge(pair_set, 2 * p + 2)
                    for n in range(4):
                        bias(n)
                        greatest(n)
                        minus_greatest(n)
                    for n in range(2):
                        floor_sum(n)
                        invert_sum(n)
                        gate_over_sum(n)
                    for n in range(N - 2):
                        ahead = n + 4 < N
                        if ahead:
                            bias(n + 4)
                        floor_sum(n + 2)
                        if ahead:
                            greatest(n + 4)
                        invert_sum(n + 2)
                        if ahead:
                            minus_greatest(n + 4)
                        gate_over_sum(n + 2)
                    after(dve, pv_out, done + N - 1)
                    nc.vector.tensor_copy(K.yT[:, p, :], ps[:, 4, :]).then_inc(yT_kept, 1)

        @block.scalar
        def _(act):
            act.wait_ge(gelu_dve, 4)
            nc.scalar.activation(hid3, hid3, ACT.Tanh, scale=GELU_B).then_inc(gelu_act, 1)
            act.wait_ge(gelu_act, 1)
            nc.scalar.mul(hid, hid, 0.5).then_inc(gelu_act, 1)
            for s in (prob_kept, prob_scaled, turned_kept):
                act.sem_inc(s, BUF)
            with act.Fori(0, 4) as p:
                done = p * N

                def exps(n):
                    _, t, br = TASKS[n]
                    w = width(t, br)
                    after(act, nmax_kept, done + n)
                    after(act, turned, done + n - BUF)
                    after(act, coef_kept, done + n - BUF)
                    b = n % BUF
                    nc.scalar.activation(prob[:, b, 0:w], score[:, b, 0:w], ACT.Exp, bias=nmax[:, b, :],
                                         accum_out=total[:, b, :]).then_inc(prob_kept, 1)

                def keep_turned(n):
                    _, t, br = TASKS[n]
                    after(act, turned, done + n)
                    after(act, pv_out, done + n - 2)
                    rows, w = (32, P) if br == 0 else (P, width(t, br))
                    nc.scalar.copy(probT[0:rows, n % 2, 0:w], ps[0:rows, 2 + n % 2, 0:w]).then_inc(turned_kept, 1)

                def scale(n):
                    _, t, br = TASKS[n]
                    after(act, coef_kept, done + n)
                    probs = prob[:, n % BUF, 0:width(t, br)]
                    nc.scalar.activation(probs, probs, ACT.Copy, scale=coef[:, n % BUF, :]).then_inc(prob_scaled, 1)

                for n in range(3):
                    exps(n)
                for n in range(2):
                    scale(n)
                for n in range(N):
                    keep_turned(n)
                    if n + 3 < N:
                        exps(n + 3)
                    if n + 2 < N:
                        scale(n + 2)

DECAY = 0.6065306597126334


def recur(nc, K):
    ps, sem = K.ps, K.sem
    mem = Space(K.sb, K.F0, K.NW)
    K.w_out_sb = mem.take(8, D)
    diff = mem.take(NRW, P)
    m = mem.take(NRW, P)
    xw = mem.take(P)
    sg = mem.take(P)
    c4 = lambda: mem.take(4, P)
    ld, lam, a, gg, kk, gr, gi, gp = (c4() for _ in range(8))
    rT, kT, bT, aT, bonus, o, sq = (c4() for _ in range(7))
    b_tok, k_tok, v_tok = (c4() for _ in range(3))
    em, em_exp, gr_end = mem.take(4), mem.take(4), mem.take(4)
    S = mem.take(4, HD)
    Sh = mem.take(4, HD)
    rhs = [mem.take(4, HD) for _ in range(2)]
    SA = [mem.take(4, HD) for _ in range(2)]
    G2 = lambda: [mem.take(4, P) for _ in range(2)]
    Dm, DTm, AkT, RbT, RkT, Tm, TT, X2, X2T, X4, X4T, Y = (G2() for _ in range(12))
    A_T = [diff[:, 4 * g:4 * g + 4, :] for g in range(2)]
    X8T = X2T
    tmp = kk
    off = [[mem.take(4, P) for _ in range(3)] for _ in range(2)]
    r, k, v = m[:, 0:4, :], m[:, 4:8, :], m[:, 8:12, :]
    vec = lambda at, n=4: spread(K.vec[:, at:at + n], P)
    flat = lambda z: z.rearrange("p a b -> p (a b)")
    bank = lambda b: ps[:, b, :].rearrange("p (a b) -> p a b", b=P)

    wout_in = sem("wout_in")
    K.wout_in = wout_in
    GR = range(2)
    LV = range(3)
    chain = ("X2", "X2T", "T1", "X4", "X4T", "T2", "X8T", "T3", "TT")
    Df = Steps(sem("front_dve_step"), ["sg", "zw", "ld", "za", "a", "kk0", "kk_sq", "scan0", "scan1", "scan2", "scan3",
                                       "norm_floor", "norm_inv", "kk", "lam_rel", "lam_prev", "a1", "k"])
    Af = Steps(sem("front_act_step"), ["xw", "sg", "ld", "a", "norm", "em", "em_exp", "gr", "gi", "gp"])
    Gf = Steps(sem("front_pool_step"), ["diff", "mixed_in", "m"])
    Pf = Steps(sem("front_pe_step"), ["zw", "za", "norm"])
    Dc = Steps(sem("core_dve_step"),
               ["kT", "ba", "bT", "aT", "rT", "Sh", "gr_end"]
               + [f"{n}{g}" for g in GR for n in ("D", "DT", "T0", "AkT", "RbT", "RkT")]
               + ["rk", "rk2", "T10", "T11", "T20", "T21", "bonus", "T30", "T31"]
               + [f"{n}_{l}{g}" for l in LV for n in ("T", "TT") for g in GR if (n, l) != ("T", 2)]
               + ["S_add", "S"])
    Ac = Steps(sem("core_act_step"),
               ["v_tok", "A_T0", "A_T1", "k_tok", "X20", "X21", "X2T0", "X2T1", "b_tok", "X40", "X41", "X4T0", "X4T1",
                "X8T0", "X8T1", "zg", "TT0", "TT1"]
               + [f"Y{l}{g}" for l in LV for g in GR]
               + [f"rhs{g}" for g in GR] + [f"SA{g}" for g in GR] + ["o"])
    Gc = Steps(sem("core_pool_step"), [f"off{l}{g}" for g in GR for l in LV])
    Pc = Steps(sem("core_pe_step"),
               ["v_tok"] + [f"{n}{g}" for g in GR for n in ("A", "A_T", "AkT", "RbT", "RkT")]
               + ["k_tok", "X20", "X21", "X2T0", "X2T1", "b_tok", "T10", "T11", "X40", "X41", "X4T0", "X4T1",
                  "bonus", "T20", "T21", "zg", "X8T0", "X8T1", "T30", "T31", "TT0", "TT1"]
               + [f"{n}_{l}{g}" for l in LV for n in ("Y", "T", "TT") for g in GR if (n, l) != ("T", 2)]
               + [f"rhs{g}" for g in GR] + [f"SA{g}" for g in GR] + ["S", "o"])
    Dt = Steps(sem("tail_dve_step"), ["oc", "o_sq", "var", "std_inv", "on", "ow", "ob", "o_bonus", "y"])
    At = Steps(sem("tail_act_step"), ["std"])
    Pt = Steps(sem("tail_pe_step"), ["mean", "var"])

    waited = sem("waited")

    BANK = {"mean": 3, "v_tok": 7, "var": 3, "k_tok": 7, "b_tok": 3, "bonus": 7, "zg": 3, "zw": 7, "za": 3,
            "norm": 7, "o": 3, "S": 7}
    for g in GR:
        for j, n in enumerate(("A", "A_T", "AkT", "RbT", "RkT")):
            BANK[f"{n}{g}"] = 4 * g + j % 3
        for j, n in enumerate(chain):
            BANK[f"{n}{g}"] = 4 * g + j % 3
        for l in LV:
            for j, n in enumerate(("Y", "T", "TT")):
                BANK[f"{n}_{l}{g}"] = 4 * g + j
        BANK[f"rhs{g}"] = 4 * g
        BANK[f"SA{g}"] = 4 * g + 1
    READ = {"zw": (Df, "zw"), "za": (Df, "za"), "zg": (Ac, "zg"), "norm": (Af, "norm"),
            "bonus": (Dc, "bonus"), "b_tok": (Ac, "b_tok"), "k_tok": (Ac, "k_tok"), "v_tok": (Ac, "v_tok"),
            "o": (Ac, "o"), "S": (Dc, "S_add"), "mean": (Dt, "oc"), "var": (Dt, "var")}
    for g in GR:
        READ[f"A{g}"], READ[f"A_T{g}"] = (Dc, f"D{g}"), (Dc, f"DT{g}")
        for n in ("AkT", "RbT", "RkT", "T1", "T2", "T3"):
            READ[f"{n}{g}"] = (Dc, f"{n}{g}")
        for n in ("X2", "X2T", "X4", "X4T", "X8T", "TT", "rhs", "SA"):
            READ[f"{n}{g}"] = (Ac, f"{n}{g}")
        for l in LV:
            READ[f"Y_{l}{g}"] = (Ac, f"Y{l}{g}")
            READ[f"T_{l}{g}"], READ[f"TT_{l}{g}"] = (Dc, f"T_{l}{g}"), (Dc, f"TT_{l}{g}")

    def tiles(eng, front, core):
        front(0)
        core(0, False, True)
        with eng.Fori(0, NT - 2) as i:
            core(i + 1, True, True)
        core(NT - 1, True, False)

    with nc.Block() as block:
        @block.sync
        def _(sp):
            sp.dma_start(flat(K.w_out_sb), K.w_out).then_inc(wout_in, 16)
            sp.wait_ge(wout_in, 16)

        @block.gpsimd
        def _(pool):
            for steps in (Gf, Gc):
                pool.sem_inc(steps.sem, 1)
            tt = nc.gpsimd.tensor_tensor

            def front(j):
                if isinstance(j, int) and j == 0:
                    return
                Gf.k = 0
                Gf.await_last_run(pool, j)
                pool.sem_inc(waited, 1)
                now = K.prw[:, :, bass.ds(j * P + 1, P)]
                Gf.done(tt(diff, K.prw[:, :, bass.ds(j * P, P)], now, ALU.subtract), "diff")
                Gf.await_(pool, "diff", j)
                Gf.done(tt(diff, diff, vec(V_MU, NRW), ALU.mult), "mixed_in")
                Gf.await_(pool, "mixed_in", j)
                Pc.await_(pool, "v_tok", j - 1)
                Dc.await_(pool, "bonus", j - 1)
                pool.sem_inc(waited, 1)
                Gf.done(tt(m, diff, now, ALU.add), "m")

            def core(i, with_tail, with_front):
                Gc.k = 0
                for g in GR:
                    for l in LV:
                        if l == 0:
                            Ac.await_(pool, f"A_T{g}", i)
                        Gc.done(tt(off[g][l], A_T[g], over(K.m_off[l], 4), ALU.mult), f"off{l}{g}")
                if with_front:
                    Gc.await_last_run(pool, i + 1)
                    Dc.await_(pool, "DT1", i)
                    front(i + 1)

            tiles(pool, front, core)

        @block.vector
        def _(dve):
            vt = nc.vector
            tt, ts, stt = vt.tensor_tensor, vt.tensor_scalar, vt.scalar_tensor_tensor
            mul, add = ALU.mult, ALU.add
            dve.sem_inc(Df.sem, 1)
            dve.sem_inc(Dt.sem, 1)
            vt.memset(flat(S), 0.0).then_inc(Dc.sem, 1)

            def front(j, piece=None):
                for p in range(5) if piece is None else (piece,):
                    if p == 0:
                        Df.k = 0
                        Df.await_last_run(dve, j)
                        Af.await_(dve, "sg", j)
                        Df.done(ts(sg, sg, 0.5, 0.5, mul, add), "sg")
                        Pf.await_(dve, "zw", j)
                        Df.done(tt(ld, bank(7), vec(V_W0), add), "zw")
                    if p == 1:
                        Af.await_(dve, "ld", j)
                        Df.done(ts(ld, ld, -DECAY / 2, -DECAY / 2, mul, add), "ld")
                        Pf.await_(dve, "za", j)
                        Df.done(tt(a, bank(3), vec(V_A0), add), "za")
                    if p == 2:
                        Af.await_(dve, "a", j)
                        Df.done(ts(a, a, 0.5, 0.5, mul, add), "a")
                        Df.done(tt(kk, k, vec(V_KK), mul), "kk0")
                        Df.await_(dve, "kk0", j)
                        Df.done(tt(sq, kk, kk, mul), "kk_sq")
                    if p == 3:
                        Df.await_(dve, "ld", j)
                        for c in range(4):
                            Df.done(vt.tensor_tensor_scan(lam[:, c, :], K.ones, ld[:, c, :], 0.0, mul, add),
                                    f"scan{c}")
                    if p == 4:
                        Af.await_(dve, "norm", j)
                        Df.done(ts(sq, sq, 1e-12, None, ALU.max), "norm_floor")
                        Df.await_(dve, "norm_floor", j)
                        Df.done(vt.reciprocal(flat(sq), flat(sq)), "norm_inv")
                        Df.await_(dve, "norm_inv", j)
                        Df.done(tt(kk, kk, sq, mul), "kk")
                        Af.await_(dve, "em_exp", j)
                        Df.done(tt(lam, lam, spread(em, P), ALU.subtract), "lam_rel")
                        Df.await_(dve, "lam_rel", j)
                        Df.done(tt(gp, lam, ld, ALU.subtract), "lam_prev")
                        Df.await_(dve, "lam_prev", j)
                        Df.done(stt(out=ld, in0=a, scalar=-1.0, in1=vec(V_KA), op0=add, op1=mul), "a1")
                        Df.await_(dve, "a1", j)
                        Df.done(stt(out=k, in0=ld, scalar=1.0, in1=k, op0=add, op1=mul), "k")

            def tail(j, piece=None):
                for p in range(4) if piece is None else (piece,):
                    if p == 0:
                        Dt.k = 0
                        Dt.await_last_run(dve, j)
                        Pt.await_(dve, "mean", j)
                        Dt.done(stt(out=o, in0=bank(3), scalar=-1.0 / HD, in1=o, op0=mul, op1=add), "oc")
                        Dt.await_(dve, "oc", j)
                        Dt.done(tt(tmp, o, o, mul), "o_sq")
                    if p == 1:
                        Pt.await_(dve, "var", j)
                        Dt.done(ts(tmp, bank(3), 1.0 / HD, GN_EPS, mul, add), "var")
                    if p == 2:
                        At.await_(dve, "std", j)
                        Dt.done(vt.reciprocal(flat(tmp), flat(tmp)), "std_inv")
                        Dt.await_(dve, "std_inv", j)
                        Dt.done(tt(o, o, tmp, mul), "on")
                    if p == 3:
                        Dt.await_(dve, "on", j)
                        Dt.done(tt(o, o, vec(V_LW), mul), "ow")
                        Dt.await_(dve, "ow", j)
                        Dt.done(tt(o, o, vec(V_LB), add), "ob")
                        Dt.await_(dve, "ob", j)
                        Dt.done(tt(o, o, bonus, add), "o_bonus")
                        Dt.await_(dve, "o_bonus", j)
                        Ac.await_(dve, "zg", j)
                        Dt.done(tt(K.yT[:, 4:8, bass.ds(j * P, P)], o, gg, mul), "y")

            def core(i, with_tail, with_front):
                Dc.k = 0

                def w(*names):
                    for n in names:
                        Dc.await_(dve, n, i)

                def wp(name):
                    Pc.await_(dve, name, i)

                def masked(g):
                    b0 = 4 * g
                    wp(f"A{g}")
                    Dc.done(tt(Dm[g], bank(b0), over(K.m_d, 4), mul), f"D{g}")
                    wp(f"A_T{g}")
                    Ac.await_(dve, f"A_T{g}", i)
                    Dc.done(tt(DTm[g], bank(b0 + 1), over(K.m_dt, 4), mul), f"DT{g}")
                    w(f"D{g}")
                    Dc.done(tt(Tm[g], Dm[g], over(K.ident, 4), add), f"T0{g}")
                    for n, dst, mask in (("AkT", AkT, K.m_after), ("RbT", RbT, K.m_from), ("RkT", RkT, K.m_from)):
                        wp(f"{n}{g}")
                        Dc.done(tt(dst[g], bank(BANK[f"{n}{g}"]), over(mask, 4), mul), f"{n}{g}")

                def power(n):
                    for g in GR:
                        wp(f"{n}{g}")
                        Dc.done(tt(Tm[g], bank(BANK[f"{n}{g}"]), Tm[g], add), f"{n}{g}")

                def double(n, l):
                    dst = Tm if n == "T" else TT
                    for g in GR:
                        wp(f"{n}_{l}{g}")
                        Dc.done(tt(dst[g], bank(BANK[f"{n}_{l}{g}"]), dst[g], add), f"{n}_{l}{g}")

                Dc.await_last_run(dve, i)
                Df.await_last_run(dve, i + 1)
                Af.await_last_run(dve, i + 1)
                Dc.done(tt(kT, k, gi, mul), "kT")
                Dc.done(tt(bT, kk, a, mul), "ba")
                w("ba")
                Dc.done(tt(bT, bT, gi, mul), "bT")
                Pc.await_last_run(dve, i)
                Dc.done(stt(out=aT, in0=kk, scalar=-1.0, in1=gp, op0=mul, op1=mul), "aT")
                Dc.done(tt(rT, r, gr, mul), "rT")
                Dc.done(tt(Sh, S, spread(em_exp, HD), mul), "Sh")
                Dc.done(vt.tensor_copy(gr_end, gr[:, :, P - 1]), "gr_end")
                if with_tail:
                    w("aT")
                    tail(i - 1, 0)
                masked(0)
                if with_tail:
                    tail(i - 1, 1)
                masked(1)
                Dc.done(tt(sq, r, k, mul), "rk")
                w("rk")
                Dc.done(tt(sq, sq, vec(V_RK), mul), "rk2")
                power("T1")
                if with_tail:
                    tail(i - 1, 2)
                power("T2")
                if with_tail:
                    tail(i - 1, 3)
                    Dt.await_last_run(dve, i)
                wp("bonus")
                Dc.done(tt(bonus, bank(7), v, mul), "bonus")
                power("T3")
                double("T", 0)
                if with_front:
                    front(i + 1, 0)
                double("TT", 0)
                if with_front:
                    front(i + 1, 1)
                double("T", 1)
                if with_front:
                    front(i + 1, 2)
                double("TT", 1)
                if with_front:
                    front(i + 1, 3)
                double("TT", 2)
                if with_front:
                    front(i + 1, 4)
                wp("S")
                Dc.done(tt(S, ps[:, 7, 0:4 * HD].rearrange("p (a b) -> p a b", b=HD), Sh, add), "S_add")
                w("S_add")
                Dc.done(tt(S, S, spread(gr_end, HD), mul), "S")

            now = K.prw[:, :, 1:1 + P]
            Gf.k = 0
            Gf.await_last_run(dve, 0)
            Gf.done(tt(diff, K.prw[:, :, 0:P], now, ALU.subtract), "diff")
            Gf.await_(dve, "diff", 0)
            Gf.done(tt(diff, diff, vec(V_MU, NRW), mul), "mixed_in")
            Gf.await_(dve, "mixed_in", 0)
            Gf.done(tt(m, diff, now, add), "m")
            Gf.await_(dve, "m", 0)
            tiles(dve, front, core)
            K.dve_tail = tail

        @block.scalar
        def _(act):
            f, copy = nc.scalar.activation, nc.scalar.copy
            for steps in (Af, Ac, At):
                act.sem_inc(steps.sem, 1)

            def front(j, piece=None):
                for p in range(5) if piece is None else (piece,):
                    if p == 0:
                        Af.k = 0
                        Gf.await_(act, "m", j)
                        Af.done(f(xw[0:HD, :], m[0:HD, 12, :], ACT.Tanh), "xw")
                        Af.done(f(sg, m[:, 13, :], ACT.Tanh, scale=0.5), "sg")
                    if p == 1:
                        Df.await_(act, "zw", j)
                        Af.done(f(ld, ld, ACT.Tanh, scale=0.5), "ld")
                        Df.await_(act, "za", j)
                        Af.done(f(a, a, ACT.Tanh, scale=0.5), "a")
                    if p == 2:
                        Pf.await_(act, "norm", j)
                        Af.done(f(sq, bank(7), ACT.Sqrt), "norm")
                    if p == 3:
                        Df.await_(act, "scan3", j)
                        Af.done(copy(em, lam[:, :, 63]), "em")
                        Af.done(f(em_exp, lam[:, :, 63], ACT.Exp), "em_exp")
                    if p == 4:
                        Df.await_(act, "lam_rel", j)
                        Af.done(f(gr, lam, ACT.Exp), "gr")
                        Af.done(f(gi, lam, ACT.Exp, scale=-1.0), "gi")
                        Df.await_(act, "lam_prev", j)
                        Af.done(f(gp, gp, ACT.Exp), "gp")

            def tail(j):
                Dt.await_(act, "var", j)
                At.k = 0
                At.done(f(tmp, tmp, ACT.Sqrt), "std")

            def core(i, with_tail, with_front):
                Ac.k = 0

                def keep(dst, name):
                    Pc.await_(act, name, i)
                    Ac.done(copy(dst, bank(BANK[name])), name)

                def both(dst, name):
                    for g in GR:
                        keep(dst[g], f"{name}{g}")

                keep(v_tok, "v_tok")
                both(A_T, "A_T")
                if with_tail:
                    tail(i - 1)
                keep(k_tok, "k_tok")
                both(X2, "X2")
                both(X2T, "X2T")
                keep(b_tok, "b_tok")
                both(X4, "X4")
                both(X4T, "X4T")
                both(X8T, "X8T")
                if with_tail:
                    Dt.await_last_run(act, i)
                keep(gg, "zg")
                both(TT, "TT")
                for l in LV:
                    for g in GR:
                        Pc.await_(act, f"Y_{l}{g}", i)
                        Ac.done(copy(Y[g], bank(BANK[f"Y_{l}{g}"])), f"Y{l}{g}")
                    if with_front:
                        if l == 0:
                            Pc.await_(act, "zg", i)
                        front(i + 1, l)
                for n, dst, piece in (("rhs", rhs, 3), ("SA", SA, 4)):
                    for g in GR:
                        Pc.await_(act, f"{n}{g}", i)
                        Ac.done(copy(flat(dst[g]), ps[:, BANK[f"{n}{g}"], 0:4 * HD]), f"{n}{g}")
                    if with_front:
                        front(i + 1, piece)
                if with_tail:
                    Dt.await_last_run(act, i)
                keep(o, "o")

            tiles(act, front, core)
            K.act_tail = tail

        @block.tensor
        def _(pe):
            for steps in (Pf, Pc, Pt):
                pe.sem_inc(steps.sem, 1)
            held = {}

            def free(name, run):
                if BANK[name] in held:
                    before, its_run = held[BANK[name]]
                    steps, n = READ[before]
                    steps.await_(pe, n, its_run)
                held[BANK[name]] = name, run

            def front(j, piece=None):
                for p in range(2) if piece is None else (piece,):
                    if p == 0:
                        Pf.k = 0
                        Af.await_(pe, "xw", j)
                        free("zw", j)
                        for c in range(4):
                            mm = pe.matmul(bank(7)[:, c, :], K.lw[0:HD, c * P:(c + 1) * P], xw[0:HD, :],
                                           start=True, stop=True)
                        Pf.done(mm, "zw")
                        free("za", j)
                        for c in range(4):
                            mm = pe.matmul(bank(3)[:, c, :], K.lw[HD:P, c * P:(c + 1) * P], m[HD:P, 12, :],
                                           start=True, stop=True)
                        Pf.done(mm, "za")
                    if p == 1:
                        Df.await_(pe, "kk_sq", j)
                        free("norm", j)
                        Pf.done(pe.matmul(ps[:, 7, :], K.head_sum, flat(sq), start=True, stop=True), "norm")

            def tail(j, piece=None):
                for p in range(2) if piece is None else (piece,):
                    if p == 0:
                        Pt.k = 0
                        Ac.await_(pe, "o", j)
                        free("mean", j)
                        Pt.done(pe.matmul(ps[:, 3, :], K.head_sum, flat(o), start=True, stop=True), "mean")
                    if p == 1:
                        Dt.await_(pe, "o_sq", j)
                        free("var", j)
                        Pt.done(pe.matmul(ps[:, 3, :], K.head_sum, flat(tmp), start=True, stop=True), "var")

            def core(i, with_tail, with_front):
                Pc.k = 0
                held.clear()
                Dc.await_last_run(pe, i)
                Ac.await_last_run(pe, i)
                Df.await_last_run(pe, i + 1)
                Af.await_last_run(pe, i + 1)
                Pc.await_last_run(pe, i)

                def w(*names):
                    for n in names:
                        Dc.await_(pe, n, i)

                def wa(*names):
                    for n in names:
                        Ac.await_(pe, n, i)

                def turn(name, src):
                    free(name, i)
                    for c in range(4):
                        mm = pe.transpose(bank(BANK[name])[:, c, :], src[:, c, :], K.ident)
                    Pc.done(mm, name)

                def heads(name, g, lhs, rhs_, n=P):
                    free(f"{name}{g}", i)
                    for c in range(4):
                        mm = pe.matmul(ps[:, BANK[f"{name}{g}"], c * n:(c + 1) * n], lhs[:, c, :],
                                       rhs_[:, c, :], start=True, stop=True)
                    Pc.done(mm, f"{name}{g}")

                if with_tail:
                    tail(i - 1, 0)
                turn("v_tok", v)
                w("aT")
                for g in GR:
                    h = slice(g * HD, (g + 1) * HD)
                    heads("A", g, aT[h], bT[h])
                    heads("A_T", g, bT[h], aT[h])
                    heads("AkT", g, kT[h], aT[h])
                    w("rT")
                    heads("RbT", g, bT[h], rT[h])
                    heads("RkT", g, kT[h], rT[h])
                    if with_tail and g == 0:
                        tail(i - 1, 1)
                turn("k_tok", kT)
                for name, lhs, r_, need, needa in (
                        ("X2", DTm, Dm, ("DT",), ()), ("X2T", Dm, DTm, (), ()),
                        ("T1", X2T, Tm, ("T0",), ("X2T",)),
                        ("X4", X2T, X2, (), ("X2",)), ("X4T", X2, X2T, (), ()),
                        ("T2", X4T, Tm, ("T1",), ("X4T",)),
                        ("X8T", X4, X4T, (), ()), ("T3", X8T, Tm, ("T2",), ("X8T",))):
                    for g in GR:
                        w(*(n + str(g) for n in need))
                        wa(*(n + str(g) for n in needa))
                        heads(name, g, lhs[g], r_[g])
                    if name == "X2T":
                        turn("b_tok", bT)
                    if name == "X4T":
                        w("rk2")
                        free("bonus", i)
                        Pc.done(pe.matmul(ps[:, 7, :], K.head_sum, flat(sq), start=True, stop=True), "bonus")
                    if name == "T2":
                        free("zg", i)
                        for c in range(4):
                            mm = pe.matmul(bank(3)[:, c, :], K.lg[:, c * P:(c + 1) * P], sg, start=True, stop=True)
                        Pc.done(mm, "zg")
                for g in GR:
                    w(f"T3{g}")
                    turn(f"TT{g}", Tm[g])
                for l in LV:
                    for g in GR:
                        Gc.await_(pe, f"off{l}{g}", i)
                        if l:
                            w(f"T_{l - 1}{g}")
                        heads(f"Y_{l}", g, off[g][l], Tm[g])
                    if with_front and l == 2:
                        front(i + 1, 1)
                    if l < 2:
                        for g in GR:
                            wa(f"Y{l}{g}", f"TT{g}")
                            if l:
                                w(f"TT_{l - 1}{g}")
                            heads(f"T_{l}", g, TT[g], Y[g])
                    if with_front and l == 0:
                        front(i + 1, 0)
                    for g in GR:
                        wa(f"Y{l}{g}", f"TT{g}")
                        if l:
                            w(f"TT_{l - 1}{g}")
                        heads(f"TT_{l}", g, Y[g], TT[g])
                wa("v_tok")
                for g in GR:
                    h = slice(g * HD, (g + 1) * HD)
                    w(f"AkT{g}", "Sh")
                    free(f"rhs{g}", i)
                    for c in range(4):
                        dst = ps[:, BANK[f"rhs{g}"], c * HD:(c + 1) * HD]
                        pe.matmul(dst, AkT[g][:, c, :], v_tok[:, c, h], start=True, stop=False)
                        mm = pe.matmul(dst, aT[h, c, :], Sh[h, c, :], start=False, stop=True)
                    Pc.done(mm, f"rhs{g}")
                for g in GR:
                    w(f"TT_2{g}")
                    wa(f"rhs{g}")
                    heads("SA", g, TT[g], rhs[g], HD)
                wa("SA1")
                free("S", i)
                for g in GR:
                    h = slice(g * HD, (g + 1) * HD)
                    for c in range(4):
                        dst = ps[h, 7, c * HD:(c + 1) * HD]
                        pe.matmul(dst, b_tok[:, c, h], SA[g][:, c, :], start=True, stop=False)
                        mm = pe.matmul(dst, k_tok[:, c, h], v_tok[:, c, h], start=False, stop=True)
                Pc.done(mm, "S")
                free("o", i)
                for g in GR:
                    h = slice(g * HD, (g + 1) * HD)
                    for c in range(4):
                        dst = ps[h, 3, c * P:(c + 1) * P]
                        pe.matmul(dst, v_tok[:, c, h], RkT[g][:, c, :], start=True, stop=False)
                        pe.matmul(dst, SA[g][:, c, :], RbT[g][:, c, :], start=False, stop=False)
                        mm = pe.matmul(dst, Sh[h, c, :], rT[h, c, :], start=False, stop=True)
                Pc.done(mm, "o")

            tiles(pe, front, core)
            K.pe_tail = tail
            K.tail_steps = Dt


def experts(nc, K):
    ps, sem = K.ps, K.sem
    low = Space(K.sb, K.LOW, K.F0)
    w = [low.take(D) for _ in range(7)]
    mem = Space(K.sb, low.at, K.F0)
    high = Space(K.sb, K.F0, K.TOP)
    w += [high.take(D) for _ in range(8)]
    u = high.take(16, D)
    w += [high.take(D)]
    diag = high.take(4, P)
    g_ffn = w[15]
    g_row = mem.take(D)
    junk = K.sb[:, mem.at:mem.at + D]
    cand, cand2, hit_a, hit_b = (mem.take(16, 16) for _ in range(4))
    best, z, z2, ex, gate, wt = (mem.take(2, 16) for _ in range(6))
    pos = mem.take(16).bitcast(U32)
    pos_a = mem.take(16).bitcast(U32)
    pos_b = mem.take(16).bitcast(U32)
    i_a, i_b = mem.take(16), mem.take(16)
    idx = mem.take(2, 16).bitcast(U32)
    nbest, ex_sum = mem.take(2, 1), mem.take(2, 1)
    flat = lambda a: a.rearrange("p a b -> p (a b)")
    ring = mem.take(2, DC + 1, P)
    q_sb, sc, sc2 = mem.take(T), mem.take(NT, P), mem.take(NT, P)
    key_val, key_idx = mem.take(2, NT, 16), mem.take(2, NT, 16)
    key_num = mem.take(2, NT, 16).bitcast(U32)
    N = NT * NH
    ms, rstd = K.stat[:, 0, 0:NT], K.stat[:, 1, 0:NT]
    ms3, rstd3 = K.stat[:, 2, 0:NT], K.stat[:, 3, 0:NT]
    spent = flat(ring[:, 0, 0:DC, :])
    assert DC * P == D
    S0 = [5, 0, 5, 6]

    x_in, g_ffn_in = sem("x_again"), sem("g_ffn_in")
    y_out, x_added, sq_kept, eps_kept, rooted, inverted = (
        sem(n) for n in ("mixed_out", "x_added", "sq2_kept", "eps2_kept", "rooted2", "inverted2"))
    h_kept, h_turned, hT_kept = sem("h2_kept"), sem("h2_turned"), sem("h2T_kept")
    first = Steps(sem("first_key_step"), [f"{n}{s}" for n in ("max", "idx", "cut", "max2", "idx2") for s in range(2)]
                  + ["index"])

    u_in = [sem(f"u_in{k}") for k in range(16)]
    v_in = [sem(f"v_in{k}") for k in range(16)]
    g_in = sem("g_fin_in")
    u_used, v_used, diag_set, idx_set = sem("u_used"), sem("v_used"), sem("diag_set"), sem("idx_set")
    best_neg, exp_kept, tanh_kept, y_kept = sem("best_negated"), sem("exp_kept"), sem("tanh_kept"), sem("y_kept")
    final = [sem(f"final_step{t}") for t in range(NT)]
    waited = sem("waited2")
    rooted3, out_done = sem("rooted3"), sem("out_done")
    wq_in = [sem("wq_in0"), sem("wq_in1")]
    q_out, q_kept, s_out, s_kept = sem("query_out"), sem("query_kept"), sem("key_score_out"), sem("key_score_kept")
    top = Steps(sem("top_key_step"), [f"{n}{t}" for n in ("max", "idx", "cut", "max2", "idx2") for t in range(NT)]
                + ["index"])
    R = Steps(sem("route_step"), ["cand", "best", "pos", "cut", "best2", "pos2", "row", "col", "hit_a",
                                  "val_a", "i_a", "hit_b", "val_b", "i_b"])
    G = Steps(sem("gelu_step"), ["sq", "poly", "arg", "sum_inv", "gate", "half", "wt"])

    with nc.Block() as block:
        @block.sync
        def _(sp):
            def load(h):
                for s in range(2):
                    if not isinstance(h, int):
                        sp.wait_ge(s_out, 2 * h + s + 1)
                    sp.dma_start(ring[:, s, :, :].rearrange("p c n -> p (c n)"),
                                 K.wq_sk[2 * h + s]).then_inc(wq_in[s], 16)

            sp.dma_start(K.x1.rearrange("p t d -> p (t d)"), K.x.rearrange("p t d -> p (t d)")).then_inc(x_in, 16)
            sp.dma_start(g_ffn, K.g_ffn.to_broadcast([P, D])).then_inc(g_ffn_in, 16)
            load(0)
            sp.dma_start(g_row, K.g_fin.to_broadcast([P, D])).then_inc(g_in, 16)
            sp.wait_ge(s_out, NT)
            with sp.Fori(0, NH - 1) as h:
                load(h + 1)
            for t in range(NT):
                sp.wait_ge(final[t], 4)
                sp.dma_start(K.out[:, t, :], K.x1[:, t, :]).then_inc(out_done, 16)
            sp.wait_ge(out_done, 16 * NT)

        @block.gpsimd
        def _(pool):
            with pool.Fori(0, N // 2) as i:
                for par in range(2):
                    n = 2 * i + par
                    pool.wait_ge(idx_set, n + 1)
                    for k in range(16):
                        pool.wait_ge(u_used, n * 16 + k + 1)
                        pool.sem_inc(waited, 1)
                        pool.indirect_dma_start(
                            u[:, k, :], None, K.peer_u,
                            bass.IndirectOffsetOnAxis(ap=idx[:, par, k:k + 1], axis=0)).then_inc(u_in[k], 16)
                    pool.wait_ge(y_out, 2 * NT)
                    for k in range(16):
                        if k == 15:
                            pool.wait_ge(h_kept, NT)
                        pool.wait_ge(v_used, n * 16 + k + 1)
                        pool.sem_inc(waited, 1)
                        pool.indirect_dma_start(
                            w[k], None, K.peer_v,
                            bass.IndirectOffsetOnAxis(ap=idx[:, par, k:k + 1], axis=0)).then_inc(v_in[k], 16)

        @block.tensor
        def _(pe):
            pe.sem_inc(v_used, 16)

            def mixed(n):
                t, half = n // 2, n % 2
                if n >= 4:
                    pe.wait_ge(x_added, t - 1)
                for c in range(8):
                    mm = pe.matmul(ps[:, n % 4, :], K.yT[:, c, t * P:(t + 1) * P],
                                   K.w_out_sb[:, c, half * 512:(half + 1) * 512],
                                   start=(c == 0), stop=(c == 7))
                mm.then_inc(y_out, 1)

            def first_scores(t):
                pe.wait_ge(h_kept, t + 1)
                for half in range(2):
                    if t:
                        pe.wait_ge(hT_kept, 2 * t - 1 + half)
                    for c in range(4):
                        at = (4 * half + c) * P
                        mm = pe.transpose(ps[:, 6 + half, c * P:(c + 1) * P], K.h2[:, t, at:at + P], K.ident)
                    mm.then_inc(h_turned, 1)
                pe.wait_ge(hT_kept, 2 * t + 2)
                if t:
                    pe.wait_ge(q_kept, t)
                for s in range(2):
                    pe.wait_ge(wq_in[s], 16)
                    for c in range(DC):
                        mm = pe.matmul(ps[:, 4, s * P:(s + 1) * P], ring[:, s, c, :], K.h2T[:, c, t * P:(t + 1) * P],
                                       start=(c == 0), stop=(c == DC - 1))
                mm.then_inc(q_out, 1)
                pe.wait_ge(q_kept, t + 1)
                if t == 1:
                    pe.wait_ge(x_added, 3)
                if t == 2:
                    pe.wait_ge(s_kept, 1)
                for s in range(2):
                    mm = pe.matmul(ps[:, S0[t], s * P:(s + 1) * P], q_sb[:, s * P:(s + 1) * P],
                                   ring[:, s, DC, :], start=True, stop=True)
                mm.then_inc(s_out, 1)

            def queries(h, s):
                m = 2 * h + s
                pe.wait_ge(wq_in[s], 16 * h + 16)
                pe.wait_ge(q_kept, m + 2)
                for c in range(DC):
                    mm = pe.matmul(ps[:, 4 + s, :], ring[:, s, c, :], K.h2T[:, c, :],
                                   start=(c == 0), stop=(c == DC - 1))
                mm.then_inc(q_out, 1)

            def scores(h, s):
                m = 2 * h + s
                pe.wait_ge(q_kept, m + 3)
                pe.wait_ge(s_kept, m + 1)
                for t in range(NT):
                    mm = pe.matmul(ps[:, 6 + s, t * P:(t + 1) * P], q_sb[:, t * P:(t + 1) * P],
                                   ring[:, s, DC, :], start=True, stop=True)
                mm.then_inc(s_out, 1)

            def add_rows(n, par):
                pe.wait_ge(y_kept, n + 1)
                for k in range(16):
                    pe.wait_ge(diag_set, n * 16 + k + 1)
                    pe.wait_ge(v_in[k], n * 16 + 16)
                    for half in range(2):
                        mm = pe.matmul(ps[:, 2 * par + half, :], diag[:, k % 4, :],
                                       w[k][:, half * 512:(half + 1) * 512],
                                       start=(k == 0), stop=(k == 15))
                    mm.then_inc(v_used, 1)

            def head(h, first_one=False, last=False):
                for t in range(NT):
                    if not last and t == 0:
                        queries(h + 1, 0)
                    if not last and t == 1:
                        if first_one:
                            pe.wait_ge(s_kept, NT)
                        scores(h + 1, 0)
                        queries(h + 1, 1)
                    if not last and t == 2:
                        scores(h + 1, 1)
                    add_rows(NT * h + t, t % 2)

            K.pe_tail(NT - 1, 0)
            pe.wait_ge(K.wout_in, 16)
            mixed(0)
            K.pe_tail(NT - 1, 1)
            for n in range(1, 3):
                mixed(n)
            first_scores(0)
            K.tail_steps.await_(pe, "var", NT - 1)
            for n in range(3, 2 * NT - 2):
                mixed(n)
            K.tail_steps.await_last_run(pe, NT)
            for n in range(2 * NT - 2, 2 * NT):
                mixed(n)
            for t in range(1, NT):
                first_scores(t)
            pe.wait_ge(x_added, NT)
            pe.wait_ge(s_kept, 2)
            head(0, first_one=True)
            with pe.Fori(0, NH - 2) as i:
                head(i + 1)
            head(NH - 1, last=True)

        @block.scalar
        def _(act):
            def exps(n, par):
                act.wait_ge(best_neg, n + 1)
                nc.scalar.activation(ex[:, par, :], best[:, par, :], ACT.Exp, bias=nbest[:, par, :],
                                     accum_out=ex_sum[:, par, :]).then_inc(exp_kept, 1)

            def keep_queries(h, s):
                m = 2 * h + s
                act.wait_ge(q_out, m + 3)
                act.wait_ge(s_out, m + 2)
                nc.scalar.copy(q_sb, ps[:, 4 + s, :]).then_inc(q_kept, 1)

            def head(h, first_one=False, last=False):
                for t in range(NT):
                    n, par = NT * h + t, t % 2
                    if not (last and t == NT - 1):
                        exps(n + 1, 1 - par)
                    G.await_(act, "arg", n)
                    nc.scalar.activation(z2[:, par, :], z2[:, par, :], ACT.Tanh, scale=GELU_B).then_inc(tanh_kept, 1)
                    G.await_(act, "wt", n)
                    for k in range(16):
                        act.wait_ge(v_used, n * 16 + k + 13)
                        nc.scalar.activation(diag[:, k % 4, :], K.ident, ACT.Copy,
                                             scale=wt[:, par, k:k + 1]).then_inc(diag_set, 1)
                    if not last and t < 2:
                        keep_queries(h + 1, t)
                    if last and t:
                        final_root(t - 1)

            def root(t):
                act.wait_ge(eps_kept, t + 1)
                nc.scalar.activation(rstd[:, t:t + 1], ms[:, t:t + 1], ACT.Sqrt).then_inc(rooted, 1)

            def final_root(t):
                act.wait_ge(final[t], 2)
                nc.scalar.activation(rstd3[:, t:t + 1], ms3[:, t:t + 1], ACT.Sqrt).then_inc(rooted3, 1)

            def keep_first(t):
                for half in range(2):
                    act.wait_ge(h_turned, 2 * t + half + 1)
                    nc.scalar.copy(K.h2T[:, 4 * half:4 * half + 4, t * P:(t + 1) * P],
                                   ps[:, 6 + half, :].rearrange("p (c t) -> p c t", c=4)).then_inc(hT_kept, 1)
                act.wait_ge(q_out, t + 1)
                if t:
                    act.wait_ge(s_out, t)
                nc.scalar.copy(q_sb[:, 0:2 * P], ps[:, 4, 0:2 * P]).then_inc(q_kept, 1)

            K.act_tail(NT - 1)
            root(0)
            keep_first(0)
            for t in range(1, NT):
                root(t)
            for t in range(1, NT):
                keep_first(t)
            exps(0, 0)
            head(0, first_one=True)
            with act.Fori(0, NH - 2) as i:
                head(i + 1)
            head(NH - 1, last=True)
            final_root(NT - 1)

        @block.vector
        def _(dve):
            v = nc.vector
            dve.sem_inc(u_used, 16)
            dve.sem_inc(R.sem, 1)
            dve.sem_inc(G.sem, 1)
            dve.sem_inc(top.sem, 1)
            dve.sem_inc(first.sem, 1)
            dve.sem_inc(y_kept, 2)

            def mixed(t):
                x = K.x1[:, t, :]
                dve.wait_ge(y_out, 2 * t + 2)
                b = 2 * (t % 2)
                v.tensor_tensor(x, flat(ps[:, b:b + 2, :]), x, ALU.add).then_inc(x_added, 1)
                dve.wait_ge(x_added, t + 1)
                if t:
                    dve.wait_ge(sq_kept, t)
                v.tensor_tensor_reduce(out=junk, in0=x, in1=x, scale=1.0, scalar=0.0, op0=ALU.mult,
                                       op1=ALU.add, accum_out=ms[:, t:t + 1]).then_inc(sq_kept, 1)
                dve.wait_ge(sq_kept, t + 1)
                v.tensor_scalar(ms[:, t:t + 1], ms[:, t:t + 1], 1.0 / D, EPS, ALU.mult,
                                ALU.add).then_inc(eps_kept, 1)
                dve.wait_ge(rooted, t + 1)
                v.reciprocal(rstd[:, t:t + 1], rstd[:, t:t + 1]).then_inc(inverted, 1)
                dve.wait_ge(inverted, t + 1)
                v.scalar_tensor_tensor(out=K.h2[:, t, :], in0=x, scalar=rstd[:, t:t + 1], in1=g_ffn,
                                       op0=ALU.mult, op1=ALU.mult).then_inc(h_kept, 1)

            def first_keys(t):
                first.k = 0
                dve.wait_ge(s_out, t + 1)
                first.await_last_run(dve, t)
                v.tensor_copy(flat(sc[:, 0:2, :]), ps[:, S0[t], 0:2 * P]).then_inc(s_kept, 1)
                dve.wait_ge(s_kept, t + 1)
                val, num = key_val[:, :, t, :], key_num[:, :, t, :]
                for s in range(2):
                    first.done(v.max(val[:, s, 0:8], sc[:, s, :]), f"max{s}")
                for s in range(2):
                    first.await_(dve, f"max{s}", t)
                    first.done(v.max_index(num[:, s, 0:8], val[:, s, 0:8], sc[:, s, :]), f"idx{s}")
                for s in range(2):
                    first.done(v.match_replace(sc2[:, s, :], val[:, s, 0:8], sc[:, s, :], -3.0e38), f"cut{s}")
                for s in range(2):
                    first.await_(dve, f"cut{s}", t)
                    first.done(v.max(val[:, s, 8:16], sc2[:, s, :]), f"max2{s}")
                for s in range(2):
                    first.await_(dve, f"max2{s}", t)
                    first.done(v.max_index(num[:, s, 8:16], val[:, s, 8:16], sc2[:, s, :]), f"idx2{s}")
                first.await_(dve, "idx21", t)
                first.done(v.tensor_copy(key_idx[:, :, t, :], num), "index")
                first.await_(dve, "index", t)

            def best_keys(h, s):
                m = 2 * h + s
                top.k = 0
                dve.wait_ge(s_out, m + 3)
                top.await_last_run(dve, m - 2)
                v.tensor_copy(flat(sc), ps[:, 6 + s, :]).then_inc(s_kept, 1)
                dve.wait_ge(s_kept, m + 3)
                dve.sem_inc(waited, 1)
                val, num = key_val[:, s, :, :], key_num[:, s, :, :]
                for t in range(NT):
                    top.done(v.max(val[:, t, 0:8], sc[:, t, :]), f"max{t}")
                for t in range(NT):
                    top.await_(dve, f"max{t}", m - 2)
                    dve.sem_inc(waited, 1)
                    top.done(v.max_index(num[:, t, 0:8], val[:, t, 0:8], sc[:, t, :]), f"idx{t}")
                for t in range(NT):
                    top.done(v.match_replace(sc2[:, t, :], val[:, t, 0:8], sc[:, t, :], -3.0e38), f"cut{t}")
                for t in range(NT):
                    top.await_(dve, f"cut{t}", m - 2)
                    dve.sem_inc(waited, 1)
                    top.done(v.max(val[:, t, 8:16], sc2[:, t, :]), f"max2{t}")
                for t in range(NT):
                    top.await_(dve, f"max2{t}", m - 2)
                    dve.sem_inc(waited, 1)
                    top.done(v.max_index(num[:, t, 8:16], val[:, t, 8:16], sc2[:, t, :]), f"idx2{t}")
                top.await_(dve, f"idx2{NT - 1}", m - 2)
                top.done(v.tensor_copy(key_idx[:, s, :, :], num), "index")

            def route(n, t):
                par = t % 2
                R.k = 0
                b = best[:, par, :]

                def w_(name):
                    R.await_(dve, name, n)

                R.await_last_run(dve, n)
                R.done(v.tensor_tensor(cand, spread(key_val[:, 0, t, :], 16),
                                       over(key_val[:, 1, t, :], 16), ALU.add), "cand")
                w_("cand")
                dve.sem_inc(waited, 1)
                R.done(v.max(b[:, 0:8], flat(cand)), "best")
                w_("best")
                dve.sem_inc(waited, 1)
                R.done(v.max_index(pos[:, 0:8], b[:, 0:8], flat(cand)), "pos")
                R.done(v.match_replace(flat(cand2), b[:, 0:8], flat(cand), -3.0e38), "cut")
                w_("cut")
                dve.sem_inc(waited, 1)
                R.done(v.max(b[:, 8:16], flat(cand2)), "best2")
                w_("best2")
                dve.sem_inc(waited, 1)
                R.done(v.max_index(pos[:, 8:16], b[:, 8:16], flat(cand2)), "pos2")
                w_("pos2")
                R.done(v.tensor_scalar(pos_a, pos, 4, None, ALU.logical_shift_right), "row")
                R.done(v.tensor_scalar(pos_b, pos, 15, None, ALU.bitwise_and), "col")
                for s, hit, p_, i_, side in (("a", hit_a, pos_a, i_a, 0), ("b", hit_b, pos_b, i_b, 1)):
                    w_("row" if s == "a" else "col")
                    R.done(v.tensor_tensor(hit, spread(p_, 16), over(K.iota16, 16), ALU.is_equal), "hit_" + s)
                    w_("hit_" + s)
                    R.done(v.tensor_tensor(hit, hit, over(key_idx[:, side, t, :], 16), ALU.mult), "val_" + s)
                    w_("val_" + s)
                    R.done(v.tensor_reduce(i_, hit, AX, ALU.add), "i_" + s)
                v.tensor_scalar(nbest[:, par, :], b[:, 0:1], -1.0, None, ALU.mult).then_inc(best_neg, 1)

            def number(n, par, first=False):
                R.await_(dve, "i_b", n)
                if not first:
                    dve.wait_ge(v_used, n * 16)
                v.scalar_tensor_tensor(out=idx[:, par, :], in0=i_a, scalar=128.0, in1=i_b, op0=ALU.mult,
                                       op1=ALU.add).then_inc(idx_set, 1)

            def dots(n, t):
                G.k = 0
                par = t % 2
                for k in range(16):
                    dve.wait_ge(u_in[k], n * 16 + 16)
                    v.tensor_tensor_reduce(out=u[:, k, :], in0=u[:, k, :], in1=K.h2[:, t, :], scale=1.0, scalar=0.0,
                                           op0=ALU.mult, op1=ALU.add,
                                           accum_out=z[:, par, k:k + 1]).then_inc(u_used, 1)
                dve.wait_ge(u_used, n * 16 + 32)
                zz, z_ = z2[:, par, :], z[:, par, :]
                G.done(v.tensor_tensor(zz, z_, z_, ALU.mult), "sq")
                G.await_(dve, "sq", n)
                G.done(v.tensor_scalar(zz, zz, GELU_A, 1.0, ALU.mult, ALU.add), "poly")
                G.await_(dve, "poly", n)
                G.done(v.tensor_tensor(zz, zz, z_, ALU.mult), "arg")
                dve.wait_ge(exp_kept, n + 1)
                G.done(v.reciprocal(ex_sum[:, par, :], ex_sum[:, par, :]), "sum_inv")
                G.await_(dve, "sum_inv", n)
                G.done(v.tensor_scalar(gate[:, par, :], ex[:, par, :], ex_sum[:, par, :], 0.5, ALU.mult, ALU.mult), "gate")
                dve.wait_ge(tanh_kept, n + 1)
                G.done(v.scalar_tensor_tensor(out=zz, in0=zz, scalar=1.0, in1=z_, op0=ALU.add, op1=ALU.mult), "half")
                G.await_(dve, "half", n)
                G.done(v.tensor_tensor(wt[:, par, :], zz, gate[:, par, :], ALU.mult), "wt")

            def add_up(n, t):
                par = t % 2
                dve.wait_ge(v_used, n * 16 + 32)
                dve.wait_ge(y_kept, n + 2)
                x = K.x1[:, t, :]
                v.tensor_tensor(x, flat(ps[:, 2 * par:2 * par + 2, :]), x, ALU.add).then_inc(y_kept, 1)

            def finish(t, part):
                x = K.x1[:, t, :]
                if part == 0:
                    dve.wait_ge(y_kept, N - NT + t + 3)
                    v.tensor_tensor_reduce(out=spent, in0=x, in1=x, scale=1.0, scalar=0.0, op0=ALU.mult,
                                           op1=ALU.add, accum_out=ms3[:, t:t + 1]).then_inc(final[t], 1)
                    dve.wait_ge(final[t], 1)
                    v.tensor_scalar(ms3[:, t:t + 1], ms3[:, t:t + 1], 1.0 / D, EPS, ALU.mult,
                                    ALU.add).then_inc(final[t], 1)
                else:
                    dve.wait_ge(rooted3, t + 1)
                    v.reciprocal(rstd3[:, t:t + 1], rstd3[:, t:t + 1]).then_inc(final[t], 1)
                    dve.wait_ge(final[t], 3)
                    v.scalar_tensor_tensor(out=x, in0=x, scalar=rstd3[:, t:t + 1], in1=g_row,
                                           op0=ALU.mult, op1=ALU.mult).then_inc(final[t], 1)

            def head(h, first_one=False, last=False):
                for t in range(NT):
                    n = NT * h + t
                    dots(n, t)
                    if not (last and t == NT - 1) and not (first_one and t == 0):
                        number(n + 1, (t + 1) % 2)
                    if not (first_one and t == 0):
                        add_up(n - 1, (t - 1) % NT)
                    if last:
                        if t:
                            finish(t - 1, 0)
                        if t > 1:
                            finish(t - 2, 1)
                        if t >= NT - 2:
                            continue
                    dve.wait_ge(idx_set, n + 2)
                    if t == 2:
                        best_keys(h + 1, 1)
                        top.await_(dve, "index", 2 * h + 1)
                        dve.sem_inc(waited, 1)
                    if first_one and t < 2:
                        first_keys(t + 2)
                    route(n + 2, (t + 2) % NT)
                    if t == 1 and not last:
                        R.await_(dve, "i_b", n + 2)
                        best_keys(h + 1, 0)

            K.dve_tail(NT - 1)
            dve.wait_ge(x_in, 16)
            dve.wait_ge(g_ffn_in, 16)
            for t in range(NT):
                mixed(t)
                if t == NT - 1:
                    dve.wait_ge(sq_kept, NT)
                if t == 0:
                    first_keys(0)
                    route(0, 0)
                    number(0, 0, first=True)
                    R.await_(dve, "i_b", 0)
            first_keys(1)
            dve.wait_ge(idx_set, 1)
            route(1, 1)
            number(1, 1, first=True)
            head(0, first_one=True)
            with dve.Fori(0, NH - 2) as i:
                head(i + 1)
            dve.wait_ge(g_in, 16)
            head(NH - 1, last=True)
            add_up(N - 1, NT - 1)
            finish(NT - 1, 0)
            finish(NT - 2, 1)
            finish(NT - 1, 1)


def block_kernel(nc, x, vecs, w_ch, w_tok, pe_k, pe_v, w1_k, w1_v, w2_k, w2_v, lora_w, lora_a,
                 lora_g, w_out, g_ffn, wq_sk, peer_u, peer_v, g_fin, out):
    with ExitStack() as ctx:
        def sem(name):
            return ctx.enter_context(nc.semaphore(name))

        K = Shared()
        K.sem = sem
        K.x, K.vecs, K.w_ch, K.w_tok = x, vecs, w_ch, w_tok
        K.pe_k, K.pe_v, K.w1_k, K.w1_v, K.w2_k, K.w2_v = pe_k, pe_v, w1_k, w1_v, w2_k, w2_v
        K.lora_w, K.lora_a, K.lora_g = lora_w, lora_a, lora_g
        K.w_out, K.g_ffn, K.wq_sk = w_out, g_ffn, wq_sk
        K.peer_u, K.peer_v, K.g_fin, K.out = peer_u, peer_v, g_fin, out
        K.NW = 52900
        K.sb = sb = ctx.enter_context(nc.sbuf_tensor("sb", [P, K.NW], F32))
        K.ps = ctx.enter_context(nc.psum_tensor("ps", [P, 8, 512], F32))

        keep = Space(sb, 0, K.NW)
        K.ident = keep.take(P)
        K.iota16 = keep.take(16)
        K.stat = keep.take(4, 8)
        K.LOW = keep.at
        K.head_sum = keep.take(P)
        K.m_d = keep.take(P)
        K.m_dt = keep.take(P)
        K.m_off = [keep.take(P) for _ in range(3)]
        K.m_after = keep.take(P)
        K.m_from = keep.take(P)
        K.ones = keep.take(P)
        K.slopes = keep.take(NH)
        K.vec = keep.take(NVEC)
        K.ndist = keep.take(T)
        K.ndcmp = keep.take(NT, 32)
        K.lw = keep.take(T)
        K.lg = keep.take(T)
        K.yT = keep.take(8, T)
        K.prw = keep.take(NRW, TP)
        K.F0 = keep.at
        both = sb[:, K.F0 - NRW * TP:K.F0 + CR * TP].rearrange("p (c t) -> p c t", t=TP)

        def chunk(n):
            return both[:, n, 1:TP]
        K.chunk = chunk

        K.TOP = K.NW - 3 * NT * D
        top = Space(sb, K.TOP, K.NW)
        K.x1 = top.take(NT, D)
        K.h2 = top.take(NT, D)
        K.h2T = top.take(DC, T)

        project(nc, K)
        attend(nc, K)
        recur(nc, K)
        experts(nc, K)


_F32 = "float32"


def layouts(i):
    import numpy as np

    def cols(w, n):
        return np.ascontiguousarray(w.reshape(DC, P, n, P).transpose(2, 1, 0, 3)).reshape(n, P, DC * P)

    def chan(v):
        return v.reshape(-1, P).T

    def pairs(w):
        return np.ascontiguousarray(w.reshape(-1, P, P).transpose(1, 0, 2)).reshape(P, -1)

    w = i["w_in"][0]
    kv = 512
    main = np.concatenate([w[:, 1304:3096], w[:, 0:512], w[:, kv:kv + 128], w[:, kv + 128:kv + 256],
                           w[:, kv + 256:kv + 384], w[:, kv + 512:kv + 640]], axis=1)
    tok = np.concatenate([w[:, kv + 384:kv + 512], w[:, kv + 640:kv + 768], w[:, 1280:1304]], axis=1)
    wq = cols(i["peer_w_q"][0], 16)
    sk = i["peer_sub_keys"][0].reshape(16, P, P).transpose(0, 2, 1)
    return {
        "x": np.ascontiguousarray(i["x"][0].reshape(NT, P, D).transpose(1, 0, 2)),
        "vecs": np.ascontiguousarray(np.concatenate(
            [chan(i["norm_mix_g"][0]), chan(i["rwkv_mu"][0])]
            + [chan(i[n][0].reshape(-1)) for n in ("rwkv_w0", "rwkv_a0", "rwkv_k_k", "rwkv_k_a",
                                                   "rwkv_r_k", "rwkv_ln_w", "rwkv_ln_b")], axis=1)),
        "w_ch": cols(main, NCH),
        "w_tok": np.ascontiguousarray(tok.reshape(DC, P, NTOK).transpose(1, 0, 2)).reshape(P, DC * NTOK),
        "pe_k": np.ascontiguousarray(i["cmp_k_pe"][0].reshape(-1, P).T),
        "pe_v": np.ascontiguousarray(i["cmp_v_pe"][0].reshape(-1, P).T),
        "w1_k": pairs(i["cmp_k_w1"][0]), "w1_v": pairs(i["cmp_v_w1"][0]),
        "w2_k": i["cmp_k_w2"][0], "w2_v": i["cmp_v_w2"][0],
        "lora_w": i["rwkv_w2"][0], "lora_a": i["rwkv_a2"][0], "lora_g": i["rwkv_g2"][0],
        "w_out": np.ascontiguousarray(i["w_out"][0].reshape(8, P, D).transpose(1, 0, 2)).reshape(P, 8 * D),
        "g_ffn": i["norm_ffn_g"][0].reshape(1, D),
        "wq_sk": np.ascontiguousarray(np.concatenate([wq, sk], axis=2)),
        "peer_u": i["peer_u"][0], "peer_v": i["peer_v"][0],
        "g_fin": i["norm_final_g"].reshape(1, D),
    }


def kernel(**inputs):
    import numpy as np
    import concourse.bacc as bacc
    from concourse.bass_utils import run_bass_kernel_spmd as run

    nc = bacc.Bacc("TRN2", target_bir_lowering=False, num_devices=1)
    arrays, args = {}, []
    for name, a in layouts({k: np.asarray(v) for k, v in inputs.items()}).items():
        arrays[f"in_{name}"] = a
        args.append(nc.dram_tensor(f"in_{name}", a.shape, mybir.dt.from_np(a.dtype), kind="ExternalInput").ap())
    args.append(nc.dram_tensor("out_x", (P, NT, D), F32, kind="ExternalOutput").ap())
    block_kernel(nc, *args)
    r = run(nc, [arrays], core_ids=[0])
    y = np.asarray(r.results[0]["out_x"])
    return np.ascontiguousarray(y.transpose(1, 0, 2)).reshape(1, T, D)
```
